# Optimizing a Trainium2 kernel written in Bass

```python
import math
import jax, jax.numpy as jnp
from jax import lax
import numpy as np
import jax
import jax.numpy as jnp

D_MODEL = 1024
BATCH = 1
SEQ = 512
DEPTH = 1

GDN_HEADS = 4
GDN_HEAD_DIM = 128
GDN_WIDTH = GDN_HEADS * GDN_HEAD_DIM
CONV_WIDTH = 4
CHUNK = 64
SWA_HEADS = 8
SWA_HEAD_DIM = 64
SWA_WIDTH = SWA_HEADS * SWA_HEAD_DIM
DILATED_PATTERNS = ((128, 1), (512, 4), (2048, 16))
NUM_BUCKETS = 32
MAX_DISTANCE = 2048
MIX_WIDTH = GDN_WIDTH + SWA_WIDTH
IN_SIZES = (GDN_WIDTH, GDN_WIDTH, GDN_WIDTH, GDN_WIDTH, GDN_HEADS, GDN_HEADS,
            SWA_WIDTH, SWA_WIDTH, SWA_WIDTH)
IN_COLS = sum(IN_SIZES)
D_FF = ((-(-8 * D_MODEL // 3)) + 255) // 256 * 256
RMS_EPS = 1e-6


def rmsnorm(x, g):
    xf = x.astype(jnp.float32)
    y = xf * lax.rsqrt(jnp.mean(xf * xf, axis=-1, keepdims=True) + RMS_EPS)
    return (y * g.astype(jnp.float32)).astype(x.dtype)

def l2norm(x):
    return x * lax.rsqrt(jnp.sum(x * x, axis=-1, keepdims=True) + 1e-6)

def causal_depthwise_conv(x, w):
    K, C = w.shape
    return lax.conv_general_dilated(x, w[:, None, :].astype(x.dtype), (1,), ((K - 1, 0),),
                                    dimension_numbers=('NWC', 'WIO', 'NWC'),
                                    feature_group_count=C)

def chunk_gated_delta_rule(q, k, v, g, beta):
    Bn, S, H, Dk = q.shape
    Dv = v.shape[-1]
    N = S // CHUNK

    def chunks(t):
        t = t.reshape((Bn, N, CHUNK, H) + t.shape[3:])
        return jnp.moveaxis(jnp.moveaxis(t, 1, 0), 3, 2)

    qc, kc, vc = chunks(q), chunks(k), chunks(v)
    bc = chunks(beta)
    gc = jnp.cumsum(chunks(g), axis=-1)
    idx = jnp.arange(CHUNK)
    causal = idx[:, None] >= idx[None, :]
    strict = idx[:, None] > idx[None, :]
    decay = jnp.exp(jnp.where(causal, gc[..., :, None] - gc[..., None, :], -jnp.inf))
    kb = kc * bc[..., None]
    a = jnp.where(strict, jnp.einsum('nbhid,nbhjd->nbhij', kb, kc) * decay, 0.0)
    eye = jnp.eye(CHUNK, dtype=q.dtype)
    t_inv = lax.linalg.triangular_solve(eye + a, jnp.broadcast_to(eye, a.shape),
                                        left_side=True, lower=True)
    u = t_inv @ (vc * bc[..., None])
    w = t_inv @ (kb * jnp.exp(gc)[..., None])
    attn = jnp.einsum('nbhid,nbhjd->nbhij', qc, kc) * decay
    q_dec = qc * jnp.exp(gc)[..., None]
    k_dec = kc * jnp.exp(gc[..., -1:] - gc)[..., None]
    g_end = jnp.exp(gc[..., -1])

    def step(state, inp):
        u_i, w_i, attn_i, qd_i, kd_i, ge_i = inp
        v_new = u_i - jnp.einsum('bhck,bhkv->bhcv', w_i, state)
        o_i = (jnp.einsum('bhck,bhkv->bhcv', qd_i, state)
               + jnp.einsum('bhij,bhjv->bhiv', attn_i, v_new))
        state = state * ge_i[..., None, None] + jnp.einsum('bhck,bhcv->bhkv', kd_i, v_new)
        return state, o_i

    s0 = jnp.zeros((Bn, H, Dk, Dv), q.dtype)
    _, o = lax.scan(step, s0, (u, w, attn, q_dec, k_dec, g_end))
    return jnp.moveaxis(o, 0, 1).transpose(0, 1, 3, 2, 4).reshape(Bn, S, H, Dv)

def gated_deltanet(q, k, v, gate, beta_logit, a_logit, conv_w, a_log, dt_bias, onorm_g):
    f32 = jnp.float32
    Bn, S, _ = q.shape
    qkv = jax.nn.silu(causal_depthwise_conv(jnp.concatenate([q, k, v], axis=-1), conv_w)).astype(f32)
    q, k, v = jnp.split(qkv, 3, axis=-1)
    heads = lambda t: t.reshape(Bn, S, GDN_HEADS, GDN_HEAD_DIM)
    q = l2norm(heads(q)) * GDN_HEAD_DIM ** -0.5
    k = l2norm(heads(k))
    v = heads(v)
    beta = jax.nn.sigmoid(beta_logit.astype(f32))
    g = -jnp.exp(a_log.astype(f32)) * jax.nn.softplus(a_logit.astype(f32) + dt_bias.astype(f32))
    o = chunk_gated_delta_rule(q, k, v, g, beta)
    o = o * lax.rsqrt(jnp.mean(o * o, axis=-1, keepdims=True) + RMS_EPS) * onorm_g.astype(f32)
    o = o * jax.nn.silu(heads(gate).astype(f32))
    return o.reshape(Bn, S, GDN_WIDTH).astype(gate.dtype)

def t5_causal_bucket(dist):
    max_exact = NUM_BUCKETS // 2
    d = jnp.maximum(dist, 1).astype(jnp.float32)
    log_b = max_exact + (jnp.log(d / max_exact) / math.log(MAX_DISTANCE / max_exact)
                         * (NUM_BUCKETS - max_exact)).astype(jnp.int32)
    return jnp.where(dist < max_exact, dist, jnp.minimum(log_b, NUM_BUCKETS - 1))

def dilated_band(q, k, v, rel_bias, window, dilation):
    Bn, S, H, Dh = q.shape
    w = window // dilation
    L = S // dilation
    nb = -(-L // w)
    Lp = nb * w

    def to_sub(t):
        t = t.reshape(Bn, L, dilation, H, Dh).transpose(0, 3, 2, 1, 4)
        return jnp.pad(t, ((0, 0), (0, 0), (0, 0), (0, Lp - L), (0, 0)))

    blocks = lambda t: t.reshape(Bn, H, dilation, nb, w, Dh)

    def band(t):
        prev = jnp.pad(t, ((0, 0), (0, 0), (0, 0), (w, 0), (0, 0)))[:, :, :, :Lp]
        return jnp.concatenate([blocks(prev), blocks(t)], axis=-2)

    qb, kb, vb = blocks(to_sub(q)), band(to_sub(k)), band(to_sub(v))
    qi = jnp.arange(w)[:, None]
    kj = jnp.arange(2 * w)[None, :]
    rel = qi + w - kj
    blk = jnp.arange(nb)[:, None, None]
    valid = (rel >= 0) & (rel <= w) & (blk * w + kj - w >= 0)
    bias_steps = rel_bias[t5_causal_bucket(jnp.arange(w + 1) * dilation)]
    bias = jnp.moveaxis(bias_steps[jnp.clip(rel, 0, w)], -1, 0).astype(jnp.float32)
    logits = jnp.einsum('bhrnqd,bhrnkd->bhrnqk', qb, kb) * Dh ** -0.5 + bias[None, :, None, None]
    logits = jnp.where(valid, logits, -jnp.inf)
    m = jnp.max(logits, axis=-1)
    p = jnp.exp(logits - m[..., None])
    s = jnp.sum(p, axis=-1)
    num = jnp.einsum('bhrnqk,bhrnkd->bhrnqd', p, vb)

    def from_sub(t):
        rest = t.shape[5:]
        t = t.reshape((Bn, H, dilation, Lp) + rest)[:, :, :, :L]
        t = t.transpose((0, 3, 2, 1) + tuple(range(4, t.ndim)))
        return t.reshape((Bn, S, H) + rest)

    return from_sub(num), from_sub(m), from_sub(s)

def dilated_attention(q, k, v, rel_bias):
    Bn, S, _ = q.shape
    heads = lambda t: t.reshape(Bn, S, SWA_HEADS, SWA_HEAD_DIM).astype(jnp.float32)
    qh, kh, vh = heads(q), heads(k), heads(v)
    parts = [dilated_band(qh, kh, vh, rel_bias, win, dil) for win, dil in DILATED_PATTERNS]
    nums = jnp.stack([pt[0] for pt in parts])
    ms = jnp.stack([pt[1] for pt in parts])
    ss = jnp.stack([pt[2] for pt in parts])
    wts = jnp.exp(ms - jnp.max(ms, axis=0, keepdims=True))
    out = jnp.sum(wts[..., None] * nums, axis=0) / jnp.sum(wts * ss, axis=0)[..., None]
    return out.reshape(Bn, S, SWA_WIDTH).astype(q.dtype)

def first_inputs(seed: int = 0) -> dict:
    key = jax.random.key(seed)
    ks = jax.random.split(key, 16)
    f32 = jnp.float32
    nrm = lambda k_, shape, scale: jax.random.normal(k_, shape, f32) * scale
    dt = jnp.exp(jax.random.uniform(ks[4], (DEPTH, GDN_HEADS), f32, math.log(1e-3), math.log(1e-1)))
    return {
        'x': nrm(ks[0], (BATCH, SEQ, D_MODEL), 1.0),
        'w_in': nrm(ks[1], (DEPTH, D_MODEL, IN_COLS), D_MODEL ** -0.5),
        'conv_w': nrm(ks[2], (DEPTH, CONV_WIDTH, 3 * GDN_WIDTH), CONV_WIDTH ** -0.5),
        'a_log': jnp.log(jax.random.uniform(ks[3], (DEPTH, GDN_HEADS), f32, 1.0, 16.0)),
        'dt_bias': dt + jnp.log(-jnp.expm1(-dt)),
        'onorm_g': 1.0 + nrm(ks[5], (DEPTH, GDN_HEAD_DIM), 0.1),
        'rel_bias': nrm(ks[6], (NUM_BUCKETS, SWA_HEADS), 0.2),
        'w_out': nrm(ks[7], (DEPTH, MIX_WIDTH, D_MODEL), MIX_WIDTH ** -0.5),
        'g_mix_pre': 1.0 + nrm(ks[8], (DEPTH, D_MODEL), 0.1),
        'g_mix_post': 1.0 + nrm(ks[9], (DEPTH, D_MODEL), 0.1),
        'w_gate': nrm(ks[10], (DEPTH, D_MODEL, D_FF), D_MODEL ** -0.5),
        'w_up': nrm(ks[11], (DEPTH, D_MODEL, D_FF), D_MODEL ** -0.5),
        'w_down': nrm(ks[12], (DEPTH, D_FF, D_MODEL), D_FF ** -0.5),
        'g_ffn_pre': 1.0 + nrm(ks[13], (DEPTH, D_MODEL), 0.1),
        'g_ffn_post': 1.0 + nrm(ks[14], (DEPTH, D_MODEL), 0.1),
    }

def first_block(x, w_in, conv_w, a_log, dt_bias, onorm_g, rel_bias, w_out, g_mix_pre, g_mix_post,
              w_gate, w_up, w_down, g_ffn_pre, g_ffn_post):
    split_at = [int(c) for c in np.cumsum(IN_SIZES)[:-1]]
    for l in range(DEPTH):
        h = rmsnorm(x, g_mix_pre[l])
        proj = h @ w_in[l]
        qa, ka, va, gate_a, beta_a, alpha_a, qb, kb, vb = jnp.split(proj, split_at, axis=-1)
        out_a = gated_deltanet(qa, ka, va, gate_a, beta_a, alpha_a,
                               conv_w[l], a_log[l], dt_bias[l], onorm_g[l])
        out_b = dilated_attention(qb, kb, vb, rel_bias)
        mix = jnp.concatenate([out_a, out_b], axis=-1) @ w_out[l]
        x = x + rmsnorm(mix, g_mix_post[l])
        h = rmsnorm(x, g_ffn_pre[l])
        f = (jax.nn.silu(h @ w_gate[l]) * (h @ w_up[l])) @ w_down[l]
        x = x + rmsnorm(f, g_ffn_post[l])
    return x


DEPTH_2 = 2

GRID_W = 64
CTX_LEN = 256
HEAD_DIM = 64
Q_BLOCK = 128
ROPE_THETA = 10000.0
EPS = 1e-6
MIX_HALF = D_MODEL // 2
NA_HEADS = MIX_HALF // HEAD_DIM
NA_WIN_R = 8
NA_WIN_C = 16
DA_VDIM = 2 * HEAD_DIM
DA_HEADS = MIX_HALF // DA_VDIM
GQA_Q_HEADS = MIX_HALF // HEAD_DIM
GQA_KV_HEADS = GQA_Q_HEADS // 4
HY_WIDTH = MIX_HALF
HY_EMB_DIM = 33
HY_FILTER_ORDER = 64
HY_FAST_DECAY = 0.3
HY_SLOW_DECAY = 1.5
HY_DECAY_TARGET = 1e-2
FFN_HIDDEN = ((8 * D_MODEL // 3 + 255) // 256) * 256

NA_WIDTH = NA_HEADS * HEAD_DIM
DA_QK_WIDTH = DA_HEADS * 2 * HEAD_DIM
DA_V_WIDTH = DA_HEADS * DA_VDIM
EVEN_IN = 3 * NA_WIDTH + 2 * DA_QK_WIDTH + DA_V_WIDTH
EVEN_MIX = NA_WIDTH + DA_V_WIDTH
GQA_Q_WIDTH = GQA_Q_HEADS * HEAD_DIM
GQA_KV_WIDTH = GQA_KV_HEADS * HEAD_DIM
ODD_IN = GQA_Q_WIDTH + 2 * GQA_KV_WIDTH + 3 * HY_WIDTH
ODD_MIX = GQA_Q_WIDTH + HY_WIDTH
N_EVEN = (DEPTH_2 + 1) // 2
N_ODD = DEPTH_2 // 2


F32 = jnp.float32

def rms_norm(x, gain=None):
    xf = x.astype(F32)
    y = xf * lax.rsqrt(jnp.mean(xf * xf, axis=-1, keepdims=True) + EPS)
    if gain is not None:
        y = y * gain.astype(F32)
    return y.astype(x.dtype)

def modulate(x, shift, scale):
    return rms_norm(x) * (1 + scale) + shift

def split_heads(x, n, d):
    b, l = x.shape[:2]
    return x.reshape(b, l, n, d).transpose(0, 2, 1, 3)

def merge_heads(x):
    b, h, l, d = x.shape
    return x.transpose(0, 2, 1, 3).reshape(b, l, h * d)

def dwconv3(x, w, b):
    xp = jnp.pad(x, ((0, 0), (1, 1), (0, 0)))
    return xp[:, :-2] * w[0] + xp[:, 1:-1] * w[1] + xp[:, 2:] * w[2] + b

def axial_rope(length, head_dim):
    t = jnp.arange(length, dtype=jnp.int32)
    row = (t // GRID_W).astype(F32)
    col = (t % GRID_W).astype(F32)
    n_pairs = head_dim // 4
    inv_freq = ROPE_THETA ** (-jnp.arange(n_pairs, dtype=F32) / n_pairs)
    ang = jnp.concatenate([row[:, None] * inv_freq, col[:, None] * inv_freq], axis=-1)
    return jnp.cos(ang), jnp.sin(ang)

def apply_rope(x, cos, sin):
    xf = x.astype(F32).reshape(x.shape[:-1] + (x.shape[-1] // 2, 2))
    x0, x1 = xf[..., 0], xf[..., 1]
    out = jnp.stack([x0 * cos - x1 * sin, x0 * sin + x1 * cos], axis=-1)
    return out.reshape(x.shape).astype(x.dtype)

def sweep_query_blocks(fn, *qs):
    b, h, l = qs[0].shape[:3]
    n = l // Q_BLOCK
    blocks = tuple(jnp.moveaxis(q.reshape(b, h, n, Q_BLOCK, q.shape[-1]), 2, 0) for q in qs)
    out = lax.map(lambda qb: fn(*qb), blocks)
    return jnp.moveaxis(out, 0, 2).reshape(b, h, l, out.shape[-1])

def attend(q, k, v):
    scale = q.shape[-1] ** -0.5
    s = jnp.einsum('bhqd,bhsd->bhqs', q, k).astype(F32) * scale
    p = jax.nn.softmax(s, axis=-1).astype(v.dtype)
    return jnp.einsum('bhqs,bhsd->bhqd', p, v)

def diff_attend(q1, q2, k1, k2, v, lam):
    scale = q1.shape[-1] ** -0.5
    p1 = jax.nn.softmax(jnp.einsum('bhqd,bhsd->bhqs', q1, k1).astype(F32) * scale, axis=-1)
    p2 = jax.nn.softmax(jnp.einsum('bhqd,bhsd->bhqs', q2, k2).astype(F32) * scale, axis=-1)
    return jnp.einsum('bhqs,bhsd->bhqd', (p1 - lam * p2).astype(v.dtype), v)

def gqa_attend(q, k, v):
    b, hq, nq, d = q.shape
    hkv = k.shape[1]
    qg = q.reshape(b, hkv, hq // hkv, nq, d)
    s = jnp.einsum('bkgqd,bksd->bkgqs', qg, k).astype(F32) * (d ** -0.5)
    p = jax.nn.softmax(s, axis=-1).astype(v.dtype)
    return jnp.einsum('bkgqs,bksd->bkgqd', p, v).reshape(b, hq, nq, d)

def neighbourhood_attention(q, k, v, k_ctx, v_ctx, rpb):
    b, h, l, d = q.shape
    rows = l // GRID_W
    win_r = min(NA_WIN_R, rows)
    n_win = win_r * NA_WIN_C
    scale = d ** -0.5
    qg = q.reshape(b, h, rows, GRID_W, d)
    kg = k.reshape(b, h, rows, GRID_W, d)
    vg = v.reshape(b, h, rows, GRID_W, d)
    row_start = jnp.clip(jnp.arange(rows) - win_r // 2, 0, rows - win_r)
    col_ids = jnp.arange(GRID_W)
    col_start = jnp.clip(col_ids - NA_WIN_C // 2, 0, GRID_W - NA_WIN_C)
    col_idx = col_start[:, None] + jnp.arange(NA_WIN_C)
    col_off = col_idx - col_ids[:, None] + NA_WIN_C - 1
    rpb32 = rpb.astype(F32)

    def one_row(args):
        q_row, r, r0 = args
        k_rows = lax.dynamic_slice_in_dim(kg, r0, win_r, axis=2)
        v_rows = lax.dynamic_slice_in_dim(vg, r0, win_r, axis=2)
        k_win = k_rows[:, :, :, col_idx]
        v_win = v_rows[:, :, :, col_idx]
        row_off = r0 + jnp.arange(win_r) - r + NA_WIN_R - 1
        bias = rpb32[:, row_off[None, :, None], col_off[:, None, :]]
        s_win = jnp.einsum('bhwd,bhrwcd->bhwrc', q_row, k_win).astype(F32) * scale + bias
        s_ctx = jnp.einsum('bhwd,bhsd->bhws', q_row, k_ctx).astype(F32) * scale
        s = jnp.concatenate([s_win.reshape(b, h, GRID_W, n_win), s_ctx], axis=-1)
        p = jax.nn.softmax(s, axis=-1).astype(v.dtype)
        p_win = p[..., :n_win].reshape(b, h, GRID_W, win_r, NA_WIN_C)
        return (jnp.einsum('bhwrc,bhrwcd->bhwd', p_win, v_win)
                + jnp.einsum('bhws,bhsd->bhwd', p[..., n_win:], v_ctx))

    out = lax.map(one_row, (jnp.moveaxis(qg, 2, 0), jnp.arange(rows), row_start))
    return jnp.moveaxis(out, 0, 2).reshape(b, h, l, d)

def hyena_filter(length, w1, b1, w2, b2, w3, b3, w4, freq):
    t = jnp.linspace(0.0, 1.0, length, dtype=F32)[:, None]
    bands = (HY_EMB_DIM - 1) // 2
    w = 2.0 * math.pi * jnp.arange(length, dtype=F32)[:, None] / length
    f = jnp.linspace(1e-4, bands - 1, bands, dtype=F32)[None, :]
    z = jnp.concatenate([t, jnp.cos(f * w), -jnp.sin(f * w)], axis=-1)
    fr = freq.astype(F32)
    hdn = jnp.sin(fr * (z @ w1.astype(F32) + b1.astype(F32)))
    hdn = jnp.sin(fr * (hdn @ w2.astype(F32) + b2.astype(F32)))
    hdn = jnp.sin(fr * (hdn @ w3.astype(F32) + b3.astype(F32)))
    hdn = hdn @ w4.astype(F32)
    max_decay = math.log(HY_DECAY_TARGET) / HY_FAST_DECAY
    min_decay = math.log(HY_DECAY_TARGET) / HY_SLOW_DECAY
    deltas = jnp.linspace(min_decay, max_decay, HY_WIDTH, dtype=F32)
    decay = jnp.exp(-t * jnp.abs(deltas))
    h_fwd = hdn[:, :HY_WIDTH] * decay
    h_bwd = hdn[:, HY_WIDTH:] * decay
    k_two = jnp.concatenate([h_fwd, jnp.zeros((1, HY_WIDTH), F32), h_bwd[:0:-1]], axis=0)
    return k_two / jnp.sum(jnp.abs(k_two), axis=0, keepdims=True)

def hyena(u, conv_w, conv_b, w1, b1, w2, b2, w3, b3, w4, freq, skip):
    length = u.shape[1]
    u = dwconv3(u, conv_w, conv_b)
    x0, x1, val = jnp.split(u, 3, axis=-1)
    z = (val * x1).astype(F32)
    kf = jnp.fft.rfft(hyena_filter(length, w1, b1, w2, b2, w3, b3, w4, freq), n=2 * length, axis=0)
    zf = jnp.fft.rfft(z, n=2 * length, axis=1)
    y = jnp.fft.irfft(zf * kf, n=2 * length, axis=1)[:, :length]
    return (x0.astype(F32) * (y + skip.astype(F32) * z)).astype(u.dtype)

def even_mixer(h_l, h_c, w_in, w_out, na_qg, na_kg, rpb, da_qg, da_kg, lq1, lk1, lq2, lk2, subln,
               lam_init, cos, sin, with_ctx):
    offs = [NA_WIDTH, 2 * NA_WIDTH, 3 * NA_WIDTH, 3 * NA_WIDTH + DA_QK_WIDTH, 3 * NA_WIDTH + 2 * DA_QK_WIDTH]
    qa_l, ka_l, va_l, qb_l, kb_l, vb_l = jnp.split(h_l @ w_in, offs, axis=-1)
    qa_c, ka_c, va_c, qb_c, kb_c, vb_c = jnp.split(h_c @ w_in, offs, axis=-1)
    qa_l = rms_norm(split_heads(qa_l, NA_HEADS, HEAD_DIM), na_qg)
    ka_l = rms_norm(split_heads(ka_l, NA_HEADS, HEAD_DIM), na_kg)
    va_l = split_heads(va_l, NA_HEADS, HEAD_DIM)
    ka_c = rms_norm(split_heads(ka_c, NA_HEADS, HEAD_DIM), na_kg)
    va_c = split_heads(va_c, NA_HEADS, HEAD_DIM)
    ya_l = neighbourhood_attention(qa_l, ka_l, va_l, ka_c, va_c, rpb)
    lam = (jnp.exp(jnp.sum(lq1.astype(F32) * lk1.astype(F32)))
           - jnp.exp(jnp.sum(lq2.astype(F32) * lk2.astype(F32))) + lam_init)
    qb_l = apply_rope(rms_norm(split_heads(qb_l, 2 * DA_HEADS, HEAD_DIM), da_qg), cos, sin)
    kb_l = apply_rope(rms_norm(split_heads(kb_l, 2 * DA_HEADS, HEAD_DIM), da_kg), cos, sin)
    vb_l = split_heads(vb_l, DA_HEADS, DA_VDIM)
    kb_c = rms_norm(split_heads(kb_c, 2 * DA_HEADS, HEAD_DIM), da_kg)
    vb_c = split_heads(vb_c, DA_HEADS, DA_VDIM)
    k1_all = jnp.concatenate([kb_l[:, 0::2], kb_c[:, 0::2]], axis=2)
    k2_all = jnp.concatenate([kb_l[:, 1::2], kb_c[:, 1::2]], axis=2)
    v_all = jnp.concatenate([vb_l, vb_c], axis=2)
    yb_l = sweep_query_blocks(lambda q1, q2: diff_attend(q1, q2, k1_all, k2_all, v_all, lam),
                              qb_l[:, 0::2], qb_l[:, 1::2])
    y_l = jnp.concatenate([merge_heads(ya_l), merge_heads(rms_norm(yb_l, subln) * (1.0 - lam_init))],
                          axis=-1) @ w_out
    if not with_ctx:
        return y_l, None
    qa_c = rms_norm(split_heads(qa_c, NA_HEADS, HEAD_DIM), na_qg)
    ya_c = attend(qa_c, ka_c, va_c)
    qb_c = rms_norm(split_heads(qb_c, 2 * DA_HEADS, HEAD_DIM), da_qg)
    yb_c = diff_attend(qb_c[:, 0::2], qb_c[:, 1::2], kb_c[:, 0::2], kb_c[:, 1::2], vb_c, lam)
    y_c = jnp.concatenate([merge_heads(ya_c), merge_heads(rms_norm(yb_c, subln) * (1.0 - lam_init))],
                          axis=-1) @ w_out
    return y_l, y_c

def odd_mixer(h_l, h_c, w_in, w_out, qg, kg, conv_w, conv_b, w1, b1, w2, b2, w3, b3, w4, freq, skip,
              cos, sin, with_ctx):
    offs = [GQA_Q_WIDTH, GQA_Q_WIDTH + GQA_KV_WIDTH, GQA_Q_WIDTH + 2 * GQA_KV_WIDTH]
    q_l, k_l, v_l, hy_l = jnp.split(h_l @ w_in, offs, axis=-1)
    q_c, k_c, v_c, hy_c = jnp.split(h_c @ w_in, offs, axis=-1)
    q_l = apply_rope(rms_norm(split_heads(q_l, GQA_Q_HEADS, HEAD_DIM), qg), cos, sin)
    k_l = apply_rope(rms_norm(split_heads(k_l, GQA_KV_HEADS, HEAD_DIM), kg), cos, sin)
    v_l = split_heads(v_l, GQA_KV_HEADS, HEAD_DIM)
    k_c = rms_norm(split_heads(k_c, GQA_KV_HEADS, HEAD_DIM), kg)
    v_c = split_heads(v_c, GQA_KV_HEADS, HEAD_DIM)
    k_all = jnp.concatenate([k_l, k_c], axis=2)
    v_all = jnp.concatenate([v_l, v_c], axis=2)
    yc_l = sweep_query_blocks(lambda qb: gqa_attend(qb, k_all, v_all), q_l)
    yd_l = hyena(hy_l, conv_w, conv_b, w1, b1, w2, b2, w3, b3, w4, freq, skip)
    y_l = jnp.concatenate([merge_heads(yc_l), yd_l], axis=-1) @ w_out
    if not with_ctx:
        return y_l, None
    q_c = rms_norm(split_heads(q_c, GQA_Q_HEADS, HEAD_DIM), qg)
    yc_c = gqa_attend(q_c, k_c, v_c)
    yd_c = hyena(hy_c, conv_w, conv_b, w1, b1, w2, b2, w3, b3, w4, freq, skip)
    y_c = jnp.concatenate([merge_heads(yc_c), yd_c], axis=-1) @ w_out
    return y_l, y_c

def conv_ffn(h, w_up, conv_w, conv_b, w_down):
    g, v = jnp.split(h @ w_up, 2, axis=-1)
    g = dwconv3(g, conv_w, conv_b)
    return (jax.nn.silu(g) * v) @ w_down

def second_inputs(seed: int = 0) -> dict:
    key = jax.random.key(seed)
    D = D_MODEL
    specs = [
        ('x', (BATCH, SEQ, D), 1.0, 0.0),
        ('c', (BATCH, D), 1.0, 0.0),
        ('ctx', (BATCH, CTX_LEN, D), 1.0, 0.0),
        ('c_ctx', (D,), 1.0, 0.0),
        ('w_ada', (DEPTH_2, D, 6 * D), D ** -0.5, 0.0),
        ('b_ada', (DEPTH_2, 6 * D), 0.02, 0.0),
        ('w_up', (DEPTH_2, D, 2 * FFN_HIDDEN), D ** -0.5, 0.0),
        ('ffn_conv_w', (DEPTH_2, 3, FFN_HIDDEN), 3 ** -0.5, 0.0),
        ('ffn_conv_b', (DEPTH_2, FFN_HIDDEN), 0.02, 0.0),
        ('w_down', (DEPTH_2, FFN_HIDDEN, D), FFN_HIDDEN ** -0.5, 0.0),
        ('w_in_e', (N_EVEN, D, EVEN_IN), D ** -0.5, 0.0),
        ('w_out_e', (N_EVEN, EVEN_MIX, D), EVEN_MIX ** -0.5, 0.0),
        ('na_q_gain', (N_EVEN, HEAD_DIM), 0.05, 1.0),
        ('na_k_gain', (N_EVEN, HEAD_DIM), 0.05, 1.0),
        ('na_rpb', (N_EVEN, NA_HEADS, 2 * NA_WIN_R - 1, 2 * NA_WIN_C - 1), 0.02, 0.0),
        ('da_q_gain', (N_EVEN, HEAD_DIM), 0.05, 1.0),
        ('da_k_gain', (N_EVEN, HEAD_DIM), 0.05, 1.0),
        ('da_lambda_q1', (N_EVEN, HEAD_DIM), 0.1, 0.0),
        ('da_lambda_k1', (N_EVEN, HEAD_DIM), 0.1, 0.0),
        ('da_lambda_q2', (N_EVEN, HEAD_DIM), 0.1, 0.0),
        ('da_lambda_k2', (N_EVEN, HEAD_DIM), 0.1, 0.0),
        ('da_subln_gain', (N_EVEN, DA_VDIM), 0.05, 1.0),
        ('w_in_o', (N_ODD, D, ODD_IN), D ** -0.5, 0.0),
        ('w_out_o', (N_ODD, ODD_MIX, D), ODD_MIX ** -0.5, 0.0),
        ('gqa_q_gain', (N_ODD, HEAD_DIM), 0.05, 1.0),
        ('gqa_k_gain', (N_ODD, HEAD_DIM), 0.05, 1.0),
        ('hy_conv_w', (N_ODD, 3, 3 * HY_WIDTH), 3 ** -0.5, 0.0),
        ('hy_conv_b', (N_ODD, 3 * HY_WIDTH), 0.02, 0.0),
        ('hy_w1', (N_ODD, HY_EMB_DIM, HY_FILTER_ORDER), HY_EMB_DIM ** -0.5, 0.0),
        ('hy_b1', (N_ODD, HY_FILTER_ORDER), HY_EMB_DIM ** -0.5, 0.0),
        ('hy_w2', (N_ODD, HY_FILTER_ORDER, HY_FILTER_ORDER), HY_FILTER_ORDER ** -0.5, 0.0),
        ('hy_b2', (N_ODD, HY_FILTER_ORDER), HY_FILTER_ORDER ** -0.5, 0.0),
        ('hy_w3', (N_ODD, HY_FILTER_ORDER, HY_FILTER_ORDER), HY_FILTER_ORDER ** -0.5, 0.0),
        ('hy_b3', (N_ODD, HY_FILTER_ORDER), HY_FILTER_ORDER ** -0.5, 0.0),
        ('hy_w4', (N_ODD, HY_FILTER_ORDER, 2 * HY_WIDTH), HY_FILTER_ORDER ** -0.5, 0.0),
        ('hy_freq', (N_ODD, HY_FILTER_ORDER), 0.05, 1.0),
        ('hy_skip', (N_ODD, HY_WIDTH), 1.0, 0.0),
    ]
    keys = jax.random.split(key, len(specs))
    return {name: off + scale * jax.random.normal(keys[i], shape, F32)
            for i, (name, shape, scale, off) in enumerate(specs)}

def second_block(x, c, ctx, c_ctx, w_ada, b_ada, w_up, ffn_conv_w, ffn_conv_b, w_down, w_in_e, w_out_e,
              na_q_gain, na_k_gain, na_rpb, da_q_gain, da_k_gain, da_lambda_q1, da_lambda_k1, da_lambda_q2,
              da_lambda_k2, da_subln_gain, w_in_o, w_out_o, gqa_q_gain, gqa_k_gain, hy_conv_w, hy_conv_b,
              hy_w1, hy_b1, hy_w2, hy_b2, hy_w3, hy_b3, hy_w4, hy_freq, hy_skip):
    cos, sin = axial_rope(x.shape[1], HEAD_DIM)
    x_l, x_c = x, ctx
    for layer in range(DEPTH_2):
        with_ctx = layer < DEPTH_2 - 1
        mod_l = (jax.nn.silu(c) @ w_ada[layer] + b_ada[layer])[:, None, :]
        mod_c = jax.nn.silu(c_ctx) @ w_ada[layer] + b_ada[layer]
        sh1_l, sc1_l, g1_l, sh2_l, sc2_l, g2_l = jnp.split(mod_l, 6, axis=-1)
        sh1_c, sc1_c, g1_c, sh2_c, sc2_c, g2_c = jnp.split(mod_c, 6, axis=-1)
        h_l = modulate(x_l, sh1_l, sc1_l)
        h_c = modulate(x_c, sh1_c, sc1_c)
        i = layer // 2
        if layer % 2 == 0:
            lam_init = 0.8 - 0.6 * math.exp(-0.3 * layer)
            y_l, y_c = even_mixer(h_l, h_c, w_in_e[i], w_out_e[i], na_q_gain[i], na_k_gain[i], na_rpb[i],
                                  da_q_gain[i], da_k_gain[i], da_lambda_q1[i], da_lambda_k1[i],
                                  da_lambda_q2[i], da_lambda_k2[i], da_subln_gain[i], lam_init, cos, sin,
                                  with_ctx)
        else:
            y_l, y_c = odd_mixer(h_l, h_c, w_in_o[i], w_out_o[i], gqa_q_gain[i], gqa_k_gain[i],
                                 hy_conv_w[i], hy_conv_b[i], hy_w1[i], hy_b1[i], hy_w2[i], hy_b2[i],
                                 hy_w3[i], hy_b3[i], hy_w4[i], hy_freq[i], hy_skip[i], cos, sin, with_ctx)
        x_l = x_l + g1_l * y_l
        x_l = x_l + g2_l * conv_ffn(modulate(x_l, sh2_l, sc2_l), w_up[layer], ffn_conv_w[layer],
                                    ffn_conv_b[layer], w_down[layer])
        if with_ctx:
            x_c = x_c + g1_c * y_c
            x_c = x_c + g2_c * conv_ffn(modulate(x_c, sh2_c, sc2_c), w_up[layer], ffn_conv_w[layer],
                                        ffn_conv_b[layer], w_down[layer])
    return x_l


def setup_inputs(seed=0):
    out = dict(first_inputs(seed))
    for name, value in second_inputs(seed + 1).items():
        if name != "x":
            out[name + "_2"] = value
    return out


def reference(
    x, w_in, conv_w, a_log, dt_bias, onorm_g, rel_bias, w_out, g_mix_pre, g_mix_post, w_gate,
    w_up, w_down, g_ffn_pre, g_ffn_post, c_2, ctx_2, c_ctx_2, w_ada_2, b_ada_2, w_up_2,
    ffn_conv_w_2, ffn_conv_b_2, w_down_2, w_in_e_2, w_out_e_2, na_q_gain_2, na_k_gain_2,
    na_rpb_2, da_q_gain_2, da_k_gain_2, da_lambda_q1_2, da_lambda_k1_2, da_lambda_q2_2,
    da_lambda_k2_2, da_subln_gain_2, w_in_o_2, w_out_o_2, gqa_q_gain_2, gqa_k_gain_2,
    hy_conv_w_2, hy_conv_b_2, hy_w1_2, hy_b1_2, hy_w2_2, hy_b2_2, hy_w3_2, hy_b3_2, hy_w4_2,
    hy_freq_2, hy_skip_2,
):
    x = first_block(
        x, w_in, conv_w, a_log, dt_bias, onorm_g, rel_bias, w_out, g_mix_pre, g_mix_post,
        w_gate, w_up, w_down, g_ffn_pre, g_ffn_post,
    )
    return second_block(
        x, c_2, ctx_2, c_ctx_2, w_ada_2, b_ada_2, w_up_2, ffn_conv_w_2, ffn_conv_b_2, w_down_2,
        w_in_e_2, w_out_e_2, na_q_gain_2, na_k_gain_2, na_rpb_2, da_q_gain_2, da_k_gain_2,
        da_lambda_q1_2, da_lambda_k1_2, da_lambda_q2_2, da_lambda_k2_2, da_subln_gain_2,
        w_in_o_2, w_out_o_2, gqa_q_gain_2, gqa_k_gain_2, hy_conv_w_2, hy_conv_b_2, hy_w1_2,
        hy_b1_2, hy_w2_2, hy_b2_2, hy_w3_2, hy_b3_2, hy_w4_2, hy_freq_2, hy_skip_2,
    )


_drawn_inputs = setup_inputs


def setup_inputs(seed=0):
    import zlib

    import numpy as np

    out = dict(_drawn_inputs(seed))
    spreads = {}
    factors = {'ffn_conv_b_2': 7.279,
     'na_q_gain_2': 8.0,
     'na_k_gain_2': 8.0,
     'na_rpb_2': 64.0,
     'da_q_gain_2': 8.0,
     'da_k_gain_2': 8.0,
     'da_lambda_q1_2': 6.789,
     'da_lambda_k1_2': 5.757,
     'da_lambda_q2_2': 8.0,
     'da_lambda_k2_2': 8.0,
     'da_subln_gain_2': 4.798,
     'gqa_q_gain_2': 8.0,
     'gqa_k_gain_2': 8.0,
     'hy_conv_b_2': 4.462,
     'hy_b2_2': 2.732,
     'hy_freq_2': 8.0}
    for name, (base, spread) in spreads.items():
        noise = np.random.default_rng([zlib.crc32(name.encode()), seed]).standard_normal(out[name].shape)
        drawn = base * np.exp(spread * noise) if base else spread * noise
        out[name] = jnp.asarray(drawn.astype(out[name].dtype))
    for name, factor in factors.items():
        out[name] = (out[name] * factor).astype(out[name].dtype)
    return out
```

```python
import concourse.bass as bass
import numpy as np
from concourse import mybir
from concourse.alu_op_type import AluOpType as ALU
from contextlib import ExitStack

F32 = mybir.dt.float32
ACT = mybir.ActivationFunctionType
AX = mybir.AxisListType

P = 128
D = 1024
DT = D // P
S = 512
CTX = 256
T = S + CTX
F = 2816
FT = F // P
HALF = D // 2
HT = HALF // P
HD = 64
CHUNK = 64
PAIRS = S // P
GH = 4
GRID_W = 64
WIN_R, WIN_C = 8, 16
EMB, ORDER = 33, 64
BUCKETS = 32
MASKED = -1.0e30
EPS = 1e-6
ROUND = 1.5 * 2.0 ** 23
TWO_PI_HI = 6.28125
TWO_PI_LO = 2.0 * np.pi - TWO_PI_HI
PI_IN = 3.1415925
LAM_INIT = 0.2

SLOTS = 4
UNIT = 11 * P
LINE = 640

PARAMS = [
    ("g_mix_pre", 8), ("g_mix_post", 8), ("g_ffn_pre", 8), ("g_ffn_post", 8), ("conv_w", 48),
    ("a_log", 1), ("dt_bias", 1), ("onorm", 1),
    ("na_q", 1), ("na_k", 1), ("da_q", 1), ("da_k", 1), ("subln", 1), ("gqa_q", 1), ("gqa_k", 1),
    ("lambdas", 4), ("cond", 16), ("b_ada0", 96), ("b_ada1", 96),
    ("ffn_w0", 66), ("ffn_w1", 66), ("ffn_b0", 22), ("ffn_b1", 22),
    ("hy_conv_w", 36), ("hy_conv_b", 12), ("hy_b", 3), ("hy_freq", 1), ("hy_skip", 4), ("hy_first", 1), ("eps", 1), ("one", 1),
]
COL = {}
_at = 0
for _name, _n in PARAMS:
    COL[_name] = (_at, _n)
    _at += _n
NPARAM = _at

CONSTS = [("ident", P), ("ones", P), ("ones_d", P), ("heads64", P), ("heads128", P), ("flip", P), ("rope_swap", P),
          ("later", P), ("upto", P), ("levels", 6 * P), ("na_mask", S), ("cos", S), ("sin", S)]
CCOL = {}
_at = 0
for _name, _n in CONSTS:
    CCOL[_name] = (_at, _n)
    _at += _n
NCONST = _at

STAGES = [
    "start", "norm1", "dil_project", "dil_attend", "gdn_project", "gdn_gates", "gdn_norm_qk", "gdn_masks",
    "gdn_products", "gdn_invert", "gdn_apply", "gdn_scan", "gdn_out", "mix1_out", "mix1_post", "norm2", "ffn1_up",
    "ffn1_down", "ffn1_post", "ada0",
    "mod_a0", "na_project", "na_norm", "na_attend", "diff_project", "diff_norm", "diff_attend", "diff_subln",
    "mix_e_out", "mod_f0", "ffn2_up", "ffn2_down", "ada1",
    "mod_a1", "gqa_project", "gqa_norm", "gqa_attend", "hy_project", "hy_filter", "hy_taps", "hy_forward",
    "hy_inverse", "mix_o_out", "mod_f1", "ffn3_up", "ffn3_down", "end",
]

STREAM = [
    ("w_dil_qk", 8, D), ("w_dil_v", 4, D), ("w_gdn", 16, D), ("w_gdn_gates", 1, 8 * DT), ("w_out1", 8, D),
    ("w_ffn1_up", 2 * FT, D), ("w_ffn1_down", 16, UNIT), ("w_ada0", 48, D),
    ("w_na_qk", 8, D), ("w_na_v", 4, D), ("w_diff_qk", 8, D), ("w_diff_v", 4, D), ("w_out_e", 8, D),
    ("w_ffn2_up", 2 * FT, D), ("w_ffn2_down", 16, UNIT), ("w_ada1", 48, D),
    ("w_gqa_qk", 5, D), ("w_gqa_v", 1, D), ("w_hy", 12, D), ("w_out_o", 8, D),
    ("w_ffn3_up", 2 * FT, D), ("w_ffn3_down", 16, UNIT),
]
FIRST = {}
_at = 0
for _name, _n, _w in STREAM:
    FIRST[_name] = _at
    _at += _n
NUNIT = _at


class Serial:

    def __init__(self, eng, own):
        self.eng, self.own, self.n, self.at, self.per = eng, own, 0, None, 0
        self.counts = {}

    def enter(self, at, per):
        self.at, self.per, self.begin = at, per, self.n

    def leave(self, passes):
        assert self.n == self.begin + self.per
        self.n = self.begin + passes * self.per
        self.at = None


def link(e, ins):
    e.n += 1
    ins.then_inc(e.own, 1)
    e.eng.wait_ge(e.own, e.n if e.at is None else e.at * e.per + (e.n - e.per))


class Core:

    def __init__(self, nc, ctx, dram):
        self.nc, self.ctx, self.dram = nc, ctx, dram
        sb = lambda name, cols: ctx.enter_context(nc.sbuf_tensor(name, [P, cols], F32))
        self.x = sb("x_res", DT * T)[:, :].rearrange("p (t n) -> p t n", t=DT)
        self.h_flat = sb("h_act", DT * T)
        self.h = self.h_flat[:, :].rearrange("p (t n) -> p t n", t=DT)
        self.mix_flat = sb("mix", DT * T)
        self.mix = self.mix_flat[:, :].rearrange("p (t n) -> p t n", t=DT)
        self.big = sb("big", FT * T)
        self.ring = sb("ring", SLOTS * UNIT)[:, :].rearrange("p (s n) -> p s n", s=SLOTS)
        self.sq = sb("sq", 2 * T)[:, :].rearrange("p (s n) -> p s n", s=2)
        self.rstd = sb("rstd", T)
        self.probs = sb("probs", 2 * T)[:, :].rearrange("p (s n) -> p s n", s=2)
        self.probs_t = sb("probs_t", T)
        self.params = sb("params", NPARAM)
        self.eps = self.par("eps")
        self.consts = sb("consts", NCONST)
        self.mod_flat = sb("mod", 96)
        self.mod = self.mod_flat[:, :].rearrange("p (n s) -> p n s", s=2)
        self.small = sb("small", 256)
        self.ps = ctx.enter_context(nc.psum_tensor("ps", [P, 8 * 512], F32))
        self.sems = {}
        self.sem = self._sem
        self.slot_landed = [self.sem(f"slot_landed_{i}") for i in range(SLOTS)]
        self.unit_done = self.sem("unit_done")
        self.loaded = self.sem("loaded")
        self.vector_stages = self.sem("vector_stages")
        self.scalar_stages = self.sem("scalar_stages")

    def _sem(self, name):
        if name not in self.sems:
            self.sems[name] = self.ctx.enter_context(self.nc.semaphore(name))
        return self.sems[name]

    def bank(self, b, n=512, off=0):
        return self.ps[:, b * 512 + off:b * 512 + off + n]

    def view(self, buf, off, *shape):
        n = int(np.prod(shape))
        ap = buf[:, off:off + n]
        if len(shape) == 2:
            ap = ap.rearrange("p (a b) -> p a b", a=shape[0])
        if len(shape) == 3:
            ap = ap.rearrange("p (a b c) -> p a b c", a=shape[0], b=shape[1])
        return ap

    def par(self, name, i=0, n=1):
        return self.params[:, COL[name][0] + i:COL[name][0] + i + n]

    def const(self, name, i=0, n=None):
        return self.consts[:, CCOL[name][0] + i:CCOL[name][0] + i + (n or P)]

    def after(self, eng, stage):
        eng.wait_ge(self.vector_stages, STAGES.index(stage) + 1)
        eng.wait_ge(self.scalar_stages, STAGES.index(stage) + 1)

    def slot_ready(self, eng, u, loop=None):
        more = 0 if loop is None else loop[0] * (16 * loop[1] // SLOTS)
        eng.wait_ge(self.slot_landed[u % SLOTS], more + 16 * (u // SLOTS + 1))



def stage_end(k, eng, sem, stage):
    eng.sem_inc(sem, 1)
    k.after(eng, stage)


def dense_tensor(k, pe, name, tiles, rhs, widths, upt=1, blocks=(8,), nbuf=4, evac=None, per_evac=1, loop=False):
    u0 = FIRST[name]
    per_pass = SLOTS // upt

    def body(it, static):
        for s in range(per_pass):
            j = (it * per_pass + s) if static else s
            if static:
                if j >= nbuf:
                    pe.wait_ge(evac, (j - nbuf) // per_evac + 1)
            else:
                pe.wait_ge(evac, it * (per_pass // per_evac) + (s - nbuf) // per_evac + 1)
            buf = (s if not static else j) % nbuf
            b = 0
            for q in range(upt):
                u = (u0 + j * upt + q)
                k.slot_ready(pe, u, None if static else (it, SLOTS))
                for i in range(blocks[q]):
                    col = 0
                    for n in widths:
                        last = pe.matmul(k.bank(2 * buf, n, col), k.ring[:, u % SLOTS, i * P:(i + 1) * P],
                                         rhs(b)[:, col:col + n], start=b == 0, stop=b == sum(blocks[:upt]) - 1)
                        col += n
                    b += 1
                last.then_inc(k.unit_done, 1)

    passes = tiles // per_pass
    if loop:
        body(0, True)
        with pe.Fori(1, passes) as it:
            body(it, False)
    else:
        for it in range(passes):
            body(it, True)
        for j in range(passes * per_pass, tiles):
            u = u0 + j
            if j >= nbuf:
                pe.wait_ge(evac, (j - nbuf) // per_evac + 1)
            k.slot_ready(pe, u)
            for b in range(blocks[0]):
                col = 0
                for n in widths:
                    last = pe.matmul(k.bank(2 * (j % nbuf), n, col), k.ring[:, u % SLOTS, b * P:(b + 1) * P],
                                     rhs(b)[:, col:col + n], start=b == 0, stop=b == blocks[0] - 1)
                    col += n
            last.then_inc(k.unit_done, 1)


def values_tensor(k, pe, name, blocks, width):
    u0 = FIRST[name]
    per = 1024 // width
    for u in range(DT // per):
        k.slot_ready(pe, u0 + u)
        for b in range(blocks):
            for i in range(per):
                kt = u * per + i
                last = pe.matmul(k.bank(b, width), k.h[:, kt, b * P:(b + 1) * P],
                                 k.ring[:, (u0 + u) % SLOTS, i * width:(i + 1) * width],
                                 start=kt == 0, stop=kt == DT - 1, skip_group_check=True)
        last.then_inc(k.unit_done, 1)


NORMS = ["norm1", "mix1_post", "norm2", "ffn1_post", "mod_a0", "mod_f0", "mod_a1", "mod_f1"]


def norms_before(name):
    return NORMS.index(name)


def scaled_before(name):
    return 2 * DT * (NORMS.index(name) - NORMS.index("mod_a0"))


def norm_scalar(k, s, name, src, n):
    ready, used, c0 = k.sem("norm_squares"), k.sem("norm_summed"), DT * norms_before(name)
    for t in range(DT):
        if t >= 2:
            s.eng.wait_ge(used, c0 + t - 1)
        s.eng.activation(k.sq[:, t % 2, 0:n], src[:, t, 0:n], ACT.Square).then_inc(ready, 1)
        s.eng.wait_ge(ready, c0 + t + 1)
    s.eng.wait_ge(used, c0 + DT)
    s.eng.activation(k.rstd[:, 0:n], k.ps[:, 0:n], ACT.Sqrt, bias=k.eps).then_inc(k.sem("norm_rooted"), 1)
    s.eng.wait_ge(k.sem("norm_rooted"), norms_before(name) + 1)


def norm_tensor(k, pe, name, n):
    ready, used, c0 = k.sem("norm_squares"), k.sem("norm_summed"), DT * norms_before(name)
    for t in range(DT):
        pe.wait_ge(ready, c0 + t + 1)
        last = pe.matmul(k.bank(0), k.const("ones_d"), k.sq[:, t % 2, 0:S], start=t == 0, stop=t == DT - 1)
        if n > S:
            last = pe.matmul(k.bank(1, n - S), k.const("ones_d"), k.sq[:, t % 2, S:n], start=t == 0, stop=t == DT - 1)
        last.then_inc(used, 1)


def norm_rstd(k, v, name, n):
    v.eng.wait_ge(k.sem("norm_rooted"), norms_before(name) + 1)
    link(v, v.eng.reciprocal(k.rstd[:, 0:n], k.rstd[:, 0:n]))


def modulate_vector(k, v, name, scale0, n):
    norm_rstd(k, v, name, n)
    for t in range(DT):
        for seq, (a, b) in enumerate(((0, S), (S, n))):
            if b > a:
                v.eng.scalar_tensor_tensor(k.h[:, t, a:b], k.x[:, t, a:b], k.mod[:, scale0 + t, seq:seq + 1],
                                           k.rstd[:, a:b], ALU.mult, ALU.mult).then_inc(k.sem("norm_scaled"), 1)
                v.eng.wait_ge(k.sem("norm_scaled"), scaled_before(name) + t * (1 + (n > S)) + seq + 1)


def modulate_scalar(k, s, name, shift0, n):
    norm_scalar(k, s, name, k.x, n)
    for t in range(DT):
        for seq, (a, b) in enumerate(((0, S), (S, n))):
            if b > a:
                s.eng.wait_ge(k.sem("norm_scaled"), scaled_before(name) + t * (1 + (n > S)) + seq + 1)
                link(s, s.eng.activation(k.h[:, t, a:b], k.h[:, t, a:b], ACT.Identity,
                                        bias=k.mod[:, shift0 + t, seq:seq + 1]))


class HeadNorm:

    def __init__(self, k, before, rotated_before, jobs):
        self.k, self.b, self.r, self.jobs = k, before, rotated_before, jobs
        self.squares, self.summed = k.sem("head_squares"), k.sem("head_summed")
        self.rooted, self.normed = k.sem("head_rooted"), k.sem("head_normed")
        self.swapped, self.rotated = k.sem("head_swapped"), k.sem("head_rotated")
        turns = [j[4] for j in jobs]
        self.before = [sum(turns[:i]) for i in range(len(jobs) + 1)]

    def scalar(self, s):
        k = self.k

        def root(j):
            n = self.jobs[j][0].shape[-1]
            s.eng.wait_ge(self.summed, self.b + j + 1)
            if j >= 2:
                s.eng.wait_ge(self.normed, self.b + j - 1)
            s.eng.activation(k.probs[:, j % 2, 0:n], k.ps[:, 1024 * (j % 2):1024 * (j % 2) + n], ACT.Sqrt,
                             bias=k.eps).then_inc(self.rooted, 1)
            s.eng.wait_ge(self.rooted, self.b + j + 1)

        for j, (x, _, _, _, _) in enumerate(self.jobs):
            if j >= 2:
                s.eng.wait_ge(self.summed, self.b + j - 1)
            s.eng.activation(k.sq[:, j % 2, 0:x.shape[-1]], x, ACT.Square).then_inc(self.squares, 1)
            s.eng.wait_ge(self.squares, self.b + j + 1)
            if j >= 1:
                root(j - 1)
        root(len(self.jobs) - 1)

    def tensor(self, pe):
        k = self.k

        def turn(j):
            x, _, _, _, rotate = self.jobs[j]
            if rotate:
                pe.wait_ge(self.normed, self.b + j + 1)
                if self.before[j]:
                    pe.wait_ge(self.rotated, self.r + self.before[j])
                pe.matmul(k.bank(4), k.const("rope_swap"), x[:, 0:S], start=True, stop=True).then_inc(self.swapped, 1)

        for j, (x, sums, _, _, _) in enumerate(self.jobs):
            n = x.shape[-1]
            pe.wait_ge(self.squares, self.b + j + 1)
            if j >= 2:
                pe.wait_ge(self.rooted, self.b + j - 1)
            last = pe.matmul(k.bank(2 * (j % 2)), sums, k.sq[:, j % 2, 0:S], start=True, stop=True)
            if n > S:
                last = pe.matmul(k.bank(2 * (j % 2) + 1, n - S), sums, k.sq[:, j % 2, S:n], start=True, stop=True)
            last.then_inc(self.summed, 1)
            if j >= 1:
                turn(j - 1)
        turn(len(self.jobs) - 1)

    def vector(self, v):
        k = self.k

        def turn(j):
            x, _, _, _, rotate = self.jobs[j]
            if rotate:
                v.eng.wait_ge(self.swapped, self.r + self.before[j] + 1)
                link(v, v.eng.tensor_tensor(k.probs_t[:, 0:S], k.bank(4), k.const("sin", 0, S), ALU.mult))
                link(v, v.eng.tensor_tensor(x[:, 0:S], x[:, 0:S], k.const("cos", 0, S), ALU.mult))
                v.eng.tensor_tensor(x[:, 0:S], x[:, 0:S], k.probs_t[:, 0:S], ALU.add).then_inc(self.rotated, 1)
                v.eng.wait_ge(self.rotated, self.r + self.before[j] + 1)

        for j, (x, _, gain, factor, _) in enumerate(self.jobs):
            n = x.shape[-1]
            v.eng.wait_ge(self.rooted, self.b + j + 1)
            link(v, v.eng.reciprocal(k.rstd[:, 0:n], k.probs[:, j % 2, 0:n]))
            if factor != 1.0:
                link(v, v.eng.tensor_scalar(k.rstd[:, 0:n], k.rstd[:, 0:n], factor, None, ALU.mult))
            if gain is None:
                ins = v.eng.tensor_tensor(x, x, k.rstd[:, 0:n], ALU.mult)
            else:
                ins = v.eng.scalar_tensor_tensor(x, x, gain, k.rstd[:, 0:n], ALU.mult, ALU.mult)
            ins.then_inc(self.normed, 1)
            v.eng.wait_ge(self.normed, self.b + j + 1)
            if j >= 1:
                turn(j - 1)
        turn(len(self.jobs) - 1)


class Attention:

    def __init__(self, k, before, products_before, items):
        self.k, self.b, self.items = k, before, items
        self.scores, self.maxed, self.exps = k.sem("att_scores"), k.sem("att_maxed"), k.sem("att_exps")
        self.normed, self.turned, self.copied = k.sem("att_normed"), k.sem("att_turned"), k.sem("att_copied")
        self.summed, self.stored = k.sem("att_summed"), k.sem("att_stored")
        self.m, n = [], products_before
        for it in items:
            self.m.append(n)
            n += not it["open"]

    def tensor(self, pe):
        k, N = self.k, len(self.items)
        for i in range(N + 2):
            if i < N:
                it = self.items[i]
                if i >= 2:
                    pe.wait_ge(self.exps, self.b + i - 1)
                base = 1024 * (i % 2)
                done = 0
                for kap, col in it["keys"]:
                    n = kap.shape[-1]
                    extra = [(a, b) for a, b, c in it["bias"] if c == col]
                    last = pe.matmul(k.ps[:, base + col:base + col + n], it["q"], kap, start=True, stop=not extra)
                    for e, (a, b) in enumerate(extra):
                        last = pe.matmul(k.ps[:, base + col:base + col + n], a, b, start=False, stop=e == len(extra) - 1)
                last.then_inc(self.scores, 1)
            if i >= 2 and not self.items[i - 2]["open"]:
                it, m = self.items[i - 2], self.m[i - 2]
                pe.wait_ge(self.copied, m + 1)
                if m >= self.m[0] + 2:
                    pe.wait_ge(self.stored, m - 1)
                for b, val in enumerate(it["values"]):
                    last = pe.matmul(k.bank(6 + m % 2, P), val, k.probs_t[:, b * P:(b + 1) * P], start=b == 0,
                                     stop=b == len(it["values"]) - 1)
                last.then_inc(self.summed, 1)
            if 1 <= i <= N and not self.items[i - 1]["open"]:
                it = self.items[i - 1]
                pe.wait_ge(self.normed, self.b + i)
                if self.m[i - 1] >= self.m[0] + 1:
                    pe.wait_ge(self.copied, self.m[i - 1])
                for b in range(len(it["values"])):
                    last = pe.transpose(k.bank(4 + b // 4, P, (b % 4) * P), k.probs[:, (i - 1) % 2, b * P:(b + 1) * P],
                                        k.const("ident"))
                last.then_inc(self.turned, 1)

    def vector(self, v):
        k, N = self.k, len(self.items)
        for i in range(N + 2):
            if i < N:
                n = P * len(self.items[i]["values"])
                v.eng.wait_ge(self.scores, self.b + i + 1)
                v.eng.tensor_reduce(k.small[:, i % 4:i % 4 + 1], k.ps[:, 1024 * (i % 2):1024 * (i % 2) + n],
                                    AX.X, ALU.max, negate=True).then_inc(self.maxed, 1)
                v.eng.wait_ge(self.maxed, self.b + i + 1)
            if 1 <= i <= N:
                it = self.items[i - 1]
                j, n = (i - 1) % 4, P * len(it["values"])
                pr = k.probs[:, (i - 1) % 2, 0:n]
                v.eng.wait_ge(self.exps, self.b + i)
                link(v, v.eng.reciprocal(k.small[:, 8 + j:9 + j], k.small[:, 4 + j:5 + j]))
                if it["factor"] is not None:
                    link(v, v.eng.tensor_tensor(k.small[:, 8 + j:9 + j], k.small[:, 8 + j:9 + j], it["factor"], ALU.mult))
                if it["adds"]:
                    ins = v.eng.scalar_tensor_tensor(pr, pr, k.small[:, 8 + j:9 + j], k.probs[:, i % 2, 0:n],
                                                     ALU.mult, ALU.add)
                else:
                    ins = v.eng.tensor_scalar(pr, pr, k.small[:, 8 + j:9 + j], None, ALU.mult)
                ins.then_inc(self.normed, 1)
                v.eng.wait_ge(self.normed, self.b + i)
            if i >= 2 and not self.items[i - 2]["open"]:
                it, m = self.items[i - 2], self.m[i - 2]
                v.eng.wait_ge(self.summed, m + 1)
                v.eng.tensor_copy(it["out"], k.bank(6 + m % 2, P)[it["rows"]]).then_inc(self.stored, 1)
                v.eng.wait_ge(self.stored, m + 1)

    def scalar(self, s):
        k, N = self.k, len(self.items)
        for i in range(N + 1):
            if i < N:
                n = P * len(self.items[i]["values"])
                s.eng.wait_ge(self.maxed, self.b + i + 1)
                if i >= 2:
                    if self.items[i - 2]["open"]:
                        s.eng.wait_ge(self.normed, self.b + i)
                    else:
                        s.eng.wait_ge(self.turned, self.m[i - 2] + 1)
                s.eng.activation(k.probs[:, i % 2, 0:n], k.ps[:, 1024 * (i % 2):1024 * (i % 2) + n], ACT.Exp,
                                 bias=k.small[:, i % 4:i % 4 + 1],
                                 accum_out=k.small[:, 4 + i % 4:5 + i % 4]).then_inc(self.exps, 1)
                s.eng.wait_ge(self.exps, self.b + i + 1)
            if i >= 1 and not self.items[i - 1]["open"]:
                n = P * len(self.items[i - 1]["values"])
                m = self.m[i - 1]
                s.eng.wait_ge(self.turned, m + 1)
                if m >= self.m[0] + 1:
                    s.eng.wait_ge(self.summed, m)
                s.eng.copy(k.probs_t[:, 0:n], k.ps[:, 2048:2048 + n]).then_inc(self.copied, 1)
                s.eng.wait_ge(self.copied, m + 1)


def plain_norm(k, eng, kind, name, gain, n):
    if kind == "scalar":
        norm_scalar(k, eng, name, k.x, n)
    if kind == "tensor":
        norm_tensor(k, eng, name, n)
    if kind == "vector":
        norm_rstd(k, eng, name, n)
        for t in range(DT):
            link(eng, eng.eng.scalar_tensor_tensor(k.h[:, t, 0:n], k.x[:, t, 0:n], k.par(gain, t), k.rstd[:, 0:n],
                                                  ALU.mult, ALU.mult))


def post_norm_vector(k, v, name, m, gain):
    norm_rstd(k, v, name, S)
    for t in range(DT):
        link(v, v.eng.scalar_tensor_tensor(m[:, t, 0:S], m[:, t, 0:S], k.par(gain, t), k.rstd[:, 0:S],
                                          ALU.mult, ALU.mult))
        link(v, v.eng.tensor_tensor(k.x[:, t, 0:S], k.x[:, t, 0:S], m[:, t, 0:S], ALU.add))


def copy_out_scalar(k, s, name, tiles, dst, width, evac, scale=None):
    for j in range(tiles):
        s.eng.wait_ge(k.unit_done, FIRST[name] + j + 1)
        w = width(j)
        src = k.ps[:, 1024 * (j % 4):1024 * (j % 4) + w]
        s.eng.activation(dst(j), src, ACT.Copy, scale=1.0 if scale is None else scale(j)).then_inc(evac, 1)
        s.eng.wait_ge(evac, j + 1)


def residual_vector(k, v, name, gate0, n, upt, nbuf, evac, loop):
    u0 = FIRST[name]
    parts = ((0, S), (S, n)) if n > S else ((0, S),)

    def tile(j, buf, value, ready):
        v.eng.wait_ge(k.unit_done, ready)
        for seq, (a, b) in enumerate(parts):
            ins = v.eng.scalar_tensor_tensor(k.x[:, j, a:b], k.ps[:, 1024 * buf + a:1024 * buf + b],
                                             k.mod[:, gate0 + j, seq:seq + 1], k.x[:, j, a:b], ALU.mult, ALU.add)
            if seq == len(parts) - 1:
                ins.then_inc(evac, 1)
                v.eng.wait_ge(evac, value)
            else:
                link(v, ins)

    if not loop:
        for j in range(DT):
            tile(j, j % nbuf, j + 1, u0 + upt * (j + 1))
        return
    for s in range(2):
        tile(s, s, s + 1, u0 + upt * (s + 1))
    with v.eng.Fori(1, DT // 2) as it:
        v.enter(it, 2 * (len(parts) - 1))
        for s in range(2):
            tile(it * 2 + s, s, it * 2 + (s + 1), it * SLOTS + (u0 + upt * (s + 1)))
    v.leave(DT // 2 - 1)


def copy_down_vector(k, v, name, dst, evac):
    u0 = FIRST[name]

    def tile(j, buf, value, ready):
        v.eng.wait_ge(k.unit_done, ready)
        v.eng.tensor_copy(dst[:, j, 0:S], k.bank(2 * buf)).then_inc(evac, 1)
        v.eng.wait_ge(evac, value)

    for s in range(2):
        tile(s, s, s + 1, u0 + 2 * (s + 1))
    with v.eng.Fori(1, DT // 2) as it:
        for s in range(2):
            tile(it * 2 + s, s, it * 2 + (s + 1), it * SLOTS + (u0 + 2 * (s + 1)))



def ffn_buffers(k, m):
    return 1024 * ((2 * m) % 4), 1024 * ((2 * m + 1) % 4)


def ffn_up_scalar(k, s, name, conv, n):
    lin, act, hid, taps = k.sem(name + "_lin"), k.sem(name + "_act"), k.sem(name + "_hidden"), k.sem(name + "_taps")
    u0 = FIRST[name]

    def tile(m, a, more, static):
        g, _ = ffn_buffers(k, a)
        tmp = k.probs[:, a, 0:n]
        s.eng.wait_ge(k.unit_done, m * 2 + (u0 + 1))
        if not static or m >= 2:
            s.eng.wait_ge(hid, m - 1)
        if conv is None:
            s.eng.activation(tmp, k.ps[:, g:g + n], ACT.Silu).then_inc(act, 1)
            s.eng.wait_ge(act, m + 1)
        else:
            w, b = conv
            s.eng.activation(tmp, k.ps[:, g:g + n], ACT.Identity, bias=k.params[:, b(m)], scale=k.params[:, w(m, 1)]).then_inc(lin, 1)
            s.eng.wait_ge(lin, m + 1)
            s.eng.wait_ge(taps, m + 1)
            s.eng.activation(tmp, tmp, ACT.Silu).then_inc(act, 1)
            s.eng.wait_ge(act, m + 1)

    for a in range(2):
        tile(a, a, 0, True)
    with s.eng.Fori(1, FT // 2) as it:
        for a in range(2):
            tile(it * 2 + a, a, it, False)


def ffn_up_vector(k, v, name, conv, n, hidden):
    lin, act, hid, taps = k.sem(name + "_lin"), k.sem(name + "_act"), k.sem(name + "_hidden"), k.sem(name + "_taps")
    u0 = FIRST[name]
    parts = ((0, S), (S, n)) if n > S else ((0, S),)

    def tile(m, a):
        g, u = ffn_buffers(k, a)
        tmp = k.probs[:, a, :]
        if conv is not None:
            w, _ = conv
            v.eng.wait_ge(lin, m + 1)
            for q, (lo, hi) in enumerate(parts):
                link(v, v.eng.scalar_tensor_tensor(tmp[:, lo + 1:hi], k.ps[:, g + lo:g + hi - 1], k.params[:, w(m, 0)],
                                                  tmp[:, lo + 1:hi], ALU.mult, ALU.add))
                ins = v.eng.scalar_tensor_tensor(tmp[:, lo:hi - 1], k.ps[:, g + lo + 1:g + hi], k.params[:, w(m, 2)],
                                                 tmp[:, lo:hi - 1], ALU.mult, ALU.add)
                if q == len(parts) - 1:
                    ins.then_inc(taps, 1)
                    v.eng.wait_ge(taps, m + 1)
                else:
                    link(v, ins)
        v.eng.wait_ge(k.unit_done, m * 2 + (u0 + 2))
        v.eng.wait_ge(act, m + 1)
        v.eng.tensor_tensor(hidden[:, m, 0:n], tmp[:, 0:n], k.ps[:, u:u + n], ALU.mult).then_inc(hid, 1)
        v.eng.wait_ge(hid, m + 1)

    for a in range(2):
        tile(a, a)
    with v.eng.Fori(1, FT // 2) as it:
        if conv is not None:
            v.enter(it, 2 * (2 * len(parts) - 1))
        for a in range(2):
            tile(it * 2 + a, a)
    if conv is not None:
        v.leave(FT // 2 - 1)


def ffn_conv(layer):
    w0, b0 = COL[f"ffn_w{layer}"][0], COL[f"ffn_b{layer}"][0]
    return (lambda m, tap: bass.ds(m * 3 + (w0 + tap), 1)), (lambda m: bass.ds(m + b0, 1))



def ada_tensor(k, pe, name, layer):
    u0, left = FIRST[name], k.sem(name + "_left")

    def half(it, a, static):
        if not static:
            pe.wait_ge(left, it * 2 + (a - 1))
        for s in range(4):
            u = u0 + 4 * a + s
            k.slot_ready(pe, u, None if static else (it, 8))
            for b in range(DT):
                last = pe.matmul(k.bank(a, 2, 2 * s), k.ring[:, u % SLOTS, b * P:(b + 1) * P],
                                 k.small[:, 96 + 2 * b:98 + 2 * b], start=b == 0, stop=b == DT - 1)
            last.then_inc(k.unit_done, 1)

    half(0, 0, True)
    half(0, 1, True)
    with pe.Fori(1, 6) as it:
        half(it, 0, False)
        half(it, 1, False)


def ada_vector(k, v, name, layer):
    u0, left = FIRST[name], k.sem(name + "_left")
    b0 = COL[f"b_ada{layer}"][0]
    flat = k.mod_flat

    with v.eng.Fori(0, 6) as it:
        for a in range(2):
            v.eng.wait_ge(k.unit_done, it * 8 + (u0 + 4 * a + 4))
            v.eng.tensor_tensor(flat[:, bass.ds(it * 16 + 8 * a, 8)], k.bank(a, 8),
                                k.params[:, bass.ds(it * 16 + (b0 + 8 * a), 8)], ALU.add).then_inc(left, 1)
            v.eng.wait_ge(left, it * 2 + (a + 1))
    for at in (8, 32):
        link(v, v.eng.tensor_scalar(k.mod[:, at:at + 8, :], k.mod[:, at:at + 8, :], 1.0, None, ALU.add))



def gdn_views(k):
    b = {}
    b["qkvg"] = k.view(k.big, 0, 16, S)
    b["v_out"] = k.view(k.big, 4096, GH, PAIRS * P)
    b["at"] = k.view(k.big, 4096, 16, P)
    b["k_tok"] = k.view(k.big, 8192, 16, P)
    b["v_tok"] = k.view(k.big, 10240, 16, P)
    b["a"] = k.view(k.big, 12288, 16, P)
    b["t"] = k.view(k.big, 14336, 16, P)
    b["kbe"] = k.view(k.big, 2048, 16, P)
    b["tt"] = k.view(k.h_flat, 0, 16, P)
    b["attn"] = k.view(k.h_flat, 2048, 16, P)
    b["egc"] = k.view(k.h_flat, 4096, GH, S)
    b["am"] = k.view(k.mix_flat, 0, 16, P)
    b["state"] = k.view(k.probs_t, 0, GH, P)
    b["v_new"] = k.sq[:, 0, 0:S].rearrange("p (h n) -> p h n", h=GH)
    return b


def attn_views(k):
    return (k.view(k.big, 0, 4, T), k.view(k.big, 4 * T, 4, T), k.view(k.big, 8 * T, 6, HALF))


def dil_views(k):
    return (k.view(k.big, 0, 4, S), k.view(k.big, 2048, 4, S), k.view(k.big, 4096, 4, HALF),
            k.view(k.big, 6144, 8, S))


def item(q, keys, bias, values, out, rows=slice(0, P), factor=None, adds=False, is_open=False):
    return dict(q=q, keys=keys, bias=bias, values=values, out=out, rows=rows, factor=factor, adds=adds, open=is_open)


def dil_items(k):
    q, key, val, bias = dil_views(k)
    out = []
    for h in range(8):
        r, t = slice(HD * (h % 2), HD * (h % 2) + HD), h // 2
        for i in range(4):
            n = (i + 1) * P
            blk = slice(i * P, n)
            out.append(item(q[r, t, blk], [(key[r, t, 0:n], 0)],
                            [(k.const("flip"), bias[:, h, S - n:S], 0)],
                            [val[:, b, t * P:(t + 1) * P] for b in range(i + 1)], k.mix[r, 4 + t, blk], rows=r))
    return out


def na_items(k):
    q, key, val = attn_views(k)
    bias = k.view(k.big, 12 * T, 8, 14 * GRID_W)
    out = []
    for h in range(8):
        r, t = slice(HD * (h % 2), HD * (h % 2) + HD), h // 2
        vals = [val[:, b, t * P:(t + 1) * P] for b in range(6)]
        for i in range(6):
            blk = slice(i * P, (i + 1) * P)
            if i < 4:
                out.append(item(q[r, t, blk], [(key[r, t, 0:S], 0), (key[r, t, S:T], S)],
                                [(k.const("flip"), bias[:, h, (6 - 2 * i) * GRID_W:(6 - 2 * i) * GRID_W + S], 0),
                                 (k.const("ident"), k.const("na_mask", 0, S), 0)],
                                vals, k.mix[r, t, blk], rows=r))
            else:
                out.append(item(q[r, t, blk], [(key[r, t, S:T], 0)], [], vals[4:], k.mix[r, t, blk], rows=r))
    return out


def diff_items(k):
    q, key, val = attn_views(k)
    out = []
    for t in range(4):
        vals = [val[:, b, t * P:(t + 1) * P] for b in range(6)]
        for i in range(6):
            blk = slice(i * P, (i + 1) * P)
            for sub in range(2):
                r = slice(HD * sub, HD * sub + HD)
                keys = [(key[r, t, 0:S], 0), (key[r, t, S:T], S)] if i < 4 else [(key[r, t, S:T], 0)]
                out.append(item(q[r, t, blk], keys, [], vals if i < 4 else vals[4:], k.mix[:, 4 + t, blk],
                                factor=k.small[:, 116:117] if sub else None, adds=sub == 1, is_open=sub == 0))
    return out


def gqa_views(k):
    return k.view(k.big, 0, 4, T), k.view(k.big, 4 * T, 1, T), k.view(k.big, 5 * T, 6, P)


def gqa_items(k):
    q, key, val = gqa_views(k)
    out = []
    for t in range(4):
        for e in range(2):
            r = slice(HD * e, HD * e + HD)
            for i in range(4):
                blk = slice(i * P, (i + 1) * P)
                out.append(item(q[r, t, blk], [(key[r, 0, 0:S], 0), (key[r, 0, S:T], S)], [],
                                [val[:, b, :] for b in range(6)], k.mix[r, t, blk], rows=r))
    return out


def na_norm(k):
    q, key, _ = attn_views(k)
    return HeadNorm(k, 8, 0, [(q[:, t, :], k.const("heads64"), k.par("na_q"), HD ** -0.5, False) for t in range(4)]
                    + [(key[:, t, :], k.const("heads64"), k.par("na_k"), 1.0, False) for t in range(4)])


def diff_norm(k):
    q, key, _ = attn_views(k)
    return HeadNorm(k, 16, 0, [(q[:, t, :], k.const("heads64"), k.par("da_q"), HD ** -0.5, True) for t in range(4)]
                    + [(key[:, t, :], k.const("heads64"), k.par("da_k"), 1.0, True) for t in range(4)])


def gqa_norm(k):
    q, key, _ = gqa_views(k)
    return HeadNorm(k, 28, 8, [(q[:, t, 0:S], k.const("heads64"), k.par("gqa_q"), HD ** -0.5, True) for t in range(4)]
                    + [(key[:, 0, :], k.const("heads64"), k.par("gqa_k"), 1.0, True)])


def gdn_norm(k):
    x = gdn_views(k)["qkvg"]
    return HeadNorm(k, 0, 0, [(x[:, t, :], k.const("ones"), None, P ** -0.5 if t < 4 else 1.0, False)
                                    for t in range(8)])


def subln(k):
    return HeadNorm(k, 24, 8, [(k.mix[:, 4 + t, :], k.const("heads128"), k.par("subln"), 1.0 - LAM_INIT, False)
                                 for t in range(4)])


def hy_views(k):
    b = {}
    b["x"] = k.view(k.big, 0, 12, S)
    b["z"] = k.view(k.big, 6144, 4, S)
    b["even"] = k.view(k.big, 8192, 4, S)
    b["odd"] = k.view(k.big, 10240, 4, S)
    b["yc"] = k.view(k.big, 12288, 4, S)
    b["ys"] = k.view(k.big, 14336, 4, S)
    b["w4"] = k.big[0:ORDER, 12288:12288 + D]
    b["w1"] = k.big[0:EMB, 13312:13312 + ORDER]
    b["w2"] = k.big[0:ORDER, 13376:13376 + ORDER]
    b["w3"] = k.big[0:ORDER, 13440:13440 + ORDER]
    b["feats"] = k.big[0:EMB, 13568:13568 + S]
    b["cos"] = k.view(k.h_flat, 0, 4, S)
    b["sin"] = k.view(k.h_flat, 2048, 4, S)
    b["decay"] = k.view(k.h_flat, 4096, 4, S)
    return b



def spread(ap, n):
    return ap.unsqueeze(2).broadcast_to([ap.shape[0], ap.shape[1], n])


def by_head(k, col):
    return k.small[:, col:col + 16].rearrange("p (b h) -> p h b", h=GH)


def all_blocks(mat):
    return mat.unsqueeze(1).broadcast_to([P, 16, P])


def start_vector(k, v):
    v.eng.wait_ge(k.loaded, 64)
    v.eng.tensor_tensor(k.small[0:HD, 112:114], k.params[0:HD, COL["lambdas"][0]:COL["lambdas"][0] + 2],
                        k.params[0:HD, COL["lambdas"][0] + 2:COL["lambdas"][0] + 4], ALU.mult).then_inc(k.sem("lam_products"), 1)
    v.eng.wait_ge(k.sem("lam_products"), 1)
    v.eng.wait_ge(k.sem("lam_exps"), 1)
    link(v, v.eng.scalar_tensor_tensor(k.small[:, 116:117], k.small[:, 115:116], -LAM_INIT, k.small[:, 114:115],
                                      ALU.add, ALU.subtract))


def start_tensor(k, pe):
    pe.wait_ge(k.loaded, 64)
    pe.wait_ge(k.sem("lam_products"), 1)
    pe.matmul(k.bank(7, 2), k.consts[0:HD, CCOL["ones"][0]:CCOL["ones"][0] + P], k.small[0:HD, 112:114],
              start=True, stop=True).then_inc(k.sem("lam_sums"), 1)


def start_scalar(k, s):
    s.eng.wait_ge(k.loaded, 64)
    link(s, s.eng.activation(k.small[:, 96:112], k.par("cond", 0, 16), ACT.Silu))
    s.eng.wait_ge(k.sem("lam_sums"), 1)
    s.eng.activation(k.small[:, 114:116], k.bank(7, 2), ACT.Exp).then_inc(k.sem("lam_exps"), 1)
    s.eng.wait_ge(k.sem("lam_exps"), 1)


def values_vector(k, v, name, units, dst, width, blocks):
    v.eng.wait_ge(k.unit_done, FIRST[name] + units)
    for b in range(blocks):
        link(v, v.eng.tensor_copy(dst[:, b, :], k.bank(b, width)))



def dil_project_tensor(k, pe):
    dense_tensor(k, pe, "w_dil_qk", 8, lambda b: k.h[:, b, :], (S,), evac=k.sem("dil_project_evac"))
    pe.wait_ge(k.sem("dil_project_evac"), 8)
    pe.wait_ge(k.sem("dil_tables"), 48)
    hot, rel, logs = k.big[0:BUCKETS, 10240:10240 + LINE], k.big[0:BUCKETS, 10880:10888], k.big[0:1, 10888:10888 + LINE]
    for off, n, b in ((0, 512, 6), (512, LINE - 512, 7)):
        pe.matmul(k.ps[0:8, b * 512:b * 512 + n], rel, hot[:, off:off + n], start=True, stop=False)
        last = pe.matmul(k.ps[0:8, b * 512:b * 512 + n], k.consts[0:1, CCOL["ones"][0]:CCOL["ones"][0] + 8],
                         logs[:, off:off + n], start=False, stop=True)
    last.then_inc(k.sem("dil_lines"), 1)
    values_tensor(k, pe, "w_dil_v", 4, HALF)


def dil_project_vector(k, v):
    v.eng.wait_ge(k.sem("dil_lines"), 1)
    v.eng.tensor_copy(k.big[0:8, 11528:11528 + LINE], k.ps[0:8, 6 * 512:6 * 512 + LINE]).then_inc(k.sem("dil_lines_kept"), 1)
    v.eng.wait_ge(k.sem("dil_lines_kept"), 1)
    values_vector(k, v, "w_dil_v", 4, dil_views(k)[2], HALF, 4)


def dil_project_scalar(k, s):
    q, key, _, _ = dil_views(k)
    copy_out_scalar(k, s, "w_dil_qk", 8, lambda j: (q if j < 4 else key)[:, j % 4, :], lambda j: S,
                    k.sem("dil_project_evac"), lambda j: HD ** -0.5 if j < 4 else 1.0)


def gdn_project_tensor(k, pe):
    dense_tensor(k, pe, "w_gdn", 16, lambda b: k.h[:, b, :], (S,), evac=k.sem("gdn_taps"))
    u = FIRST["w_gdn_gates"]
    k.slot_ready(pe, u)
    pe.wait_ge(k.sem("gdn_gate_left"), 2)
    for half in range(2):
        for b in range(DT):
            last = pe.matmul(k.ps[0:GH, half * 512:half * 512 + S], k.ring[:, u % SLOTS, b * 8 + half * GH:b * 8 + half * GH + GH],
                             k.h[:, b, 0:S], start=b == 0, stop=b == DT - 1)
    last.then_inc(k.unit_done, 1)


def gdn_project_scalar(k, s):
    x = gdn_views(k)["qkvg"]

    def silu(j):
        s.eng.wait_ge(k.sem("gdn_taps"), j + 1)
        link(s, s.eng.activation(x[:, j, :], x[:, j, :], ACT.Silu))

    for j in range(16):
        s.eng.wait_ge(k.unit_done, FIRST["w_gdn"] + j + 1)
        src = k.bank(2 * (j % 4))
        if j < 12:
            s.eng.activation(x[:, j, :], src, ACT.Copy, scale=k.par("conv_w", 4 * j + 3)).then_inc(k.sem("gdn_lin"), 1)
            s.eng.wait_ge(k.sem("gdn_lin"), j + 1)
        else:
            s.eng.activation(x[:, j, :], src, ACT.Silu).then_inc(k.sem("gdn_gate_left"), 1)
            s.eng.wait_ge(k.sem("gdn_gate_left"), j - 11)
        if 1 <= j <= 12:
            silu(j - 1)


def gdn_project_vector(k, v):
    x = gdn_views(k)["qkvg"]
    for j in range(12):
        v.eng.wait_ge(k.sem("gdn_lin"), j + 1)
        for back in (1, 2, 3):
            ins = v.eng.scalar_tensor_tensor(x[:, j, back:S], k.bank(2 * (j % 4), S - back), k.par("conv_w", 4 * j + 3 - back),
                                             x[:, j, back:S], ALU.mult, ALU.add)
            if back == 3:
                ins.then_inc(k.sem("gdn_taps"), 1)
                v.eng.wait_ge(k.sem("gdn_taps"), j + 1)
            else:
                link(v, ins)


def gdn_gates_scalar(k, s):
    r = slice(0, GH)
    s.eng.wait_ge(k.unit_done, FIRST["w_gdn_gates"] + 1)
    s.eng.activation(k.probs[r, 0, 0:S], k.ps[r, 0:S], ACT.Exp, scale=-1.0).then_inc(k.sem("gates_exp"), 1)
    s.eng.wait_ge(k.sem("gates_exp"), 1)
    link(s, s.eng.activation(k.small[r, 120:121], k.par("a_log")[r], ACT.Exp))
    s.eng.wait_ge(k.sem("gates_abs"), 1)
    link(s, s.eng.activation(k.rstd[r, 0:S], k.rstd[r, 0:S], ACT.Exp, scale=-1.0))
    s.eng.activation(k.rstd[r, 0:S], k.rstd[r, 0:S], ACT.Ln, bias=k.par("one")[r]).then_inc(k.sem("gates_exp"), 1)
    s.eng.wait_ge(k.sem("gates_exp"), 2)
    s.eng.wait_ge(k.sem("gates_sums"), 1)
    link(s, s.eng.activation(k.small[:, 48:64], k.bank(4, 16), ACT.Exp))
    s.eng.activation(k.small[:, 64:80], k.bank(5, 16), ACT.Exp).then_inc(k.sem("gates_exp"), 1)
    s.eng.wait_ge(k.sem("gates_exp"), 3)


def gdn_gates_vector(k, v):
    r = slice(0, GH)
    beta, y, soft = k.probs[r, 0, 0:S], k.probs[r, 1, 0:S], k.rstd[r, 0:S]
    v.eng.wait_ge(k.unit_done, FIRST["w_gdn_gates"] + 1)
    link(v, v.eng.tensor_scalar(y, k.ps[r, 512:512 + S], k.par("dt_bias")[r], None, ALU.add))
    v.eng.scalar_tensor_tensor(soft, y, -1.0, y, ALU.mult, ALU.max).then_inc(k.sem("gates_abs"), 1)
    v.eng.wait_ge(k.sem("gates_abs"), 1)
    v.eng.wait_ge(k.sem("gates_exp"), 2)
    link(v, v.eng.tensor_scalar(beta, beta, 1.0, None, ALU.add))
    link(v, v.eng.reciprocal(beta, beta))
    link(v, v.eng.scalar_tensor_tensor(y, y, 0.0, soft, ALU.max, ALU.add))
    v.eng.tensor_scalar(y, y, k.small[r, 120:121], -1.0, ALU.mult, ALU.mult).then_inc(k.sem("gates_rows"), 1)
    v.eng.wait_ge(k.sem("gates_rows"), 1)
    v.eng.wait_ge(k.sem("gates_turned"), 1)
    v.eng.tensor_copy(k.small[:, 16:48], k.bank(2, 32)).then_inc(k.sem("gates_cols"), 1)
    v.eng.wait_ge(k.sem("gates_cols"), 1)
    v.eng.wait_ge(k.sem("gates_exp"), 3)
    link(v, v.eng.tensor_tensor(k.small[:, 80:96], k.small[:, 48:64], k.small[:, 32:48], ALU.mult))


def gdn_gates_tensor(k, pe):
    r = slice(0, GH)
    pe.wait_ge(k.sem("gates_rows"), 1)
    for row, col in ((1, 0), (0, 16)):
        for b in range(PAIRS):
            last = pe.transpose(k.bank(2, GH, col + GH * b), k.probs[r, row, b * P:(b + 1) * P], k.const("ident")[r, 0:GH])
    last.then_inc(k.sem("gates_turned"), 1)
    pe.wait_ge(k.sem("gates_cols"), 1)
    pe.matmul(k.bank(4, 16), k.const("upto"), k.small[:, 16:32], start=True, stop=True)
    pe.matmul(k.bank(5, 16), k.const("later"), k.small[:, 16:32], start=True, stop=True).then_inc(k.sem("gates_sums"), 1)


def gdn_masks_tensor(k, pe):
    m = gdn_views(k)
    left = k.sem("masks_left")
    for g in range(8):
        if g >= 2:
            pe.wait_ge(left, g - 1)
        for b in range(PAIRS):
            last = pe.transpose(k.bank(g % 2, P, b * P), m["qkvg"][:, 4 + g, b * P:(b + 1) * P], k.const("ident"))
        last.then_inc(k.sem("masks_turned"), 1)
    pe.wait_ge(k.sem("masks_decays"), 1)
    for h in range(GH):
        if h >= 1:
            pe.wait_ge(k.sem("masks_exp"), 3 * h)
        for b in range(PAIRS):
            i = 4 * h + b
            pe.matmul(k.bank(2, P, b * P), k.const("upto"), m["tt"][:, i, :], start=True, stop=True)
            pe.matmul(k.bank(3, P, b * P), m["tt"][:, i, :], k.const("upto"), start=True, stop=True)
            last = pe.matmul(k.bank(4, P, b * P), m["attn"][:, i, :], k.const("upto"), start=True, stop=True)
        last.then_inc(k.sem("masks_sums"), 1)


def gdn_masks_vector(k, v):
    m = gdn_views(k)
    g_col = by_head(k, 16)
    for h in range(GH):
        link(v, v.eng.tensor_tensor(m["tt"][:, 4 * h:4 * h + 4, :], k.const("later").unsqueeze(1).broadcast_to([P, 4, P]),
                                   spread(g_col[:, h, :], P), ALU.mult))
        ins = v.eng.tensor_tensor(m["attn"][:, 4 * h:4 * h + 4, :], k.const("ones").unsqueeze(1).broadcast_to([P, 4, P]),
                                  spread(g_col[:, h, :], P), ALU.mult)
        if h < GH - 1:
            link(v, ins)
        else:
            ins.then_inc(k.sem("masks_decays"), 1)
            v.eng.wait_ge(k.sem("masks_decays"), 1)
    for g in range(8):
        v.eng.wait_ge(k.sem("masks_turned"), g + 1)
        src = k.bank(g % 2).rearrange("p (b n) -> p b n", b=PAIRS)
        if g < 4:
            ins = v.eng.tensor_copy(m["k_tok"][:, 4 * g:4 * g + 4, :], src)
        else:
            ins = v.eng.tensor_tensor(m["v_tok"][:, 4 * g - 16:4 * g - 12, :], src, spread(by_head(k, 32)[:, g - 4, :], P),
                                      ALU.mult)
        ins.then_inc(k.sem("masks_left"), 1)
        v.eng.wait_ge(k.sem("masks_left"), g + 1)
    v.eng.wait_ge(k.sem("masks_exp"), 12)
    link(v, v.eng.tensor_tensor(m["a"], m["a"], all_blocks(k.const("later")), ALU.mult))
    link(v, v.eng.tensor_tensor(m["at"], m["at"], all_blocks(k.const("upto")), ALU.mult))


def gdn_masks_scalar(k, s):
    m = gdn_views(k)
    s.eng.wait_ge(k.sem("masks_turned"), 8)
    for h in range(GH):
        s.eng.wait_ge(k.sem("masks_sums"), h + 1)
        blk = slice(4 * h, 4 * h + 4)
        for n, (dst, b) in enumerate(((m["a"][:, blk, :], 2), (m["at"][:, blk, :], 3),
                                      (m["egc"][:, h, :].rearrange("p (b n) -> p b n", b=4), 4))):
            s.eng.activation(dst, k.bank(b).rearrange("p (b n) -> p b n", b=4), ACT.Exp).then_inc(k.sem("masks_exp"), 1)
            s.eng.wait_ge(k.sem("masks_exp"), 3 * h + n + 1)


def gdn_products_tensor(k, pe):
    m = gdn_views(k)
    x = m["qkvg"]
    for h in range(GH):
        for b in range(PAIRS):
            kb = x[:, 4 + h, b * P:(b + 1) * P]
            pe.matmul(k.bank(h, P, b * P), kb, kb, start=True, stop=True)
            last = pe.matmul(k.bank(4 + h, P, b * P), kb, x[:, h, b * P:(b + 1) * P], start=True, stop=True)
        last.then_inc(k.sem("products_made"), 1)
    for h in range(GH):
        pe.wait_ge(k.sem("products_used"), h + 1)
        for b in range(PAIRS):
            last = pe.transpose(k.bank(h, P, b * P), m["a"][:, 4 * h + b, :], k.const("ident"))
        last.then_inc(k.sem("products_turned"), 1)


def gdn_products_vector(k, v):
    m = gdn_views(k)
    four = lambda ap: ap.rearrange("p (b n) -> p b n", b=4)
    for h in range(GH):
        blk = slice(4 * h, 4 * h + 4)
        v.eng.wait_ge(k.sem("products_made"), h + 1)
        link(v, v.eng.tensor_tensor(m["attn"][:, blk, :], four(k.bank(4 + h)), m["at"][:, blk, :], ALU.mult))
        link(v, v.eng.tensor_tensor(m["a"][:, blk, :], m["a"][:, blk, :], spread(by_head(k, 32)[:, h, :], P), ALU.mult))
        v.eng.tensor_tensor(m["a"][:, blk, :], four(k.bank(h)), m["a"][:, blk, :], ALU.mult).then_inc(k.sem("products_used"), 1)
        v.eng.wait_ge(k.sem("products_used"), h + 1)
    for h in range(GH):
        v.eng.wait_ge(k.sem("products_turned"), h + 1)
        link(v, v.eng.tensor_copy(m["at"][:, 4 * h:4 * h + 4, :], four(k.bank(h))))
    link(v, v.eng.tensor_copy(m["t"], all_blocks(k.const("ident"))))
    link(v, v.eng.tensor_copy(m["tt"], all_blocks(k.const("ident"))))


LEVELS = 6


def gdn_invert_vector(k, v):
    m = gdn_views(k)
    four = lambda ap: ap.rearrange("p (b n) -> p b n", b=4)
    for lev in range(LEVELS):
        v.eng.tensor_tensor(m["am"], m["at"], all_blocks(k.const("levels", lev * P)), ALU.mult).then_inc(k.sem("inv_masked"), 1)
        v.eng.wait_ge(k.sem("inv_masked"), lev + 1)
        for h in range(GH):
            blk = slice(4 * h, 4 * h + 4)
            v.eng.wait_ge(k.sem("inv_z"), GH * lev + h + 1)
            link(v, v.eng.tensor_tensor(m["t"][:, blk, :], m["t"][:, blk, :], four(k.bank(4 + h)), ALU.subtract))
            v.eng.tensor_tensor(m["tt"][:, blk, :], m["tt"][:, blk, :], four(k.bank(h)), ALU.subtract).then_inc(k.sem("inv_updated"), 1)
            v.eng.wait_ge(k.sem("inv_updated"), GH * lev + h + 1)


def gdn_invert_tensor(k, pe):
    m = gdn_views(k)
    for lev in range(LEVELS):
        pe.wait_ge(k.sem("inv_masked"), lev + 1)
        for h in range(GH):
            if lev >= 1:
                pe.wait_ge(k.sem("inv_updated"), GH * (lev - 1) + h + 1)
            for b in range(PAIRS):
                last = pe.matmul(k.bank(h, P, b * P), m["am"][:, 4 * h + b, :], m["t"][:, 4 * h + b, :], start=True, stop=True)
            last.then_inc(k.sem("inv_x"), 1)
        for h in range(GH):
            pe.wait_ge(k.sem("inv_x_kept"), GH * lev + h + 1)
            for b in range(PAIRS):
                i = 4 * h + b
                pe.matmul(k.bank(4 + h, P, b * P), m["tt"][:, i, :], m["a"][:, i, :], start=True, stop=True)
                last = pe.matmul(k.bank(h, P, b * P), m["a"][:, i, :], m["tt"][:, i, :], start=True, stop=True)
            last.then_inc(k.sem("inv_z"), 1)


def gdn_invert_scalar(k, s):
    m = gdn_views(k)
    for lev in range(LEVELS):
        for h in range(GH):
            s.eng.wait_ge(k.sem("inv_x"), GH * lev + h + 1)
            s.eng.copy(m["a"][:, 4 * h:4 * h + 4, :], k.bank(h).rearrange("p (b n) -> p b n", b=4)).then_inc(k.sem("inv_x_kept"), 1)
            s.eng.wait_ge(k.sem("inv_x_kept"), GH * lev + h + 1)


def gdn_apply_vector(k, v):
    m = gdn_views(k)
    four = lambda ap: ap.rearrange("p (b n) -> p b n", b=4)
    for h in range(GH):
        blk = slice(4 * h, 4 * h + 4)
        v.eng.tensor_tensor(m["kbe"][:, blk, :], m["k_tok"][:, blk, :], spread(by_head(k, 80)[:, h, :], P), ALU.mult).then_inc(k.sem("apply_kbe"), 1)
        v.eng.wait_ge(k.sem("apply_kbe"), h + 1)
        link(v, v.eng.tensor_tensor(m["k_tok"][:, blk, :], m["k_tok"][:, blk, :], spread(by_head(k, 64)[:, h, :], P), ALU.mult))
        link(v, v.eng.tensor_tensor(m["qkvg"][:, h, :], m["qkvg"][:, h, :], m["egc"][:, h, :], ALU.mult))
    for h in range(GH):
        v.eng.wait_ge(k.sem("apply_made"), h + 1)
        link(v, v.eng.tensor_copy(m["t"][:, 4 * h:4 * h + 4, :], four(k.bank(4 + h))))
    link(v, v.eng.memset(m["state"], 0.0))


def gdn_apply_scalar(k, s):
    m = gdn_views(k)
    for h in range(GH):
        s.eng.wait_ge(k.sem("apply_made"), h + 1)
        link(s, s.eng.copy(m["a"][:, 4 * h:4 * h + 4, :], k.bank(h).rearrange("p (b n) -> p b n", b=4)))


def gdn_apply_tensor(k, pe):
    m = gdn_views(k)
    for h in range(GH):
        pe.wait_ge(k.sem("apply_kbe"), h + 1)
        for b in range(PAIRS):
            i = 4 * h + b
            pe.matmul(k.bank(h, P, b * P), m["tt"][:, i, :], m["v_tok"][:, i, :], start=True, stop=True)
            last = pe.matmul(k.bank(4 + h, P, b * P), m["kbe"][:, i, :], m["tt"][:, i, :], start=True, stop=True)
        last.then_inc(k.sem("apply_made"), 1)


def gdn_scan_tensor(k, pe):
    m = gdn_views(k)
    for n in range(S // CHUNK):
        r, c = slice(CHUNK * (n % 2), CHUNK * (n % 2) + CHUNK), slice(CHUNK * n, CHUNK * (n + 1))
        if n:
            pe.wait_ge(k.sem("scan_state"), n)
        for h in range(GH):
            last = pe.matmul(k.ps[r, 4 * 512 + h * P:4 * 512 + (h + 1) * P], m["t"][:, 4 * h + n // 2, r],
                             m["state"][:, h, :], start=True, stop=True)
        last.then_inc(k.sem("scan_read"), 1)
        for h in range(GH):
            pe.matmul(k.ps[:, h * 512 + n * CHUNK:h * 512 + (n + 1) * CHUNK], m["state"][:, h, :], m["qkvg"][:, h, c],
                      start=True, stop=False)
        pe.wait_ge(k.sem("scan_new"), n + 1)
        for h in range(GH):
            pe.matmul(k.ps[:, h * 512 + n * CHUNK:h * 512 + (n + 1) * CHUNK], m["v_new"][r, h, :],
                      m["attn"][r, 4 * h + n // 2, r], start=False, stop=True)
        for h in range(GH):
            last = pe.matmul(k.bank(5, P, h * P), m["k_tok"][r, 4 * h + n // 2, :], m["v_new"][r, h, :],
                             start=True, stop=True)
        last.then_inc(k.sem("scan_added"), 1)


def gdn_scan_vector(k, v):
    m = gdn_views(k)
    for n in range(S // CHUNK):
        r = slice(CHUNK * (n % 2), CHUNK * (n % 2) + CHUNK)
        u = m["a"].rearrange("p (h b) n -> p h b n", h=GH)[r, :, n // 2, :]
        v.eng.wait_ge(k.sem("scan_read"), n + 1)
        v.eng.tensor_tensor(m["v_new"][r], u, k.bank(4)[r].rearrange("p (h n) -> p h n", h=GH), ALU.subtract).then_inc(k.sem("scan_new"), 1)
        v.eng.wait_ge(k.sem("scan_new"), n + 1)
        v.eng.wait_ge(k.sem("scan_added"), n + 1)
        for h in range(GH):
            ins = v.eng.scalar_tensor_tensor(m["state"][:, h, :], m["state"][:, h, :],
                                             m["egc"][:, h, CHUNK * n + CHUNK - 1:CHUNK * (n + 1)], k.bank(5, P, h * P),
                                             ALU.mult, ALU.add)
            if h < GH - 1:
                link(v, ins)
            else:
                ins.then_inc(k.sem("scan_state"), 1)
                v.eng.wait_ge(k.sem("scan_state"), n + 1)


def gdn_out_scalar(k, s):
    for h in range(GH):
        if h >= 2:
            s.eng.wait_ge(k.sem("gdn_out_sums"), h - 1)
        s.eng.activation(k.sq[:, h % 2, 0:S], k.bank(h), ACT.Square).then_inc(k.sem("gdn_out_squares"), 1)
        s.eng.wait_ge(k.sem("gdn_out_squares"), h + 1)
    for h in range(GH):
        s.eng.wait_ge(k.sem("gdn_out_sums"), h + 1)
        s.eng.activation(k.bank(4 + h), k.bank(4 + h), ACT.Sqrt, bias=k.eps).then_inc(k.sem("gdn_out_roots"), 1)
        s.eng.wait_ge(k.sem("gdn_out_roots"), h + 1)


def gdn_out_tensor(k, pe):
    for h in range(GH):
        pe.wait_ge(k.sem("gdn_out_squares"), h + 1)
        pe.matmul(k.bank(4 + h), k.const("heads128"), k.sq[:, h % 2, 0:S], start=True, stop=True)\
            .then_inc(k.sem("gdn_out_sums"), 1)


def gdn_out_vector(k, v):
    gate = gdn_views(k)["qkvg"]
    for h in range(GH):
        out = k.mix[:, h, 0:S]
        v.eng.wait_ge(k.sem("gdn_out_roots"), h + 1)
        link(v, v.eng.reciprocal(k.rstd[:, 0:S], k.bank(4 + h)))
        link(v, v.eng.scalar_tensor_tensor(out, k.bank(h), k.par("onorm"), k.rstd[:, 0:S], ALU.mult, ALU.mult))
        link(v, v.eng.tensor_tensor(out, out, gate[:, 12 + h, :], ALU.mult))


def mix1_out_vector(k, v):
    m = k.view(k.big, 0, DT, S)
    for j in range(DT):
        v.eng.wait_ge(k.unit_done, FIRST["w_out1"] + j + 1)
        v.eng.tensor_copy(m[:, j, :], k.bank(2 * (j % 4))).then_inc(k.sem("mix1_evac"), 1)
        v.eng.wait_ge(k.sem("mix1_evac"), j + 1)



def hy_project_scalar(k, s):
    x = hy_views(k)["x"]
    for j in range(12):
        s.eng.wait_ge(k.unit_done, FIRST["w_hy"] + j + 1)
        s.eng.activation(x[:, j, :], k.bank(2 * (j % 4)), ACT.Identity, bias=k.par("hy_conv_b", j),
                         scale=k.par("hy_conv_w", 3 * j + 1)).then_inc(k.sem("hy_lin"), 1)
        s.eng.wait_ge(k.sem("hy_lin"), j + 1)


def hy_project_vector(k, v):
    x = hy_views(k)["x"]
    for j in range(12):
        v.eng.wait_ge(k.sem("hy_lin"), j + 1)
        link(v, v.eng.scalar_tensor_tensor(x[:, j, 1:S], k.bank(2 * (j % 4), S - 1), k.par("hy_conv_w", 3 * j),
                                          x[:, j, 1:S], ALU.mult, ALU.add))
        v.eng.scalar_tensor_tensor(x[:, j, 0:S - 1], k.bank(2 * (j % 4), S - 1, 1), k.par("hy_conv_w", 3 * j + 2),
                                   x[:, j, 0:S - 1], ALU.mult, ALU.add).then_inc(k.sem("hy_taps_done"), 1)
        v.eng.wait_ge(k.sem("hy_taps_done"), j + 1)
    for t in range(4):
        link(v, v.eng.tensor_tensor(x[:, 8 + t, :], x[:, 8 + t, :], x[:, 4 + t, :], ALU.mult))


def hy_filter_tensor(k, pe):
    b = hy_views(k)
    pe.wait_ge(k.sem("hy_net_loaded"), 80)
    pe.matmul(k.ps[0:ORDER, 0:S], b["w1"], b["feats"], start=True, stop=True).then_inc(k.sem("hy_layer"), 1)
    for t in range(4):
        if t >= 2:
            pe.wait_ge(k.sem("hy_z_kept"), t - 1)
        for c in range(4):
            last = pe.transpose(k.bank(6 + t % 2, P, c * P), b["x"][:, 8 + c, t * P:(t + 1) * P], k.const("ident"))
        last.then_inc(k.sem("hy_z_turned"), 1)
    for n, w in ((1, "w2"), (2, "w3")):
        pe.wait_ge(k.sem("hy_sin"), n)
        pe.matmul(k.ps[0:ORDER, 0:S], b[w], k.probs[0:ORDER, 0, 0:S], start=True, stop=True).then_inc(k.sem("hy_layer"), 1)


def hy_filter_scalar(k, s):
    b = hy_views(k)
    for t in range(4):
        s.eng.wait_ge(k.sem("hy_z_turned"), t + 1)
        s.eng.copy(b["z"][:, t, :], k.bank(6 + t % 2)).then_inc(k.sem("hy_z_kept"), 1)
        s.eng.wait_ge(k.sem("hy_z_kept"), t + 1)
    for n in range(3):
        s.eng.wait_ge(k.sem("hy_reduced"), n + 1)
        s.eng.activation(k.probs[0:ORDER, 0, 0:S], k.probs[0:ORDER, 1, 0:S], ACT.Sin).then_inc(k.sem("hy_sin"), 1)
        s.eng.wait_ge(k.sem("hy_sin"), n + 1)


def hy_filter_vector(k, v):
    r = slice(0, ORDER)
    arg, turns = k.probs[r, 1, 0:S], k.sq[r, 0, 0:S]
    for n in range(3):
        v.eng.wait_ge(k.sem("hy_layer"), n + 1)
        link(v, v.eng.tensor_scalar(arg, k.ps[r, 0:S], k.par("hy_b", n)[r], k.par("hy_freq")[r], ALU.add, ALU.mult))
        link(v, v.eng.tensor_scalar(turns, arg, 1.0 / (2.0 * np.pi), ROUND, ALU.mult, ALU.add))
        link(v, v.eng.tensor_scalar(turns, turns, ROUND, None, ALU.subtract))
        link(v, v.eng.scalar_tensor_tensor(arg, turns, -TWO_PI_HI, arg, ALU.mult, ALU.add))
        link(v, v.eng.scalar_tensor_tensor(arg, turns, -TWO_PI_LO, arg, ALU.mult, ALU.add))
        v.eng.tensor_scalar(arg, arg, PI_IN, -PI_IN, ALU.min, ALU.max).then_inc(k.sem("hy_reduced"), 1)
        v.eng.wait_ge(k.sem("hy_reduced"), n + 1)


def hy_taps_tensor(k, pe):
    b = hy_views(k)

    def sums(t):
        pe.wait_ge(k.sem("hy_sizes"), t + 1)
        for c in range(4):
            last = pe.matmul(k.bank(4 + c, 1), k.sq[:, t % 2, c * P:(c + 1) * P], k.const("ones")[:, 0:1],
                             start=t == 0, stop=t == 3)
        last.then_inc(k.sem("hy_summed"), 1)

    for t in range(4):
        if t >= 2:
            pe.wait_ge(k.sem("hy_taps_made"), t - 1)
        hid = k.probs[0:ORDER, 0, t * P:(t + 1) * P]
        pe.matmul(k.bank(2 * (t % 2)), hid, b["w4"][:, 0:S], start=True, stop=True)
        pe.matmul(k.bank(2 * (t % 2) + 1), hid, b["w4"][:, S:2 * S], start=True, stop=True).then_inc(k.sem("hy_raw"), 1)
        if t >= 1:
            sums(t - 1)
    sums(3)


def hy_taps_vector(k, v):
    b = hy_views(k)
    v.eng.wait_ge(k.sem("hy_tables"), 48)
    fwd, bwd = k.rstd[:, 0:S], k.probs_t[:, 0:S]
    for t in range(4):
        v.eng.wait_ge(k.sem("hy_raw"), t + 1)
        link(v, v.eng.tensor_tensor(fwd, k.bank(2 * (t % 2)), b["decay"][:, t, :], ALU.mult))
        if t == 0:
            link(v, v.eng.scalar_tensor_tensor(bwd, k.bank(1), k.par("hy_first"), b["decay"][:, 0, :], ALU.mult, ALU.mult))
        else:
            link(v, v.eng.tensor_tensor(bwd, k.bank(2 * (t % 2) + 1), b["decay"][:, t, :], ALU.mult))
        link(v, v.eng.tensor_tensor(b["even"][:, t, :], fwd, bwd, ALU.add))
        link(v, v.eng.tensor_tensor(b["odd"][:, t, :], fwd, bwd, ALU.subtract))
        v.eng.scalar_tensor_tensor(fwd, fwd, -1.0, fwd, ALU.mult, ALU.max).then_inc(k.sem("hy_taps_made"), 1)
        v.eng.wait_ge(k.sem("hy_taps_made"), t + 1)
        link(v, v.eng.scalar_tensor_tensor(bwd, bwd, -1.0, bwd, ALU.mult, ALU.max))
        if t >= 2:
            v.eng.wait_ge(k.sem("hy_summed"), t - 1)
        v.eng.tensor_tensor(k.sq[:, t % 2, 0:S], fwd, bwd, ALU.add).then_inc(k.sem("hy_sizes"), 1)
        v.eng.wait_ge(k.sem("hy_sizes"), t + 1)
    v.eng.wait_ge(k.sem("hy_summed"), 4)
    for c in range(4):
        link(v, v.eng.reciprocal(k.small[:, 124 + c:125 + c], k.bank(4 + c, 1)))


def hy_forward_tensor(k, pe):
    b = hy_views(k)
    for f in range(4):
        if f >= 2:
            pe.wait_ge(k.sem("hy_product"), f - 1)
        col = slice(f * P, (f + 1) * P)
        for n, (table, src) in enumerate((("cos", "z"), ("sin", "z"), ("cos", "even"), ("sin", "odd"))):
            for t in range(4):
                last = pe.matmul(k.bank(4 * (f % 2) + n), b[table][:, t, col], b[src][:, t, :], start=t == 0, stop=t == 3)
        last.then_inc(k.sem("hy_bins"), 1)


def hy_forward_scalar(k, s):
    for f in range(4):
        s.eng.wait_ge(k.sem("hy_bins"), f + 1)
        if f >= 1:
            s.eng.wait_ge(k.sem("hy_product"), f)
        link(s, s.eng.copy(k.sq[:, 0, 0:S], k.bank(4 * (f % 2))))
        s.eng.copy(k.sq[:, 1, 0:S], k.bank(4 * (f % 2) + 1)).then_inc(k.sem("hy_bins_kept"), 1)
        s.eng.wait_ge(k.sem("hy_bins_kept"), f + 1)


def hy_forward_vector(k, v):
    b = hy_views(k)
    zc, zs, tmp = k.sq[:, 0, 0:S], k.sq[:, 1, 0:S], k.rstd[:, 0:S]
    for f in range(4):
        kc, ks = k.bank(4 * (f % 2) + 2), k.bank(4 * (f % 2) + 3)
        yc, ys = b["yc"][:, f, :], b["ys"][:, f, :]
        v.eng.wait_ge(k.sem("hy_bins_kept"), f + 1)
        link(v, v.eng.tensor_tensor(yc, zc, kc, ALU.mult))
        link(v, v.eng.tensor_tensor(tmp, zs, ks, ALU.mult))
        link(v, v.eng.tensor_tensor(yc, yc, tmp, ALU.subtract))
        link(v, v.eng.tensor_tensor(ys, zc, ks, ALU.mult))
        link(v, v.eng.tensor_tensor(tmp, zs, kc, ALU.mult))
        v.eng.tensor_tensor(ys, ys, tmp, ALU.add).then_inc(k.sem("hy_product"), 1)
        v.eng.wait_ge(k.sem("hy_product"), f + 1)


def hy_inverse_tensor(k, pe):
    b = hy_views(k)
    pe.wait_ge(k.sem("hy_tables"), 80)
    for c in range(4):
        for n, (src, table) in enumerate((("yc", "cos"), ("ys", "sin"))):
            for f in range(4):
                last = pe.matmul(k.bank(c), b[src][:, f, c * P:(c + 1) * P], b[table][:, f, :],
                                 start=n == 0 and f == 0, stop=n == 1 and f == 3)
        last.then_inc(k.sem("hy_back"), 1)


def hy_inverse_vector(k, v):
    x = hy_views(k)["x"]
    for c in range(4):
        out = k.mix[:, 4 + c, 0:S]
        v.eng.wait_ge(k.sem("hy_back"), c + 1)
        link(v, v.eng.tensor_scalar(out, k.bank(c), k.small[:, 124 + c:125 + c], None, ALU.mult))
        link(v, v.eng.scalar_tensor_tensor(out, x[:, 8 + c, :], k.par("hy_skip", c), out, ALU.mult, ALU.add))
        link(v, v.eng.tensor_tensor(out, out, x[:, c, :], ALU.mult))



def sync_program(k, sp):
    d = k.dram
    sp.dma_start(k.x[:, :, 0:S], d["x"]).then_inc(k.loaded, 16)
    sp.dma_start(k.x[:, :, S:T], d["ctx"]).then_inc(k.loaded, 16)
    sp.dma_start(k.params[:, :], d["params"]).then_inc(k.loaded, 16)
    sp.dma_start(k.consts[:, :], d["consts"]).then_inc(k.loaded, 16)
    for name, n, width in STREAM:
        u0 = FIRST[name]

        def load(i, u, done):
            if done is not None:
                sp.wait_ge(k.unit_done, done)
            sp.dma_start(k.ring[:, u % SLOTS, 0:width], d[name][i]).then_inc(k.slot_landed[u % SLOTS], 16)

        if n % SLOTS == 0 and u0 >= SLOTS:
            with sp.Fori(0, n // SLOTS) as it:
                for a in range(SLOTS):
                    load(it * SLOTS + a, u0 + a, it * SLOTS + (u0 + a - SLOTS + 1))
        else:
            for i in range(n):
                load(i, u0 + i, u0 + i - SLOTS + 1 if u0 + i >= SLOTS else None)
    k.after(sp, "ffn3_down")
    sp.dma_start(d["out"], k.x[:, :, 0:S]).then_inc(k.sem("out_written"), 16)
    sp.wait_ge(k.sem("out_written"), 16)


def gpsimd_program(k, pool):
    d = k.dram
    hot = k.sem("dil_tables")
    pool.dma_start(k.big[0:BUCKETS, 10240:10240 + LINE], d["buckets"]).then_inc(hot, 16)
    pool.dma_start(k.big[0:BUCKETS, 10880:10888], d["rel_bias"]).then_inc(hot, 16)
    pool.dma_start(k.big[0:1, 10888:10888 + LINE], d["log_counts"]).then_inc(hot, 16)
    pool.wait_ge(k.sem("dil_lines_kept"), 1)
    pool.dma_start(d["lines"].ap(), k.big[0:8, 11528:11528 + LINE]).then_inc(k.sem("dil_lines_out"), 16)
    pool.wait_ge(k.sem("dil_lines_out"), 16)
    pool.dma_start(dil_views(k)[3], bass.AP(d["lines"], 0, [[1, P], [LINE, 8], [1, S]])).then_inc(k.sem("dil_bias"), 16)
    k.after(pool, "ffn1_post")
    bias = k.view(k.big, 12 * T, 8, 14 * GRID_W)
    wide = 2 * GRID_W - 1
    for h in range(8):
        for a in range(2):
            pool.dma_start(bias[GRID_W * a:GRID_W * (a + 1), h, :].rearrange("p (r c) -> p r c", c=GRID_W),
                           bass.AP(d["rpb"], (h * 15 + a) * wide, [[1, GRID_W], [wide, 14], [1, GRID_W]]))\
                .then_inc(k.sem("na_bias"), 16)
    k.after(pool, "hy_project")
    b = hy_views(k)
    for name, src in (("w1", "hy_w1"), ("w2", "hy_w2"), ("w3", "hy_w3"), ("w4", "hy_w4"), ("feats", "feats")):
        pool.dma_start(b[name], d[src]).then_inc(k.sem("hy_net_loaded"), 16)
    for name, src in (("decay", "decay"), ("cos", "dft_cos"), ("sin", "dft_sin")):
        pool.dma_start(b[name], d[src]).then_inc(k.sem("hy_tables"), 16)
    k.after(pool, "hy_forward")
    for name, src in (("cos", "idft_cos"), ("sin", "idft_sin")):
        pool.dma_start(b[name], d[src]).then_inc(k.sem("hy_tables"), 16)


def tensor_program(k, pe):
    start_tensor(k, pe)
    k.after(pe, "start")
    plain_norm(k, pe, "tensor", "norm1", "g_mix_pre", S)
    k.after(pe, "norm1")
    dil_project_tensor(k, pe)
    k.after(pe, "dil_project")
    pe.wait_ge(k.sem("dil_bias"), 16)
    Attention(k, 0, 0, dil_items(k)).tensor(pe)
    k.after(pe, "dil_attend")
    gdn_project_tensor(k, pe)
    k.after(pe, "gdn_project")
    gdn_gates_tensor(k, pe)
    k.after(pe, "gdn_gates")
    gdn_norm(k).tensor(pe)
    k.after(pe, "gdn_norm_qk")
    gdn_masks_tensor(k, pe)
    k.after(pe, "gdn_masks")
    gdn_products_tensor(k, pe)
    k.after(pe, "gdn_products")
    gdn_invert_tensor(k, pe)
    k.after(pe, "gdn_invert")
    gdn_apply_tensor(k, pe)
    k.after(pe, "gdn_apply")
    gdn_scan_tensor(k, pe)
    k.after(pe, "gdn_scan")
    gdn_out_tensor(k, pe)
    k.after(pe, "gdn_out")
    dense_tensor(k, pe, "w_out1", DT, lambda b: k.mix[:, b, :], (S,), evac=k.sem("mix1_evac"))
    k.after(pe, "mix1_out")
    norm_tensor(k, pe, "mix1_post", S)
    k.after(pe, "mix1_post")
    plain_norm(k, pe, "tensor", "norm2", "g_ffn_pre", S)
    hidden = k.view(k.big, 0, FT, T)
    act = lambda b: k.h[:, b, :]
    hid = lambda b: hidden[:, b, :]
    mix = lambda b: k.mix[:, b, :]
    k.after(pe, "norm2")
    dense_tensor(k, pe, "w_ffn1_up", 2 * FT, act, (S,), evac=k.sem("w_ffn1_up_hidden"), per_evac=2, loop=True)
    k.after(pe, "ffn1_up")
    dense_tensor(k, pe, "w_ffn1_down", DT, hid, (S,), upt=2, blocks=(11, 11), nbuf=2, evac=k.sem("ffn1_down_evac"), loop=True)
    k.after(pe, "ffn1_down")
    norm_tensor(k, pe, "ffn1_post", S)
    k.after(pe, "ffn1_post")
    ada_tensor(k, pe, "w_ada0", 0)
    k.after(pe, "ada0")
    norm_tensor(k, pe, "mod_a0", T)
    k.after(pe, "mod_a0")
    dense_tensor(k, pe, "w_na_qk", 8, act, (S, CTX), evac=k.sem("na_project_evac"))
    pe.wait_ge(k.sem("na_project_evac"), 8)
    values_tensor(k, pe, "w_na_v", 6, HALF)
    k.after(pe, "na_project")
    na_norm(k).tensor(pe)
    k.after(pe, "na_norm")
    pe.wait_ge(k.sem("na_bias"), 256)
    Attention(k, 32, 32, na_items(k)).tensor(pe)
    k.after(pe, "na_attend")
    dense_tensor(k, pe, "w_diff_qk", 8, act, (S, CTX), evac=k.sem("diff_project_evac"))
    pe.wait_ge(k.sem("diff_project_evac"), 8)
    values_tensor(k, pe, "w_diff_v", 6, HALF)
    k.after(pe, "diff_project")
    diff_norm(k).tensor(pe)
    k.after(pe, "diff_norm")
    Attention(k, 80, 80, diff_items(k)).tensor(pe)
    k.after(pe, "diff_attend")
    subln(k).tensor(pe)
    k.after(pe, "diff_subln")
    dense_tensor(k, pe, "w_out_e", DT, mix, (S, CTX), evac=k.sem("mix_e_evac"))
    k.after(pe, "mix_e_out")
    norm_tensor(k, pe, "mod_f0", T)
    k.after(pe, "mod_f0")
    dense_tensor(k, pe, "w_ffn2_up", 2 * FT, act, (S, CTX), evac=k.sem("w_ffn2_up_hidden"), per_evac=2, loop=True)
    k.after(pe, "ffn2_up")
    dense_tensor(k, pe, "w_ffn2_down", DT, hid, (S, CTX), upt=2, blocks=(11, 11), nbuf=2, evac=k.sem("ffn2_down_evac"),
                 loop=True)
    k.after(pe, "ffn2_down")
    ada_tensor(k, pe, "w_ada1", 1)
    k.after(pe, "ada1")
    norm_tensor(k, pe, "mod_a1", T)
    k.after(pe, "mod_a1")
    dense_tensor(k, pe, "w_gqa_qk", 5, act, (S, CTX), evac=k.sem("gqa_project_evac"))
    pe.wait_ge(k.sem("gqa_project_evac"), 5)
    values_tensor(k, pe, "w_gqa_v", 6, P)
    k.after(pe, "gqa_project")
    gqa_norm(k).tensor(pe)
    k.after(pe, "gqa_norm")
    Attention(k, 128, 104, gqa_items(k)).tensor(pe)
    k.after(pe, "gqa_attend")
    dense_tensor(k, pe, "w_hy", 12, act, (S,), evac=k.sem("hy_taps_done"))
    k.after(pe, "hy_project")
    hy_filter_tensor(k, pe)
    k.after(pe, "hy_filter")
    hy_taps_tensor(k, pe)
    k.after(pe, "hy_taps")
    hy_forward_tensor(k, pe)
    k.after(pe, "hy_forward")
    hy_inverse_tensor(k, pe)
    k.after(pe, "hy_inverse")
    dense_tensor(k, pe, "w_out_o", DT, mix, (S,), evac=k.sem("mix_o_evac"))
    k.after(pe, "mix_o_out")
    norm_tensor(k, pe, "mod_f1", S)
    k.after(pe, "mod_f1")
    dense_tensor(k, pe, "w_ffn3_up", 2 * FT, act, (S,), evac=k.sem("w_ffn3_up_hidden"), per_evac=2, loop=True)
    k.after(pe, "ffn3_up")
    dense_tensor(k, pe, "w_ffn3_down", DT, hid, (S,), upt=2, blocks=(11, 11), nbuf=2, evac=k.sem("ffn3_down_evac"), loop=True)


def scalar_program(k, act):
    s = Serial(act, k.sem("scalar_own"))
    end = lambda stage: stage_end(k, act, k.scalar_stages, stage)
    m1 = k.view(k.big, 0, DT, S)
    start_scalar(k, s)
    end("start")
    plain_norm(k, s, "scalar", "norm1", "g_mix_pre", S)
    end("norm1")
    dil_project_scalar(k, s)
    end("dil_project")
    Attention(k, 0, 0, dil_items(k)).scalar(s)
    end("dil_attend")
    gdn_project_scalar(k, s)
    end("gdn_project")
    gdn_gates_scalar(k, s)
    end("gdn_gates")
    gdn_norm(k).scalar(s)
    end("gdn_norm_qk")
    gdn_masks_scalar(k, s)
    end("gdn_masks")
    end("gdn_products")
    gdn_invert_scalar(k, s)
    end("gdn_invert")
    gdn_apply_scalar(k, s)
    end("gdn_apply")
    end("gdn_scan")
    gdn_out_scalar(k, s)
    end("gdn_out")
    end("mix1_out")
    norm_scalar(k, s, "mix1_post", m1, S)
    end("mix1_post")
    plain_norm(k, s, "scalar", "norm2", "g_ffn_pre", S)
    end("norm2")
    ffn_up_scalar(k, s, "w_ffn1_up", None, S)
    end("ffn1_up")
    end("ffn1_down")
    norm_scalar(k, s, "ffn1_post", k.mix, S)
    end("ffn1_post")
    end("ada0")
    modulate_scalar(k, s, "mod_a0", 0, T)
    end("mod_a0")
    q, key, _ = attn_views(k)
    copy_out_scalar(k, s, "w_na_qk", 8, lambda j: (q if j < 4 else key)[:, j % 4, :], lambda j: T, k.sem("na_project_evac"))
    end("na_project")
    na_norm(k).scalar(s)
    end("na_norm")
    Attention(k, 32, 32, na_items(k)).scalar(s)
    end("na_attend")
    copy_out_scalar(k, s, "w_diff_qk", 8, lambda j: (q if j < 4 else key)[:, j % 4, :], lambda j: T,
                    k.sem("diff_project_evac"))
    end("diff_project")
    diff_norm(k).scalar(s)
    end("diff_norm")
    Attention(k, 80, 80, diff_items(k)).scalar(s)
    end("diff_attend")
    subln(k).scalar(s)
    end("diff_subln")
    end("mix_e_out")
    modulate_scalar(k, s, "mod_f0", 24, T)
    end("mod_f0")
    ffn_up_scalar(k, s, "w_ffn2_up", ffn_conv(0), T)
    end("ffn2_up")
    end("ffn2_down")
    end("ada1")
    modulate_scalar(k, s, "mod_a1", 0, T)
    end("mod_a1")
    gq, gk, _ = gqa_views(k)
    copy_out_scalar(k, s, "w_gqa_qk", 5, lambda j: gq[:, j, :] if j < 4 else gk[:, 0, :], lambda j: T,
                    k.sem("gqa_project_evac"))
    end("gqa_project")
    gqa_norm(k).scalar(s)
    end("gqa_norm")
    Attention(k, 128, 104, gqa_items(k)).scalar(s)
    end("gqa_attend")
    hy_project_scalar(k, s)
    end("hy_project")
    hy_filter_scalar(k, s)
    end("hy_filter")
    end("hy_taps")
    hy_forward_scalar(k, s)
    end("hy_forward")
    end("hy_inverse")
    end("mix_o_out")
    modulate_scalar(k, s, "mod_f1", 24, S)
    end("mod_f1")
    ffn_up_scalar(k, s, "w_ffn3_up", ffn_conv(1), S)
    end("ffn3_up")
    end("ffn3_down")


def vector_program(k, dve):
    v = Serial(dve, k.sem("vector_own"))
    end = lambda stage: stage_end(k, dve, k.vector_stages, stage)
    m1 = k.view(k.big, 0, DT, S)
    hidden = k.view(k.big, 0, FT, T)
    start_vector(k, v)
    end("start")
    plain_norm(k, v, "vector", "norm1", "g_mix_pre", S)
    end("norm1")
    dil_project_vector(k, v)
    end("dil_project")
    Attention(k, 0, 0, dil_items(k)).vector(v)
    end("dil_attend")
    gdn_project_vector(k, v)
    end("gdn_project")
    gdn_gates_vector(k, v)
    end("gdn_gates")
    gdn_norm(k).vector(v)
    end("gdn_norm_qk")
    gdn_masks_vector(k, v)
    end("gdn_masks")
    gdn_products_vector(k, v)
    end("gdn_products")
    gdn_invert_vector(k, v)
    end("gdn_invert")
    gdn_apply_vector(k, v)
    end("gdn_apply")
    gdn_scan_vector(k, v)
    end("gdn_scan")
    gdn_out_vector(k, v)
    end("gdn_out")
    mix1_out_vector(k, v)
    end("mix1_out")
    post_norm_vector(k, v, "mix1_post", m1, "g_mix_post")
    end("mix1_post")
    plain_norm(k, v, "vector", "norm2", "g_ffn_pre", S)
    end("norm2")
    ffn_up_vector(k, v, "w_ffn1_up", None, S, hidden)
    end("ffn1_up")
    copy_down_vector(k, v, "w_ffn1_down", k.mix, k.sem("ffn1_down_evac"))
    end("ffn1_down")
    post_norm_vector(k, v, "ffn1_post", k.mix, "g_ffn_post")
    end("ffn1_post")
    ada_vector(k, v, "w_ada0", 0)
    end("ada0")
    modulate_vector(k, v, "mod_a0", 8, T)
    end("mod_a0")
    values_vector(k, v, "w_na_v", 4, attn_views(k)[2], HALF, 6)
    end("na_project")
    na_norm(k).vector(v)
    end("na_norm")
    Attention(k, 32, 32, na_items(k)).vector(v)
    end("na_attend")
    values_vector(k, v, "w_diff_v", 4, attn_views(k)[2], HALF, 6)
    end("diff_project")
    diff_norm(k).vector(v)
    end("diff_norm")
    Attention(k, 80, 80, diff_items(k)).vector(v)
    end("diff_attend")
    subln(k).vector(v)
    end("diff_subln")
    residual_vector(k, v, "w_out_e", 16, T, 1, 4, k.sem("mix_e_evac"), False)
    end("mix_e_out")
    modulate_vector(k, v, "mod_f0", 32, T)
    end("mod_f0")
    ffn_up_vector(k, v, "w_ffn2_up", ffn_conv(0), T, hidden)
    end("ffn2_up")
    residual_vector(k, v, "w_ffn2_down", 40, T, 2, 2, k.sem("ffn2_down_evac"), True)
    end("ffn2_down")
    ada_vector(k, v, "w_ada1", 1)
    end("ada1")
    modulate_vector(k, v, "mod_a1", 8, T)
    end("mod_a1")
    values_vector(k, v, "w_gqa_v", 1, gqa_views(k)[2], P, 6)
    end("gqa_project")
    gqa_norm(k).vector(v)
    end("gqa_norm")
    Attention(k, 128, 104, gqa_items(k)).vector(v)
    end("gqa_attend")
    hy_project_vector(k, v)
    end("hy_project")
    hy_filter_vector(k, v)
    end("hy_filter")
    hy_taps_vector(k, v)
    end("hy_taps")
    hy_forward_vector(k, v)
    end("hy_forward")
    hy_inverse_vector(k, v)
    end("hy_inverse")
    residual_vector(k, v, "w_out_o", 16, S, 1, 4, k.sem("mix_o_evac"), False)
    end("mix_o_out")
    modulate_vector(k, v, "mod_f1", 32, S)
    end("mod_f1")
    ffn_up_vector(k, v, "w_ffn3_up", ffn_conv(1), S, hidden)
    end("ffn3_up")
    residual_vector(k, v, "w_ffn3_down", 40, S, 2, 2, k.sem("ffn3_down_evac"), True)
    end("ffn3_down")


def build(nc, dram):
    with ExitStack() as ctx:
        k = Core(nc, ctx, dram)
        block = ctx.enter_context(nc.Block())

        @block.sync
        def _(sp):
            sync_program(k, sp)

        @block.gpsimd
        def _(pool):
            gpsimd_program(k, pool)

        @block.tensor
        def _(pe):
            tensor_program(k, pe)

        @block.scalar
        def _(act):
            scalar_program(k, act)

        @block.vector
        def _(dve):
            vector_program(k, dve)



def constants():
    f = np.float32
    out = {name: np.zeros((P, n), f) for name, n in CONSTS}
    i, j = np.arange(P)[:, None], np.arange(P)[None, :]
    same = i // CHUNK == j // CHUNK
    out["ident"][:] = i == j
    out["ones"][:] = 1
    out["ones_d"][:] = 1 / D
    out["heads64"][:] = (i // HD == j // HD) / HD
    out["heads128"][:] = 1 / P
    out["flip"][:] = i == P - 1 - j
    out["rope_swap"][:] = np.where((i == j + 1) & (j % 2 == 0), -1, 0) + np.where((i == j - 1) & (j % 2 == 1), 1, 0)
    out["later"][:] = same & (i > j)
    out["upto"][:] = same & (i <= j)
    for lev in range(LEVELS):
        s = 1 << lev
        out["levels"][:, lev * P:(lev + 1) * P] = (i // (2 * s) == j // (2 * s)) & (i // s + 1 == j // s)
    cq, ck = np.arange(P)[:, None] % GRID_W, np.arange(S)[None, :] % GRID_W
    first = np.clip(cq - WIN_C // 2, 0, GRID_W - WIN_C)
    out["na_mask"][:] = np.where((ck >= first) & (ck < first + WIN_C), 0, MASKED)
    t = np.arange(S)
    pairs = HD // 4
    inv = f(10000.0) ** (-np.arange(pairs, dtype=f) / f(pairs))
    ang = np.concatenate([(t // GRID_W).astype(f)[:, None] * inv, (t % GRID_W).astype(f)[:, None] * inv], axis=1)
    which = (np.arange(P) % HD) // 2
    out["cos"][:] = np.cos(ang)[:, which].T
    out["sin"][:] = np.sin(ang)[:, which].T
    return np.concatenate([out[name] for name, _ in CONSTS], axis=1)


def distance_tables():
    f = np.float32
    d = S - 1 - np.arange(LINE)
    far = np.maximum(d, 1).astype(f)
    log_b = 16 + (np.log(far / f(16)) / f(np.log(2048 / 16)) * f(16)).astype(np.int32)
    bucket = np.where(d < 16, np.maximum(d, 0), np.minimum(log_b, BUCKETS - 1))
    hot = (np.arange(BUCKETS)[:, None] == bucket[None, :]).astype(f)
    count = (d <= 128).astype(int) + (d % 4 == 0) + (d % 16 == 0)
    logs = np.where((d >= 0) & (count > 0), np.log(np.maximum(count, 1)), MASKED)
    return hot, logs.astype(f)[None, :]


def hyena_tables():
    f = np.float32
    t = np.linspace(0.0, 1.0, S, dtype=f)[:, None]
    bands = (EMB - 1) // 2
    w = f(2.0 * np.pi) * np.arange(S, dtype=f)[:, None] / f(S)
    freq = np.linspace(1e-4, bands - 1, bands, dtype=f)[None, :]
    feats = np.concatenate([t, np.cos(freq * w), -np.sin(freq * w)], axis=1).T
    deltas = np.linspace(np.log(1e-2) / 1.5, np.log(1e-2) / 0.3, HALF, dtype=f)
    decay = np.exp(-t * np.abs(deltas))
    angle = np.pi / (2 * S) * ((2 * np.arange(S)[None, :] + 1) * np.arange(S)[:, None] % (4 * S))
    tiles = lambda a: np.ascontiguousarray(a.reshape(4, P, -1).transpose(1, 0, 2).astype(f))
    return {"feats": np.ascontiguousarray(feats.astype(f)), "decay": tiles(decay),
            "dft_cos": tiles(np.cos(angle)), "dft_sin": tiles(np.sin(angle)),
            "idft_cos": tiles(np.cos(angle).T / S), "idft_sin": tiles(np.sin(angle).T / S)}



def by_output(w, blocks=DT):
    kt, nt = w.shape[0] // P, w.shape[1] // P
    a = w.reshape(kt // blocks, blocks, P, nt, P).transpose(3, 0, 2, 1, 4)
    return np.ascontiguousarray(a.reshape(nt * (kt // blocks), P, blocks * P))


def by_input(w):
    n = w.shape[1]
    per = 1024 // n
    return np.ascontiguousarray(w.reshape(DT // per, per, P, n).transpose(0, 2, 1, 3).reshape(DT // per, P, per * n))


def alternate(a, b):
    a, b = by_output(a), by_output(b)
    return np.stack([a, b], axis=1).reshape(2 * len(a), P, D)


def cols(vec):
    return np.asarray(vec).reshape(-1, P).T


def padded(a):
    a = np.asarray(a, np.float32)
    out = np.zeros((P, a.shape[1]), np.float32)
    out[:a.shape[0]] = a
    return out


def layout(i):
    g = {name: np.asarray(a) for name, a in i.items()}
    W = g["w_in"][0]
    o = {}
    gw = GH * P
    q0 = 4 * gw + 2 * GH
    o["w_dil_qk"] = by_output(W[:, q0:q0 + 2 * HALF])
    o["w_dil_v"] = by_input(W[:, q0 + 2 * HALF:q0 + 3 * HALF])
    o["w_gdn"] = by_output(W[:, 0:4 * gw])
    o["w_gdn_gates"] = np.ascontiguousarray(W[:, 4 * gw:q0].reshape(DT, P, 2 * GH).transpose(1, 0, 2).reshape(1, P, 8 * DT))
    o["w_out1"] = by_output(g["w_out"][0])
    o["w_ffn1_up"] = alternate(g["w_gate"][0], g["w_up"][0])
    o["w_ffn1_down"] = by_output(g["w_down"][0], 11)
    for l in range(2):
        o[f"w_ada{l}"] = by_output(g["w_ada_2"][l])
        up = g["w_up_2"][l]
        o[f"w_ffn{l + 2}_up"] = alternate(up[:, 0:F], up[:, F:])
        o[f"w_ffn{l + 2}_down"] = by_output(g["w_down_2"][l], 11)
    E = g["w_in_e_2"][0]
    o["w_na_qk"], o["w_na_v"] = by_output(E[:, 0:1024]), by_input(E[:, 1024:1536])
    o["w_diff_qk"], o["w_diff_v"] = by_output(E[:, 1536:2560]), by_input(E[:, 2560:3072])
    o["w_out_e"] = by_output(g["w_out_e_2"][0])
    O = g["w_in_o_2"][0]
    order = [t + 4 * e for t in range(4) for e in range(2)]
    q = O[:, 0:HALF].reshape(D, 8, HD)[:, order].reshape(D, HALF)
    o["w_gqa_qk"] = by_output(np.concatenate([q, O[:, HALF:HALF + P]], axis=1))
    o["w_gqa_v"] = by_input(O[:, HALF + P:HALF + 2 * P])
    o["w_hy"] = by_output(O[:, HALF + 2 * P:])
    wo = g["w_out_o_2"][0]
    o["w_out_o"] = by_output(np.concatenate([wo[0:HALF].reshape(8, HD, D)[order].reshape(HALF, D), wo[HALF:]]))

    o["x"] = np.ascontiguousarray(g["x"][0].T.reshape(DT, P, S).transpose(1, 0, 2))
    o["ctx"] = np.ascontiguousarray(g["ctx_2"][0].T.reshape(DT, P, CTX).transpose(1, 0, 2))
    taps = lambda w: np.stack([cols(r) for r in w], axis=2).reshape(P, -1)
    twice = lambda v: np.concatenate([v, v]).reshape(P, 1)
    both = lambda v: np.repeat(cols(v), 2, axis=1)
    p = {
        "g_mix_pre": cols(g["g_mix_pre"]), "g_mix_post": cols(g["g_mix_post"]),
        "g_ffn_pre": cols(g["g_ffn_pre"]), "g_ffn_post": cols(g["g_ffn_post"]),
        "conv_w": taps(g["conv_w"][0]), "a_log": padded(g["a_log"].T), "dt_bias": padded(g["dt_bias"].T),
        "onorm": cols(g["onorm_g"]), "na_q": twice(g["na_q_gain_2"][0]), "na_k": twice(g["na_k_gain_2"][0]),
        "da_q": twice(g["da_q_gain_2"][0]), "da_k": twice(g["da_k_gain_2"][0]), "subln": cols(g["da_subln_gain_2"]),
        "gqa_q": twice(g["gqa_q_gain_2"][0]), "gqa_k": twice(g["gqa_k_gain_2"][0]),
        "lambdas": padded(np.stack([g[f"da_lambda_{n}_2"][0] for n in ("q1", "q2", "k1", "k2")], axis=1)),
        "cond": np.stack([cols(g["c_2"]), cols(g["c_ctx_2"])], axis=2).reshape(P, 16),
        "b_ada0": both(g["b_ada_2"][0]), "b_ada1": both(g["b_ada_2"][1]),
        "ffn_w0": taps(g["ffn_conv_w_2"][0]), "ffn_w1": taps(g["ffn_conv_w_2"][1]),
        "ffn_b0": cols(g["ffn_conv_b_2"][0]), "ffn_b1": cols(g["ffn_conv_b_2"][1]),
        "hy_conv_w": taps(g["hy_conv_w_2"][0]), "hy_conv_b": cols(g["hy_conv_b_2"]),
        "hy_b": padded(np.stack([g[f"hy_b{n}_2"][0] for n in (1, 2, 3)], axis=1)), "hy_freq": padded(g["hy_freq_2"].T),
        "hy_skip": cols(g["hy_skip_2"]), "hy_first": (np.arange(P) > 0).astype(np.float32)[:, None],
        "eps": np.full((P, 1), EPS, np.float32), "one": np.ones((P, 1), np.float32),
    }
    o["params"] = np.concatenate([p[name].reshape(P, n) for name, n in PARAMS], axis=1)
    o["rel_bias"] = g["rel_bias"]
    o["rpb"] = np.pad(g["na_rpb_2"][0], ((0, 0), (0, 0), (GRID_W - WIN_C, GRID_W - WIN_C)))
    for n in (1, 2, 3, 4):
        o[f"hy_w{n}"] = g[f"hy_w{n}_2"][0]
    o["consts"] = constants()
    o["buckets"], o["log_counts"] = distance_tables()
    o.update(hyena_tables())
    return {name: np.ascontiguousarray(a) for name, a in o.items()}


def kernel(**inputs):
    import concourse.bacc as bacc
    from concourse.bass_utils import run_bass_kernel_spmd

    nc = bacc.Bacc("TRN2", target_bir_lowering=False, num_devices=1)
    arrays, dram = {}, {}
    for name, a in layout(inputs).items():
        arrays[f"in_{name}"] = a
        handle = nc.dram_tensor(f"in_{name}", a.shape, F32, kind="ExternalInput")
        dram[name] = handle if name == "rpb" else handle.ap()
    dram["lines"] = nc.dram_tensor("bias_lines", (8, LINE), F32)
    dram["out"] = nc.dram_tensor("out_0", (P, DT, S), F32, kind="ExternalOutput").ap()
    build(nc, dram)
    r = run_bass_kernel_spmd(nc, [arrays], core_ids=[0])
    got = r.results[0]["out_0"]
    return np.ascontiguousarray(np.asarray(got).transpose(2, 1, 0).reshape(1, S, D))
```

```python
import concourse.bass as bass
import numpy as np
from concourse import mybir
from concourse.alu_op_type import AluOpType as ALU
from contextlib import ExitStack

F32 = mybir.dt.float32
R32 = mybir.dt.float32r
ACT = mybir.ActivationFunctionType
AX = mybir.AxisListType

P = 128
D = 1024
DT = D // P
S = 512
CTX = 256
T = S + CTX
F = 2816
FT = F // P
HALF = D // 2
HT = HALF // P
HD = 64
CHUNK = 64
PAIRS = S // P
GH = 4
GRID_W = 64
WIN_R, WIN_C = 8, 16
EMB, ORDER = 33, 64
BUCKETS = 32
MASKED = -1.0e30
EPS = 1e-6
ROUND = 1.5 * 2.0 ** 23
TWO_PI_HI = 6.28125
TWO_PI_LO = 2.0 * np.pi - TWO_PI_HI
PI_IN = 3.1415925
LAM_INIT = 0.2

SLOTS = 4
SPLITS = 2
CHUNKS = ((0, 8), (8, 8), (16, 6))
FFN_UNITS = 2 * FT + DT * len(CHUNKS)
LINE = 640

PARAMS = [
    ("g_mix_pre", 8), ("g_mix_post", 8), ("g_ffn_pre", 8), ("g_ffn_post", 8), ("conv_w", 48),
    ("a_log", 1), ("dt_bias", 1), ("onorm", 1),
    ("na_q", 1), ("na_k", 1), ("da_q", 1), ("da_k", 1), ("subln", 1), ("gqa_q", 1), ("gqa_k", 1),
    ("lambdas", 4), ("cond", 16), ("b_ada0", 96), ("b_ada1", 96),
    ("ffn_w0", 66), ("ffn_w1", 66), ("ffn_b0", 22), ("ffn_b1", 22),
    ("hy_conv_w", 36), ("hy_conv_b", 12), ("hy_b", 3), ("hy_freq", 1), ("hy_skip", 4), ("hy_first", 1), ("eps", 1), ("one", 1),
]
COL = {}
_at = 0
for _name, _n in PARAMS:
    COL[_name] = (_at, _n)
    _at += _n
NPARAM = _at

CONSTS = [("ident", P), ("ones", P), ("ones_d", P), ("heads64", P), ("heads128", P), ("flip", P), ("rope_swap", P),
          ("later", P), ("upto", P), ("levels", 6 * P), ("na_mask", S), ("cos", S), ("sin", S)]
CCOL = {}
_at = 0
for _name, _n in CONSTS:
    CCOL[_name] = (_at, _n)
    _at += _n
NCONST = _at

STAGES = [
    "start", "norm1", "dil_project", "dil_attend", "gdn_project", "gdn_gates", "gdn_norm_qk", "gdn_masks",
    "gdn_products", "gdn_invert", "gdn_apply", "gdn_scan", "gdn_out", "mix1_split", "mix1_out", "mix1_post", "norm2",
    "ffn1", "ffn1_post",
    "mod_a0", "diff_project", "diff_norm", "diff_attend", "diff_subln", "na_project", "na_norm", "na_attend",
    "mix_e_split", "mix_e_out", "mod_f0", "ffn2",
    "mod_a1", "gqa_project", "gqa_norm", "gqa_attend", "hy_project", "hy_filter", "hy_taps", "hy_forward",
    "hy_inverse", "mix_o_split", "mix_o_out", "mod_f1", "ffn3", "end",
]

STREAM = [
    ("w_dil_qk", 8, D, True), ("w_dil_v", 4, D, True), ("w_ada0_a", 32, D, False), ("w_gdn", 16, D, True),
    ("w_gdn_gates", 1, D, True), ("w_ada0_b", 16, D, False), ("w_out1", 8, D, True), ("w_ffn1", FFN_UNITS, D, True),
    ("w_diff_qk", 8, D, True), ("w_diff_v", 4, D, True), ("w_na_qk", 8, D, True), ("w_na_v", 4, D, True),
    ("w_ada1", 48, D, False), ("w_out_e", 8, D, True), ("w_ffn2", FFN_UNITS, D, True),
    ("w_gqa_qk", 5, D, True), ("w_gqa_v", 1, D, True), ("w_hy", 12, D, True), ("w_out_o", 8, D, True),
    ("w_ffn3", FFN_UNITS, D, True),
]
FIRST = {}
VFIRST = {}
UNIT_OF = []
_at = 0
for _name, _n, _w, _split in STREAM:
    FIRST[_name], VFIRST[_name] = _at, len(UNIT_OF)
    if _split:
        UNIT_OF += range(_at, _at + _n)
    _at += _n


class Serial:

    def __init__(self, eng, own):
        self.eng, self.own, self.n, self.at, self.per = eng, own, 0, None, 0
        self.counts = {}

    def enter(self, at, per):
        self.at, self.per, self.begin = at, per, self.n

    def leave(self, passes):
        assert self.n == self.begin + self.per
        self.n = self.begin + passes * self.per
        self.at = None


def link(e, ins):
    e.n += 1
    ins.then_inc(e.own, 1)
    e.eng.wait_ge(e.own, e.n if e.at is None else e.at * e.per + (e.n - e.per))


class Core:

    def __init__(self, nc, ctx, dram):
        self.nc, self.ctx, self.dram = nc, ctx, dram
        self.at = nc.sbuf_base + (-nc.sbuf_base) % 32
        self.x = self.place("x_res", DT * T).rearrange("p (t n) -> p t n", t=DT)
        h_at = self.at
        self.h_hi = self.place("act_hi", DT * T, R32).rearrange("p (t n) -> p t n", t=DT)
        self.h_flat = self.over(h_at, "act_place", DT * T)
        mix_at = self.at
        self.mix_flat = self.place("mix", DT * T)
        self.mix = self.mix_flat.rearrange("p (t n) -> p t n", t=DT)
        self.mix_lo = self.over(mix_at, "mix_lo", DT * T, R32).rearrange("p (t n) -> p t n", t=DT)
        big_at = self.at
        self.big = self.place("big", 16384)
        self.lo1 = self.over(big_at + 4 * 12288, "act_lo_first", DT * S, R32).rearrange("p (t n) -> p t n", t=DT)
        self.lo2 = self.over(big_at + 4 * 9216, "act_lo_mixer", DT * T, R32).rearrange("p (t n) -> p t n", t=DT)
        self.lo3 = self.over(mix_at, "act_lo_ffn", DT * T, R32).rearrange("p (t n) -> p t n", t=DT)
        self.hid_hi = self.over(big_at, "hidden_hi", 8 * T, R32).rearrange("p (t n) -> p t n", t=8)
        self.hid_lo = self.over(big_at + 4 * 8 * T, "hidden_lo", 8 * T, R32).rearrange("p (t n) -> p t n", t=8)
        self.ring = self.place("ring", SLOTS * D).rearrange("p (s n) -> p s n", s=SLOTS)
        self.w_hi = self.place("w_hi", SPLITS * D, R32).rearrange("p (s n) -> p s n", s=SPLITS)
        self.w_lo = self.place("w_lo", SPLITS * D, R32).rearrange("p (s n) -> p s n", s=SPLITS)
        self.sq = self.place("sq", 2 * T).rearrange("p (s n) -> p s n", s=2)
        self.rstd = self.place("rstd", T)
        self.probs = self.place("probs", 2 * T).rearrange("p (s n) -> p s n", s=2)
        self.probs_t = self.place("probs_t", T)
        self.params = self.place("params", NPARAM)
        self.eps = self.par("eps")
        self.consts = self.place("consts", NCONST)
        self.mod_flat = self.place("mod", 2 * 96)
        self.mod = self.mod_flat.rearrange("p (l n s) -> p l n s", l=2, s=2)
        self.small = self.place("small", 128)
        self.ps = ctx.enter_context(nc.psum_tensor("ps", [P, 8 * 512], F32))
        self.sems = {}
        self.sem = self._sem
        self.slot_landed = [self.sem(f"slot_landed_{i}") for i in range(SLOTS)]
        self.unit_done = self.sem("unit_done")
        self.hi_done = self.sem("hi_done")
        self.lo_done = self.sem("lo_done")
        self.v_next = 0
        self.loaded = self.sem("loaded")
        self.vector_stages = self.sem("vector_stages")
        self.scalar_stages = self.sem("scalar_stages")

    def over(self, at, name, cols, dtype=F32):
        return self.nc.alloc_sbuf_tensor_at(name, [P, cols], dtype, offset=at)[:, :]

    def place(self, name, cols, dtype=F32):
        ap = self.over(self.at, name, cols, dtype)
        self.at += 4 * cols + (-4 * cols) % 32
        return ap

    def _sem(self, name):
        if name not in self.sems:
            self.sems[name] = self.ctx.enter_context(self.nc.semaphore(name))
        return self.sems[name]

    def bank(self, b, n=512, off=0):
        return self.ps[:, b * 512 + off:b * 512 + off + n]

    def view(self, buf, off, *shape):
        n = int(np.prod(shape))
        ap = buf[:, off:off + n]
        if len(shape) == 2:
            ap = ap.rearrange("p (a b) -> p a b", a=shape[0])
        if len(shape) == 3:
            ap = ap.rearrange("p (a b c) -> p a b c", a=shape[0], b=shape[1])
        return ap

    def par(self, name, i=0, n=1):
        return self.params[:, COL[name][0] + i:COL[name][0] + i + n]

    def const(self, name, i=0, n=None):
        return self.consts[:, CCOL[name][0] + i:CCOL[name][0] + i + (n or P)]

    def after(self, eng, stage):
        eng.wait_ge(self.vector_stages, STAGES.index(stage) + 1)
        eng.wait_ge(self.scalar_stages, STAGES.index(stage) + 1)

    def slot_ready(self, eng, u, loop=None):
        more = 0 if loop is None else loop[0] * (16 * loop[1] // SLOTS)
        eng.wait_ge(self.slot_landed[u % SLOTS], more + 16 * (u // SLOTS + 1))



def stage_end(k, eng, sem, stage):
    eng.sem_inc(sem, 1)
    k.after(eng, stage)


def split_ahead(k, s, upto):
    for v in range(k.v_next, upto):
        u = UNIT_OF[v]
        k.slot_ready(s.eng, u)
        if v >= SPLITS:
            s.eng.wait_ge(k.unit_done, UNIT_OF[v - SPLITS] + 1)
        s.eng.copy(k.w_hi[:, v % SPLITS, :], k.ring[:, u % SLOTS, :]).then_inc(k.hi_done, 1)
    k.v_next = max(k.v_next, upto)


def products(pe, out, w, x, start, stop):
    pe.matmul(out, w[0], x[0], start=start, stop=False)
    pe.matmul(out, w[0], x[1], start=False, stop=False)
    return pe.matmul(out, w[1], x[0], start=False, stop=stop)


def unit_products(k, pe, buf, slot, hi, lo, blocks, widths, ready=None):
    for b in range(blocks):
        if ready is not None:
            pe.wait_ge(ready[0], ready[1] + b + 1)
        w = (k.w_hi[:, slot, b * P:(b + 1) * P], k.w_lo[:, slot, b * P:(b + 1) * P])
        col = 0
        for n in widths:
            last = products(pe, k.bank(2 * buf, n, col), w, (hi[:, b, col:col + n], lo[:, b, col:col + n]),
                            b == 0, b == blocks - 1)
            col += n
    last.then_inc(k.unit_done, 1)


def dense_tensor(k, pe, name, tiles, hi, lo, widths, evac, ready=None, nbuf=4):
    v0 = VFIRST[name]
    for j in range(tiles):
        if j >= nbuf:
            pe.wait_ge(evac, j - nbuf + 1)
        pe.wait_ge(k.lo_done, v0 + j + 1)
        unit_products(k, pe, j % nbuf, (v0 + j) % SPLITS, hi, lo, DT, widths, ready if j == 0 else None)


def values_tensor(k, pe, name, lo, blocks, width):
    v0 = VFIRST[name]
    per = 1024 // width
    for u in range(DT // per):
        slot = (v0 + u) % SPLITS
        pe.wait_ge(k.lo_done, v0 + u + 1)
        for b in range(blocks):
            for i in range(per):
                kt = u * per + i
                x = (k.h_hi[:, kt, b * P:(b + 1) * P], lo[:, kt, b * P:(b + 1) * P])
                w = (k.w_hi[:, slot, i * width:(i + 1) * width], k.w_lo[:, slot, i * width:(i + 1) * width])
                pe.matmul(k.bank(b, width), x[0], w[0], start=kt == 0, stop=False, skip_group_check=True)
                pe.matmul(k.bank(b, width), x[0], w[1], start=False, stop=False, skip_group_check=True)
                last = pe.matmul(k.bank(b, width), x[1], w[0], start=False, stop=kt == DT - 1, skip_group_check=True)
        last.then_inc(k.unit_done, 1)


NORMS = ["norm1", "mix1_post", "norm2", "ffn1_post", "mod_a0", "mod_f0", "mod_a1", "mod_f1"]


LOWERED = ["norm1", "norm2", "mod_a0", "mod_f0", "mod_a1", "mod_f1"]


def norms_before(name):
    return NORMS.index(name)


def norm_scalar(k, s, name, src, n):
    ready, used, c0 = k.sem("norm_squares"), k.sem("norm_summed"), DT * norms_before(name)
    for t in range(DT):
        if t >= 2:
            s.eng.wait_ge(used, c0 + t - 1)
        s.eng.activation(k.sq[:, t % 2, 0:n], src[:, t, 0:n], ACT.Square).then_inc(ready, 1)
        s.eng.wait_ge(ready, c0 + t + 1)
    s.eng.wait_ge(used, c0 + DT)
    s.eng.activation(k.rstd[:, 0:n], k.ps[:, 0:n], ACT.Sqrt, bias=k.eps).then_inc(k.sem("norm_rooted"), 1)
    s.eng.wait_ge(k.sem("norm_rooted"), norms_before(name) + 1)


def norm_tensor(k, pe, name, n):
    ready, used, c0 = k.sem("norm_squares"), k.sem("norm_summed"), DT * norms_before(name)
    for t in range(DT):
        pe.wait_ge(ready, c0 + t + 1)
        last = pe.matmul(k.bank(0), k.const("ones_d"), k.sq[:, t % 2, 0:S], start=t == 0, stop=t == DT - 1)
        if n > S:
            last = pe.matmul(k.bank(1, n - S), k.const("ones_d"), k.sq[:, t % 2, S:n], start=t == 0, stop=t == DT - 1)
        last.then_inc(used, 1)


def norm_rstd(k, v, name, n):
    v.eng.wait_ge(k.sem("norm_rooted"), norms_before(name) + 1)
    link(v, v.eng.reciprocal(k.rstd[:, 0:n], k.rstd[:, 0:n]))


def modulate_vector(k, v, name, layer, scale0, lo, n):
    norm_rstd(k, v, name, n)
    parts = [(q, a, b) for q, (a, b) in enumerate(((0, S), (S, n))) if b > a]
    c0 = DT * LOWERED.index(name)

    def lower(t):
        v.eng.wait_ge(k.sem("norm_hi"), c0 + t + 1)
        for q, a, b in parts:
            ins = v.eng.scalar_tensor_tensor(lo[:, t, a:b], k.sq[:, t % 2, a:b], k.mod[:, layer, scale0 - 8 + t, q:q + 1],
                                             k.h_hi[:, t, a:b].bitcast(F32), ALU.add, ALU.subtract)
            if (q, a, b) == parts[-1]:
                ins.then_inc(k.sem("norm_lo"), 1)
                v.eng.wait_ge(k.sem("norm_lo"), c0 + t + 1)
            else:
                link(v, ins)

    for t in range(DT):
        for q, a, b in parts:
            ins = v.eng.scalar_tensor_tensor(k.sq[:, t % 2, a:b], k.x[:, t, a:b], k.mod[:, layer, scale0 + t, q:q + 1],
                                             k.rstd[:, a:b], ALU.mult, ALU.mult)
            if (q, a, b) == parts[-1]:
                ins.then_inc(k.sem("norm_scaled"), 1)
                v.eng.wait_ge(k.sem("norm_scaled"), c0 + t + 1)
            else:
                link(v, ins)
        if t >= 1:
            lower(t - 1)
    lower(DT - 1)


def modulate_scalar(k, s, name, layer, shift0, n):
    norm_scalar(k, s, name, k.x, n)
    c0 = DT * LOWERED.index(name)
    parts = [(q, a, b) for q, (a, b) in enumerate(((0, S), (S, n))) if b > a]
    for t in range(DT):
        s.eng.wait_ge(k.sem("norm_scaled"), c0 + t + 1)
        for q, a, b in parts:
            ins = s.eng.activation(k.h_hi[:, t, a:b], k.sq[:, t % 2, a:b], ACT.Identity,
                                   bias=k.mod[:, layer, shift0 + t, q:q + 1])
            if (q, a, b) == parts[-1]:
                ins.then_inc(k.sem("norm_hi"), 1)
            else:
                link(s, ins)


class HeadNorm:

    def __init__(self, k, before, rotated_before, jobs):
        self.k, self.b, self.r, self.jobs = k, before, rotated_before, jobs
        self.squares, self.summed = k.sem("head_squares"), k.sem("head_summed")
        self.rooted, self.normed = k.sem("head_rooted"), k.sem("head_normed")
        self.swapped, self.rotated = k.sem("head_swapped"), k.sem("head_rotated")
        turns = [j[4] for j in jobs]
        self.before = [sum(turns[:i]) for i in range(len(jobs) + 1)]

    def scalar(self, s):
        k = self.k

        def root(j):
            n = self.jobs[j][0].shape[-1]
            s.eng.wait_ge(self.summed, self.b + j + 1)
            if j >= 2:
                s.eng.wait_ge(self.normed, self.b + j - 1)
            s.eng.activation(k.probs[:, j % 2, 0:n], k.ps[:, 1024 * (j % 2):1024 * (j % 2) + n], ACT.Sqrt,
                             bias=k.eps).then_inc(self.rooted, 1)
            s.eng.wait_ge(self.rooted, self.b + j + 1)

        for j, (x, _, _, _, _) in enumerate(self.jobs):
            if j >= 2:
                s.eng.wait_ge(self.summed, self.b + j - 1)
            s.eng.activation(k.sq[:, j % 2, 0:x.shape[-1]], x, ACT.Square).then_inc(self.squares, 1)
            s.eng.wait_ge(self.squares, self.b + j + 1)
            if j >= 1:
                root(j - 1)
        root(len(self.jobs) - 1)

    def tensor(self, pe):
        k = self.k

        def turn(j):
            x, _, _, _, rotate = self.jobs[j]
            if rotate:
                pe.wait_ge(self.normed, self.b + j + 1)
                if self.before[j]:
                    pe.wait_ge(self.rotated, self.r + self.before[j])
                pe.matmul(k.bank(4), k.const("rope_swap"), x[:, 0:S], start=True, stop=True).then_inc(self.swapped, 1)

        for j, (x, sums, _, _, _) in enumerate(self.jobs):
            n = x.shape[-1]
            pe.wait_ge(self.squares, self.b + j + 1)
            if j >= 2:
                pe.wait_ge(self.rooted, self.b + j - 1)
            last = pe.matmul(k.bank(2 * (j % 2)), sums, k.sq[:, j % 2, 0:S], start=True, stop=True)
            if n > S:
                last = pe.matmul(k.bank(2 * (j % 2) + 1, n - S), sums, k.sq[:, j % 2, S:n], start=True, stop=True)
            last.then_inc(self.summed, 1)
            if j >= 1:
                turn(j - 1)
        turn(len(self.jobs) - 1)

    def vector(self, v):
        k = self.k

        def turn(j):
            x, _, _, _, rotate = self.jobs[j]
            if rotate:
                v.eng.wait_ge(self.swapped, self.r + self.before[j] + 1)
                link(v, v.eng.tensor_tensor(k.probs_t[:, 0:S], k.bank(4), k.const("sin", 0, S), ALU.mult))
                link(v, v.eng.tensor_tensor(x[:, 0:S], x[:, 0:S], k.const("cos", 0, S), ALU.mult))
                v.eng.tensor_tensor(x[:, 0:S], x[:, 0:S], k.probs_t[:, 0:S], ALU.add).then_inc(self.rotated, 1)
                v.eng.wait_ge(self.rotated, self.r + self.before[j] + 1)

        for j, (x, _, gain, factor, _) in enumerate(self.jobs):
            n = x.shape[-1]
            v.eng.wait_ge(self.rooted, self.b + j + 1)
            link(v, v.eng.reciprocal(k.rstd[:, 0:n], k.probs[:, j % 2, 0:n]))
            if factor != 1.0:
                link(v, v.eng.tensor_scalar(k.rstd[:, 0:n], k.rstd[:, 0:n], factor, None, ALU.mult))
            if gain is None:
                ins = v.eng.tensor_tensor(x, x, k.rstd[:, 0:n], ALU.mult)
            else:
                ins = v.eng.scalar_tensor_tensor(x, x, gain, k.rstd[:, 0:n], ALU.mult, ALU.mult)
            ins.then_inc(self.normed, 1)
            v.eng.wait_ge(self.normed, self.b + j + 1)
            if j >= 1:
                turn(j - 1)
        turn(len(self.jobs) - 1)


class Attention:

    def __init__(self, k, before, products_before, items):
        self.k, self.b, self.items = k, before, items
        self.scores, self.maxed, self.exps = k.sem("att_scores"), k.sem("att_maxed"), k.sem("att_exps")
        self.normed, self.turned, self.copied = k.sem("att_normed"), k.sem("att_turned"), k.sem("att_copied")
        self.summed, self.stored = k.sem("att_summed"), k.sem("att_stored")
        self.m, n = [], products_before
        for it in items:
            self.m.append(n)
            n += not it["open"]

    def tensor(self, pe, between=None):
        k, N = self.k, len(self.items)
        for i in range(N + 2):
            if i < N:
                it = self.items[i]
                if i >= 2:
                    pe.wait_ge(self.exps, self.b + i - 1)
                base = 1024 * (i % 2)
                done = 0
                for kap, col in it["keys"]:
                    n = kap.shape[-1]
                    extra = [(a, b) for a, b, c in it["bias"] if c == col]
                    last = pe.matmul(k.ps[:, base + col:base + col + n], it["q"], kap, start=True, stop=not extra)
                    for e, (a, b) in enumerate(extra):
                        last = pe.matmul(k.ps[:, base + col:base + col + n], a, b, start=False, stop=e == len(extra) - 1)
                last.then_inc(self.scores, 1)
            if i >= 2 and not self.items[i - 2]["open"]:
                it, m = self.items[i - 2], self.m[i - 2]
                pe.wait_ge(self.copied, m + 1)
                if m >= self.m[0] + 2:
                    pe.wait_ge(self.stored, m - 1)
                for b, val in enumerate(it["values"]):
                    last = pe.matmul(k.bank(6 + m % 2, P), val, k.probs_t[:, b * P:(b + 1) * P], start=b == 0,
                                     stop=b == len(it["values"]) - 1)
                last.then_inc(self.summed, 1)
                if between is not None:
                    between(i - 2)
            if 1 <= i <= N and not self.items[i - 1]["open"]:
                it = self.items[i - 1]
                pe.wait_ge(self.normed, self.b + i)
                if self.m[i - 1] >= self.m[0] + 1:
                    pe.wait_ge(self.copied, self.m[i - 1])
                for b in range(len(it["values"])):
                    last = pe.transpose(k.bank(4 + b // 4, P, (b % 4) * P), k.probs[:, (i - 1) % 2, b * P:(b + 1) * P],
                                        k.const("ident"))
                last.then_inc(self.turned, 1)

    def vector(self, v):
        k, N = self.k, len(self.items)
        for i in range(N + 2):
            if i < N:
                n = P * len(self.items[i]["values"])
                v.eng.wait_ge(self.scores, self.b + i + 1)
                v.eng.tensor_reduce(k.small[:, i % 4:i % 4 + 1], k.ps[:, 1024 * (i % 2):1024 * (i % 2) + n],
                                    AX.X, ALU.max, negate=True).then_inc(self.maxed, 1)
                v.eng.wait_ge(self.maxed, self.b + i + 1)
            if 1 <= i <= N:
                it = self.items[i - 1]
                j, n = (i - 1) % 4, P * len(it["values"])
                pr = k.probs[:, (i - 1) % 2, 0:n]
                v.eng.wait_ge(self.exps, self.b + i)
                link(v, v.eng.reciprocal(k.small[:, 8 + j:9 + j], k.small[:, 4 + j:5 + j]))
                if it["factor"] is not None:
                    link(v, v.eng.tensor_tensor(k.small[:, 8 + j:9 + j], k.small[:, 8 + j:9 + j], it["factor"], ALU.mult))
                if it["adds"]:
                    ins = v.eng.scalar_tensor_tensor(pr, pr, k.small[:, 8 + j:9 + j], k.probs[:, i % 2, 0:n],
                                                     ALU.mult, ALU.add)
                else:
                    ins = v.eng.tensor_scalar(pr, pr, k.small[:, 8 + j:9 + j], None, ALU.mult)
                ins.then_inc(self.normed, 1)
                v.eng.wait_ge(self.normed, self.b + i)
            if i >= 2 and not self.items[i - 2]["open"]:
                it, m = self.items[i - 2], self.m[i - 2]
                v.eng.wait_ge(self.summed, m + 1)
                v.eng.tensor_copy(it["out"], k.bank(6 + m % 2, P)[it["rows"]]).then_inc(self.stored, 1)
                v.eng.wait_ge(self.stored, m + 1)

    def scalar(self, s):
        k, N = self.k, len(self.items)
        for i in range(N + 1):
            if i < N:
                n = P * len(self.items[i]["values"])
                s.eng.wait_ge(self.maxed, self.b + i + 1)
                if i >= 2:
                    if self.items[i - 2]["open"]:
                        s.eng.wait_ge(self.normed, self.b + i)
                    else:
                        s.eng.wait_ge(self.turned, self.m[i - 2] + 1)
                s.eng.activation(k.probs[:, i % 2, 0:n], k.ps[:, 1024 * (i % 2):1024 * (i % 2) + n], ACT.Exp,
                                 bias=k.small[:, i % 4:i % 4 + 1],
                                 accum_out=k.small[:, 4 + i % 4:5 + i % 4]).then_inc(self.exps, 1)
                s.eng.wait_ge(self.exps, self.b + i + 1)
            if i >= 1 and not self.items[i - 1]["open"]:
                n = P * len(self.items[i - 1]["values"])
                m = self.m[i - 1]
                s.eng.wait_ge(self.turned, m + 1)
                if m >= self.m[0] + 1:
                    s.eng.wait_ge(self.summed, m)
                s.eng.copy(k.probs_t[:, 0:n], k.ps[:, 2048:2048 + n]).then_inc(self.copied, 1)
                s.eng.wait_ge(self.copied, m + 1)


def plain_norm_vector(k, v, name, gain, lo):
    norm_rstd(k, v, name, S)
    c0 = DT * LOWERED.index(name)

    def lower(t):
        v.eng.wait_ge(k.sem("norm_hi"), c0 + t + 1)
        v.eng.tensor_tensor(lo[:, t, 0:S], k.sq[:, t % 2, 0:S], k.h_hi[:, t, 0:S].bitcast(F32),
                            ALU.subtract).then_inc(k.sem("norm_lo"), 1)
        v.eng.wait_ge(k.sem("norm_lo"), c0 + t + 1)

    for t in range(DT):
        v.eng.scalar_tensor_tensor(k.sq[:, t % 2, 0:S], k.x[:, t, 0:S], k.par(gain, t), k.rstd[:, 0:S],
                                   ALU.mult, ALU.mult).then_inc(k.sem("norm_scaled"), 1)
        v.eng.wait_ge(k.sem("norm_scaled"), c0 + t + 1)
        if t >= 1:
            lower(t - 1)
    lower(DT - 1)


def plain_norm_scalar(k, s, name):
    norm_scalar(k, s, name, k.x, S)
    c0 = DT * LOWERED.index(name)
    for t in range(DT):
        s.eng.wait_ge(k.sem("norm_scaled"), c0 + t + 1)
        s.eng.copy(k.h_hi[:, t, 0:S], k.sq[:, t % 2, 0:S]).then_inc(k.sem("norm_hi"), 1)


MIXES = ["mix1", "mix_e", "mix_o"]


def mix_split_scalar(k, s, name, n):
    for t in range(DT):
        s.eng.copy(k.h_hi[:, t, 0:n], k.mix[:, t, 0:n]).then_inc(k.sem("mix_hi"), 1)


def mix_split_vector(k, v, name, n):
    c0 = DT * MIXES.index(name)
    for t in range(DT):
        v.eng.wait_ge(k.sem("mix_hi"), c0 + t + 1)
        link(v, v.eng.tensor_tensor(k.mix_lo[:, t, 0:n], k.mix[:, t, 0:n], k.h_hi[:, t, 0:n].bitcast(F32), ALU.subtract))


def split_along(k, s, name, units, ahead):
    for j in range(units):
        split_ahead(k, s, min(VFIRST[name] + j + 1 + SPLITS, VFIRST[name] + units + ahead))


def post_norm_vector(k, v, name, m, gain):
    norm_rstd(k, v, name, S)
    for t in range(DT):
        link(v, v.eng.scalar_tensor_tensor(m[:, t, 0:S], m[:, t, 0:S], k.par(gain, t), k.rstd[:, 0:S],
                                          ALU.mult, ALU.mult))
        link(v, v.eng.tensor_tensor(k.x[:, t, 0:S], k.x[:, t, 0:S], m[:, t, 0:S], ALU.add))


def copy_out_scalar(k, s, name, tiles, dst, width, evac, scale=None):
    for j in range(tiles):
        s.eng.wait_ge(k.unit_done, FIRST[name] + j + 1)
        split_ahead(k, s, VFIRST[name] + j + 1 + SPLITS)
        w = width(j)
        src = k.ps[:, 1024 * (j % 4):1024 * (j % 4) + w]
        s.eng.activation(dst(j), src, ACT.Copy, scale=1.0 if scale is None else scale(j)).then_inc(evac, 1)
        s.eng.wait_ge(evac, j + 1)


def residual_vector(k, v, name, layer, n, evac):
    parts = ((0, S), (S, n)) if n > S else ((0, S),)
    for j in range(DT):
        v.eng.wait_ge(k.unit_done, FIRST[name] + j + 1)
        for q, (a, b) in enumerate(parts):
            base = 1024 * (j % 4)
            ins = v.eng.scalar_tensor_tensor(k.x[:, j, a:b], k.ps[:, base + a:base + b], k.mod[:, layer, 16 + j, q:q + 1],
                                             k.x[:, j, a:b], ALU.mult, ALU.add)
            if q == len(parts) - 1:
                ins.then_inc(evac, 1)
                v.eng.wait_ge(evac, j + 1)
            else:
                link(v, ins)



class Ffn:

    def __init__(self, k, name, layer, n, total=None):
        self.k, self.name, self.layer, self.n, self.total = k, name, layer, n, total
        self.parts = ((0, S), (S, n)) if n > S else ((0, S),)
        self.u0, self.v0 = FIRST[name], VFIRST[name]
        self.lin, self.act, self.taps = k.sem(name + "_lin"), k.sem(name + "_act"), k.sem(name + "_taps")
        self.hidden, self.upper, self.ready = k.sem(name + "_hidden"), k.sem(name + "_upper"), k.sem(name + "_ready")
        self.added = k.sem(name + "_added")
        if layer is not None:
            self.w, self.b = COL[f"ffn_w{layer}"][0], COL[f"ffn_b{layer}"][0]

    def off(self, c):
        return 2 * CHUNKS[c][0] + DT * c


def ffn1(k):
    return Ffn(k, "w_ffn1", None, S, k.view(k.big, 12288, DT, S))


def ffn_tensor(f, pe, ready):
    k = f.k
    widths = tuple(b - a for a, b in f.parts)
    for c, (m0, nm) in enumerate(CHUNKS):
        off = f.off(c)

        def up(it, static):
            for s in range(4):
                if not static:
                    pe.wait_ge(f.hidden, it * 2 + (m0 + s // 2 - 1))
                elif c:
                    pe.wait_ge(f.added, DT * (c - 1) + 4 + s + 1)
                pe.wait_ge(k.lo_done, it * 4 + (f.v0 + off + s + 1))
                unit_products(k, pe, s, (f.v0 + off + s) % SPLITS, k.h_hi, k.lo3, DT, widths,
                              ready if static and c == 0 and s == 0 else None)

        up(0, True)
        with pe.Fori(1, nm // 2) as it:
            up(it, False)
        for j in range(DT):
            if j < 4:
                pe.wait_ge(f.hidden, m0 + nm - 1 + j // 2)
            else:
                pe.wait_ge(f.added, DT * c + j - 3)
            v = f.v0 + off + 2 * nm + j
            pe.wait_ge(k.lo_done, v + 1)
            unit_products(k, pe, j % 4, v % SPLITS, k.hid_hi, k.hid_lo, nm, widths, (f.ready, m0) if j == 0 else None)


def ffn_scalar(f, s):
    k, n = f.k, f.n
    for c, (m0, nm) in enumerate(CHUNKS):
        u, v = f.u0 + f.off(c), f.v0 + f.off(c)

        def upper(it, j):
            s.eng.wait_ge(k.unit_done, it * 4 + (u + j + 1))
            k.slot_ready(s.eng, u + j + 2, (it, 4))
            s.eng.copy(k.w_hi[:, (v + j) % SPLITS, :], k.ring[:, (u + j + 2) % SLOTS, :]).then_inc(k.hi_done, 1)

        def up(it, static):
            for a in range(2):
                m = it * 2 + (m0 + a)
                g = 2048 * a
                tmp = k.probs[:, a, 0:n]
                upper(it, 2 * a)
                if not (static and c == 0):
                    s.eng.wait_ge(f.ready, m - 1)
                if f.layer is None:
                    s.eng.activation(tmp, k.ps[:, g:g + n], ACT.Silu).then_inc(f.act, 1)
                else:
                    s.eng.activation(tmp, k.ps[:, g:g + n], ACT.Identity, bias=k.params[:, bass.ds(m + f.b, 1)],
                                     scale=k.params[:, bass.ds(m * 3 + (f.w + 1), 1)]).then_inc(f.lin, 1)
                    s.eng.wait_ge(f.taps, m + 1)
                    s.eng.activation(tmp, tmp, ACT.Silu).then_inc(f.act, 1)
                upper(it, 2 * a + 1)
                s.eng.wait_ge(f.hidden, m + 1)
                s.eng.copy(k.hid_hi[:, it * 2 + a, 0:n], tmp).then_inc(f.upper, 1)

        up(0, True)
        with s.eng.Fori(1, nm // 2) as it:
            up(it, False)
        k.v_next = v + 2 * nm + SPLITS
        for j in range(DT):
            split_ahead(k, s, min(v + 2 * nm + j + 1 + SPLITS, len(UNIT_OF)))


def ffn_vector(f, v):
    k, n = f.k, f.n
    for c, (m0, nm) in enumerate(CHUNKS):
        u = f.u0 + f.off(c)

        def up(it):
            for a in range(2):
                m = it * 2 + (m0 + a)
                g, val = 2048 * a, 2048 * a + 1024
                tmp = k.probs[:, a, :]
                if f.layer is not None:
                    v.eng.wait_ge(f.lin, m + 1)
                    for q, (lo, hi) in enumerate(f.parts):
                        link(v, v.eng.scalar_tensor_tensor(tmp[:, lo + 1:hi], k.ps[:, g + lo:g + hi - 1],
                                                           k.params[:, bass.ds(m * 3 + f.w, 1)], tmp[:, lo + 1:hi],
                                                           ALU.mult, ALU.add))
                        ins = v.eng.scalar_tensor_tensor(tmp[:, lo:hi - 1], k.ps[:, g + lo + 1:g + hi],
                                                         k.params[:, bass.ds(m * 3 + (f.w + 2), 1)], tmp[:, lo:hi - 1],
                                                         ALU.mult, ALU.add)
                        if q == len(f.parts) - 1:
                            ins.then_inc(f.taps, 1)
                            v.eng.wait_ge(f.taps, m + 1)
                        else:
                            link(v, ins)
                v.eng.wait_ge(k.unit_done, it * 4 + (u + 2 * a + 2))
                v.eng.wait_ge(f.act, m + 1)
                v.eng.tensor_tensor(tmp[:, 0:n], tmp[:, 0:n], k.ps[:, val:val + n], ALU.mult).then_inc(f.hidden, 1)
                v.eng.wait_ge(f.upper, m + 1)
                v.eng.tensor_tensor(k.hid_lo[:, it * 2 + a, 0:n], tmp[:, 0:n], k.hid_hi[:, it * 2 + a, 0:n].bitcast(F32),
                                    ALU.subtract).then_inc(f.ready, 1)
                v.eng.wait_ge(f.ready, m + 1)

        per = 2 * (2 * len(f.parts) - 1) if f.layer is not None else 0
        up(0)
        with v.eng.Fori(1, nm // 2) as it:
            v.enter(it, per)
            up(it)
        v.leave(nm // 2 - 1)
        for j in range(DT):
            buf = 1024 * (j % 4)
            v.eng.wait_ge(k.unit_done, u + 2 * nm + j + 1)
            if f.layer is None:
                if c == 0:
                    ins = v.eng.tensor_copy(f.total[:, j, :], k.bank(2 * (j % 4)))
                else:
                    ins = v.eng.tensor_tensor(f.total[:, j, :], k.bank(2 * (j % 4)), f.total[:, j, :], ALU.add)
            else:
                for q, (a, b) in enumerate(f.parts):
                    ins = v.eng.scalar_tensor_tensor(k.x[:, j, a:b], k.ps[:, buf + a:buf + b],
                                                     k.mod[:, f.layer, 40 + j, q:q + 1], k.x[:, j, a:b],
                                                     ALU.mult, ALU.add)
                    if q < len(f.parts) - 1:
                        link(v, ins)
            ins.then_inc(f.added, 1)
            v.eng.wait_ge(f.added, DT * c + j + 1)



def ada_unit(k, pe, u, bank, col):
    k.slot_ready(pe, u)
    for b in range(DT):
        last = pe.matmul(k.bank(bank, 2, 256 + 2 * col), k.ring[:, u % SLOTS, b * P:(b + 1) * P],
                         k.small[:, 96 + 2 * b:98 + 2 * b], start=b == 0, stop=b == DT - 1)
    last.then_inc(k.unit_done, 1)


def ada_vector(k, v, name, layer, bank, first, units):
    v.eng.wait_ge(k.unit_done, FIRST[name] + units)
    at = 96 * layer + 2 * first
    link(v, v.eng.tensor_tensor(k.mod_flat[:, at:at + 2 * units], k.bank(bank, 2 * units, 256),
                                k.par(f"b_ada{layer}", 2 * first, 2 * units), ALU.add))
    for scale in (8, 32):
        a, b = max(scale, first), min(scale + 8, first + units)
        if a < b:
            link(v, v.eng.tensor_scalar(k.mod[:, layer, a:b, :], k.mod[:, layer, a:b, :], 1.0, None, ALU.add))



def gdn_views(k):
    b = {}
    b["qkvg"] = k.view(k.big, 0, 16, S)
    b["v_out"] = k.view(k.big, 4096, GH, PAIRS * P)
    b["at"] = k.view(k.big, 4096, 16, P)
    b["k_tok"] = k.view(k.big, 8192, 16, P)
    b["v_tok"] = k.view(k.big, 10240, 16, P)
    b["a"] = k.view(k.big, 12288, 16, P)
    b["t"] = k.view(k.big, 14336, 16, P)
    b["kbe"] = k.view(k.big, 2048, 16, P)
    b["tt"] = k.view(k.h_flat, 0, 16, P)
    b["attn"] = k.view(k.h_flat, 2048, 16, P)
    b["egc"] = k.view(k.h_flat, 4096, GH, S)
    b["am"] = k.view(k.mix_flat, 0, 16, P)
    b["state"] = k.view(k.probs_t, 0, GH, P)
    b["v_new"] = k.sq[:, 0, 0:S].rearrange("p (h n) -> p h n", h=GH)
    return b


def attn_views(k):
    return (k.view(k.big, 0, 4, T), k.view(k.big, 4 * T, 4, T), k.view(k.big, 8 * T, 6, HALF))


def dil_views(k):
    return (k.view(k.big, 0, 4, S), k.view(k.big, 2048, 4, S), k.view(k.big, 4096, 4, HALF),
            k.view(k.big, 6144, 8, S))


def item(q, keys, bias, values, out, rows=slice(0, P), factor=None, adds=False, is_open=False):
    return dict(q=q, keys=keys, bias=bias, values=values, out=out, rows=rows, factor=factor, adds=adds, open=is_open)


def dil_items(k):
    q, key, val, bias = dil_views(k)
    out = []
    for h in range(8):
        r, t = slice(HD * (h % 2), HD * (h % 2) + HD), h // 2
        for i in range(4):
            n = (i + 1) * P
            blk = slice(i * P, n)
            out.append(item(q[r, t, blk], [(key[r, t, 0:n], 0)],
                            [(k.const("flip"), bias[:, h, S - n:S], 0)],
                            [val[:, b, t * P:(t + 1) * P] for b in range(i + 1)], k.mix[r, 4 + t, blk], rows=r))
    return out


def na_items(k):
    q, key, val = attn_views(k)
    bias = k.view(k.big, 12 * T, 8, 14 * GRID_W)
    out = []
    for h in range(8):
        r, t = slice(HD * (h % 2), HD * (h % 2) + HD), h // 2
        vals = [val[:, b, t * P:(t + 1) * P] for b in range(6)]
        for i in range(6):
            blk = slice(i * P, (i + 1) * P)
            if i < 4:
                out.append(item(q[r, t, blk], [(key[r, t, 0:S], 0), (key[r, t, S:T], S)],
                                [(k.const("flip"), bias[:, h, (6 - 2 * i) * GRID_W:(6 - 2 * i) * GRID_W + S], 0),
                                 (k.const("ident"), k.const("na_mask", 0, S), 0)],
                                vals, k.mix[r, t, blk], rows=r))
            else:
                out.append(item(q[r, t, blk], [(key[r, t, S:T], 0)], [], vals[4:], k.mix[r, t, blk], rows=r))
    return out


def diff_items(k):
    q, key, val = attn_views(k)
    out = []
    for t in range(4):
        vals = [val[:, b, t * P:(t + 1) * P] for b in range(6)]
        for i in range(6):
            blk = slice(i * P, (i + 1) * P)
            for sub in range(2):
                r = slice(HD * sub, HD * sub + HD)
                keys = [(key[r, t, 0:S], 0), (key[r, t, S:T], S)] if i < 4 else [(key[r, t, S:T], 0)]
                out.append(item(q[r, t, blk], keys, [], vals if i < 4 else vals[4:], k.mix[:, 4 + t, blk],
                                factor=k.small[:, 116:117] if sub else None, adds=sub == 1, is_open=sub == 0))
    return out


def gqa_views(k):
    return k.view(k.big, 0, 4, T), k.view(k.big, 4 * T, 1, T), k.view(k.big, 5 * T, 6, P)


def gqa_items(k):
    q, key, val = gqa_views(k)
    out = []
    for t in range(4):
        for e in range(2):
            r = slice(HD * e, HD * e + HD)
            for i in range(4):
                blk = slice(i * P, (i + 1) * P)
                out.append(item(q[r, t, blk], [(key[r, 0, 0:S], 0), (key[r, 0, S:T], S)], [],
                                [val[:, b, :] for b in range(6)], k.mix[r, t, blk], rows=r))
    return out


def na_norm(k):
    q, key, _ = attn_views(k)
    return HeadNorm(k, 20, 8, [(q[:, t, :], k.const("heads64"), k.par("na_q"), HD ** -0.5, False) for t in range(4)]
                    + [(key[:, t, :], k.const("heads64"), k.par("na_k"), 1.0, False) for t in range(4)])


def diff_norm(k):
    q, key, _ = attn_views(k)
    return HeadNorm(k, 8, 0, [(q[:, t, :], k.const("heads64"), k.par("da_q"), HD ** -0.5, True) for t in range(4)]
                    + [(key[:, t, :], k.const("heads64"), k.par("da_k"), 1.0, True) for t in range(4)])


def gqa_norm(k):
    q, key, _ = gqa_views(k)
    return HeadNorm(k, 28, 8, [(q[:, t, 0:S], k.const("heads64"), k.par("gqa_q"), HD ** -0.5, True) for t in range(4)]
                    + [(key[:, 0, :], k.const("heads64"), k.par("gqa_k"), 1.0, True)])


def gdn_norm(k):
    x = gdn_views(k)["qkvg"]
    return HeadNorm(k, 0, 0, [(x[:, t, :], k.const("ones"), None, P ** -0.5 if t < 4 else 1.0, False)
                                    for t in range(8)])


def subln(k):
    return HeadNorm(k, 16, 8, [(k.mix[:, 4 + t, :], k.const("heads128"), k.par("subln"), 1.0 - LAM_INIT, False)
                                 for t in range(4)])


def hy_views(k):
    b = {}
    b["x"] = k.view(k.big, 0, 12, S)
    b["z"] = k.view(k.big, 6144, 4, S)
    b["even"] = k.view(k.big, 8192, 4, S)
    b["odd"] = k.view(k.big, 10240, 4, S)
    b["yc"] = k.view(k.big, 12288, 4, S)
    b["ys"] = k.view(k.big, 14336, 4, S)
    b["w4"] = k.big[0:ORDER, 12288:12288 + D]
    b["w1"] = k.big[0:EMB, 13312:13312 + ORDER]
    b["w2"] = k.big[0:ORDER, 13376:13376 + ORDER]
    b["w3"] = k.big[0:ORDER, 13440:13440 + ORDER]
    b["feats"] = k.big[0:EMB, 13568:13568 + S]
    b["cos"] = k.view(k.h_flat, 0, 4, S)
    b["sin"] = k.view(k.h_flat, 2048, 4, S)
    b["decay"] = k.view(k.h_flat, 4096, 4, S)
    return b



def spread(ap, n):
    return ap.unsqueeze(2).broadcast_to([ap.shape[0], ap.shape[1], n])


def by_head(k, col):
    return k.small[:, col:col + 16].rearrange("p (b h) -> p h b", h=GH)


def all_blocks(mat):
    return mat.unsqueeze(1).broadcast_to([P, 16, P])


def start_vector(k, v):
    v.eng.wait_ge(k.loaded, 64)
    v.eng.tensor_tensor(k.small[0:HD, 112:114], k.params[0:HD, COL["lambdas"][0]:COL["lambdas"][0] + 2],
                        k.params[0:HD, COL["lambdas"][0] + 2:COL["lambdas"][0] + 4], ALU.mult).then_inc(k.sem("lam_products"), 1)
    v.eng.wait_ge(k.sem("lam_products"), 1)
    v.eng.wait_ge(k.sem("lam_exps"), 1)
    link(v, v.eng.scalar_tensor_tensor(k.small[:, 116:117], k.small[:, 115:116], -LAM_INIT, k.small[:, 114:115],
                                      ALU.add, ALU.subtract))


def start_tensor(k, pe):
    pe.wait_ge(k.loaded, 64)
    pe.wait_ge(k.sem("lam_products"), 1)
    pe.matmul(k.bank(7, 2), k.consts[0:HD, CCOL["ones"][0]:CCOL["ones"][0] + P], k.small[0:HD, 112:114],
              start=True, stop=True).then_inc(k.sem("lam_sums"), 1)


def start_scalar(k, s):
    s.eng.wait_ge(k.loaded, 64)
    link(s, s.eng.activation(k.small[:, 96:112], k.par("cond", 0, 16), ACT.Silu))
    s.eng.wait_ge(k.sem("lam_sums"), 1)
    s.eng.activation(k.small[:, 114:116], k.bank(7, 2), ACT.Exp).then_inc(k.sem("lam_exps"), 1)
    s.eng.wait_ge(k.sem("lam_exps"), 1)


def values_vector(k, v, name, units, dst, width, blocks):
    v.eng.wait_ge(k.unit_done, FIRST[name] + units)
    for b in range(blocks):
        link(v, v.eng.tensor_copy(dst[:, b, :], k.bank(b, width)))



def dil_project_tensor(k, pe):
    dense_tensor(k, pe, "w_dil_qk", 8, k.h_hi, k.lo1, (S,), k.sem("dil_project_evac"), (k.sem("norm_lo"), 0))
    pe.wait_ge(k.sem("dil_project_evac"), 8)
    pe.wait_ge(k.sem("dil_tables"), 48)
    hot, rel, logs = k.big[0:BUCKETS, 10240:10240 + LINE], k.big[0:BUCKETS, 10880:10888], k.big[0:1, 10888:10888 + LINE]
    for off, n, b in ((0, 512, 6), (512, LINE - 512, 7)):
        pe.matmul(k.ps[0:8, b * 512:b * 512 + n], rel, hot[:, off:off + n], start=True, stop=False)
        last = pe.matmul(k.ps[0:8, b * 512:b * 512 + n], k.consts[0:1, CCOL["ones"][0]:CCOL["ones"][0] + 8],
                         logs[:, off:off + n], start=False, stop=True)
    last.then_inc(k.sem("dil_lines"), 1)
    values_tensor(k, pe, "w_dil_v", k.lo1, 4, HALF)


def dil_project_vector(k, v):
    v.eng.wait_ge(k.sem("dil_lines"), 1)
    v.eng.tensor_copy(k.big[0:8, 11528:11528 + LINE], k.ps[0:8, 6 * 512:6 * 512 + LINE]).then_inc(k.sem("dil_lines_kept"), 1)
    v.eng.wait_ge(k.sem("dil_lines_kept"), 1)
    values_vector(k, v, "w_dil_v", 4, dil_views(k)[2], HALF, 4)


def dil_project_scalar(k, s):
    q, key, _, _ = dil_views(k)
    copy_out_scalar(k, s, "w_dil_qk", 8, lambda j: (q if j < 4 else key)[:, j % 4, :], lambda j: S,
                    k.sem("dil_project_evac"), lambda j: HD ** -0.5 if j < 4 else 1.0)
    s.eng.wait_ge(k.sem("dil_lines_kept"), 1)
    s.eng.dma_start(k.dram["lines"].ap(), k.big[0:8, 11528:11528 + LINE]).then_inc(k.sem("dil_lines_out"), 16)
    split_along(k, s, "w_dil_v", 4, 0)
    s.eng.wait_ge(k.sem("dil_lines_out"), 16)
    s.eng.dma_start(dil_views(k)[3], bass.AP(k.dram["lines"], 0, [[1, P], [LINE, 8], [1, S]])).then_inc(k.sem("dil_bias"), 16)


def gdn_project_tensor(k, pe):
    dense_tensor(k, pe, "w_gdn", 16, k.h_hi, k.lo1, (S,), k.sem("gdn_taps"))
    slot = VFIRST["w_gdn_gates"] % SPLITS
    pe.wait_ge(k.lo_done, VFIRST["w_gdn_gates"] + 1)
    pe.wait_ge(k.sem("gdn_gate_left"), 1)
    for half in range(2):
        for b in range(DT):
            w = slice(b * 8 + half * GH, b * 8 + half * GH + GH)
            last = products(pe, k.ps[0:GH, half * 512:half * 512 + S], (k.w_hi[:, slot, w], k.w_lo[:, slot, w]),
                            (k.h_hi[:, b, 0:S], k.lo1[:, b, 0:S]), b == 0, b == DT - 1)
    last.then_inc(k.unit_done, 1)


def gdn_project_scalar(k, s):
    x = gdn_views(k)["qkvg"]

    def silu(j):
        s.eng.wait_ge(k.sem("gdn_taps"), j + 1)
        link(s, s.eng.activation(x[:, j, :], x[:, j, :], ACT.Silu))

    for j in range(16):
        s.eng.wait_ge(k.unit_done, FIRST["w_gdn"] + j + 1)
        split_ahead(k, s, min(VFIRST["w_gdn"] + j + 1 + SPLITS, VFIRST["w_out1"]))
        src = k.bank(2 * (j % 4))
        if j < 12:
            s.eng.activation(x[:, j, :], src, ACT.Copy, scale=k.par("conv_w", 4 * j + 3)).then_inc(k.sem("gdn_lin"), 1)
            s.eng.wait_ge(k.sem("gdn_lin"), j + 1)
        else:
            s.eng.activation(x[:, j, :], src, ACT.Silu).then_inc(k.sem("gdn_gate_left"), 1)
            s.eng.wait_ge(k.sem("gdn_gate_left"), j - 11)
        if 1 <= j <= 12:
            silu(j - 1)


def gdn_project_vector(k, v):
    x = gdn_views(k)["qkvg"]
    for j in range(12):
        v.eng.wait_ge(k.sem("gdn_lin"), j + 1)
        for back in (1, 2, 3):
            ins = v.eng.scalar_tensor_tensor(x[:, j, back:S], k.bank(2 * (j % 4), S - back), k.par("conv_w", 4 * j + 3 - back),
                                             x[:, j, back:S], ALU.mult, ALU.add)
            if back == 3:
                ins.then_inc(k.sem("gdn_taps"), 1)
                v.eng.wait_ge(k.sem("gdn_taps"), j + 1)
            else:
                link(v, ins)


def gdn_gates_scalar(k, s):
    r = slice(0, GH)
    s.eng.wait_ge(k.unit_done, FIRST["w_gdn_gates"] + 1)
    s.eng.activation(k.probs[r, 0, 0:S], k.ps[r, 0:S], ACT.Exp, scale=-1.0).then_inc(k.sem("gates_exp"), 1)
    s.eng.wait_ge(k.sem("gates_exp"), 1)
    link(s, s.eng.activation(k.small[r, 120:121], k.par("a_log")[r], ACT.Exp))
    s.eng.wait_ge(k.sem("gates_abs"), 1)
    link(s, s.eng.activation(k.rstd[r, 0:S], k.rstd[r, 0:S], ACT.Exp, scale=-1.0))
    s.eng.activation(k.rstd[r, 0:S], k.rstd[r, 0:S], ACT.Ln, bias=k.par("one")[r]).then_inc(k.sem("gates_exp"), 1)
    s.eng.wait_ge(k.sem("gates_exp"), 2)
    s.eng.wait_ge(k.sem("gates_sums"), 1)
    link(s, s.eng.activation(k.small[:, 48:64], k.bank(4, 16), ACT.Exp))
    s.eng.activation(k.small[:, 64:80], k.bank(5, 16), ACT.Exp).then_inc(k.sem("gates_exp"), 1)
    s.eng.wait_ge(k.sem("gates_exp"), 3)


def gdn_gates_vector(k, v):
    r = slice(0, GH)
    beta, y, soft = k.probs[r, 0, 0:S], k.probs[r, 1, 0:S], k.rstd[r, 0:S]
    v.eng.wait_ge(k.unit_done, FIRST["w_gdn_gates"] + 1)
    link(v, v.eng.tensor_scalar(y, k.ps[r, 512:512 + S], k.par("dt_bias")[r], None, ALU.add))
    v.eng.scalar_tensor_tensor(soft, y, -1.0, y, ALU.mult, ALU.max).then_inc(k.sem("gates_abs"), 1)
    v.eng.wait_ge(k.sem("gates_abs"), 1)
    v.eng.wait_ge(k.sem("gates_exp"), 2)
    link(v, v.eng.tensor_scalar(beta, beta, 1.0, None, ALU.add))
    link(v, v.eng.reciprocal(beta, beta))
    link(v, v.eng.scalar_tensor_tensor(y, y, 0.0, soft, ALU.max, ALU.add))
    v.eng.tensor_scalar(y, y, k.small[r, 120:121], -1.0, ALU.mult, ALU.mult).then_inc(k.sem("gates_rows"), 1)
    v.eng.wait_ge(k.sem("gates_rows"), 1)
    v.eng.wait_ge(k.sem("gates_turned"), 1)
    v.eng.tensor_copy(k.small[:, 16:48], k.bank(2, 32)).then_inc(k.sem("gates_cols"), 1)
    v.eng.wait_ge(k.sem("gates_cols"), 1)
    v.eng.wait_ge(k.sem("gates_exp"), 3)
    link(v, v.eng.tensor_tensor(k.small[:, 80:96], k.small[:, 48:64], k.small[:, 32:48], ALU.mult))


def gdn_gates_tensor(k, pe):
    r = slice(0, GH)
    pe.wait_ge(k.sem("gates_rows"), 1)
    for row, col in ((1, 0), (0, 16)):
        for b in range(PAIRS):
            last = pe.transpose(k.bank(2, GH, col + GH * b), k.probs[r, row, b * P:(b + 1) * P], k.const("ident")[r, 0:GH])
    last.then_inc(k.sem("gates_turned"), 1)
    pe.wait_ge(k.sem("gates_cols"), 1)
    pe.matmul(k.bank(4, 16), k.const("upto"), k.small[:, 16:32], start=True, stop=True)
    pe.matmul(k.bank(5, 16), k.const("later"), k.small[:, 16:32], start=True, stop=True).then_inc(k.sem("gates_sums"), 1)


def gdn_masks_tensor(k, pe):
    m = gdn_views(k)
    left = k.sem("masks_left")
    for g in range(8):
        if g >= 2:
            pe.wait_ge(left, g - 1)
        for b in range(PAIRS):
            last = pe.transpose(k.bank(g % 2, P, b * P), m["qkvg"][:, 4 + g, b * P:(b + 1) * P], k.const("ident"))
        last.then_inc(k.sem("masks_turned"), 1)
    pe.wait_ge(k.sem("masks_decays"), 1)
    for h in range(GH):
        if h >= 1:
            pe.wait_ge(k.sem("masks_exp"), 3 * h)
        for b in range(PAIRS):
            i = 4 * h + b
            pe.matmul(k.bank(2, P, b * P), k.const("upto"), m["tt"][:, i, :], start=True, stop=True)
            pe.matmul(k.bank(3, P, b * P), m["tt"][:, i, :], k.const("upto"), start=True, stop=True)
            last = pe.matmul(k.bank(4, P, b * P), m["attn"][:, i, :], k.const("upto"), start=True, stop=True)
        last.then_inc(k.sem("masks_sums"), 1)


def gdn_masks_vector(k, v):
    m = gdn_views(k)
    g_col = by_head(k, 16)
    for h in range(GH):
        link(v, v.eng.tensor_tensor(m["tt"][:, 4 * h:4 * h + 4, :], k.const("later").unsqueeze(1).broadcast_to([P, 4, P]),
                                   spread(g_col[:, h, :], P), ALU.mult))
        ins = v.eng.tensor_tensor(m["attn"][:, 4 * h:4 * h + 4, :], k.const("ones").unsqueeze(1).broadcast_to([P, 4, P]),
                                  spread(g_col[:, h, :], P), ALU.mult)
        if h < GH - 1:
            link(v, ins)
        else:
            ins.then_inc(k.sem("masks_decays"), 1)
            v.eng.wait_ge(k.sem("masks_decays"), 1)
    for g in range(8):
        v.eng.wait_ge(k.sem("masks_turned"), g + 1)
        src = k.bank(g % 2).rearrange("p (b n) -> p b n", b=PAIRS)
        if g < 4:
            ins = v.eng.tensor_copy(m["k_tok"][:, 4 * g:4 * g + 4, :], src)
        else:
            ins = v.eng.tensor_tensor(m["v_tok"][:, 4 * g - 16:4 * g - 12, :], src, spread(by_head(k, 32)[:, g - 4, :], P),
                                      ALU.mult)
        ins.then_inc(k.sem("masks_left"), 1)
        v.eng.wait_ge(k.sem("masks_left"), g + 1)
    v.eng.wait_ge(k.sem("masks_exp"), 12)
    link(v, v.eng.tensor_tensor(m["a"], m["a"], all_blocks(k.const("later")), ALU.mult))
    link(v, v.eng.tensor_tensor(m["at"], m["at"], all_blocks(k.const("upto")), ALU.mult))


def gdn_masks_scalar(k, s):
    m = gdn_views(k)
    s.eng.wait_ge(k.sem("masks_turned"), 8)
    for h in range(GH):
        s.eng.wait_ge(k.sem("masks_sums"), h + 1)
        blk = slice(4 * h, 4 * h + 4)
        for n, (dst, b) in enumerate(((m["a"][:, blk, :], 2), (m["at"][:, blk, :], 3),
                                      (m["egc"][:, h, :].rearrange("p (b n) -> p b n", b=4), 4))):
            s.eng.activation(dst, k.bank(b).rearrange("p (b n) -> p b n", b=4), ACT.Exp).then_inc(k.sem("masks_exp"), 1)
            s.eng.wait_ge(k.sem("masks_exp"), 3 * h + n + 1)


def gdn_products_tensor(k, pe):
    m = gdn_views(k)
    x = m["qkvg"]
    for h in range(GH):
        for b in range(PAIRS):
            kb = x[:, 4 + h, b * P:(b + 1) * P]
            pe.matmul(k.bank(h, P, b * P), kb, kb, start=True, stop=True)
            last = pe.matmul(k.bank(4 + h, P, b * P), kb, x[:, h, b * P:(b + 1) * P], start=True, stop=True)
        last.then_inc(k.sem("products_made"), 1)
    for h in range(GH):
        pe.wait_ge(k.sem("products_used"), h + 1)
        for b in range(PAIRS):
            last = pe.transpose(k.bank(h, P, b * P), m["a"][:, 4 * h + b, :], k.const("ident"))
        last.then_inc(k.sem("products_turned"), 1)


def gdn_products_vector(k, v):
    m = gdn_views(k)
    four = lambda ap: ap.rearrange("p (b n) -> p b n", b=4)
    for h in range(GH):
        blk = slice(4 * h, 4 * h + 4)
        v.eng.wait_ge(k.sem("products_made"), h + 1)
        link(v, v.eng.tensor_tensor(m["attn"][:, blk, :], four(k.bank(4 + h)), m["at"][:, blk, :], ALU.mult))
        link(v, v.eng.tensor_tensor(m["a"][:, blk, :], m["a"][:, blk, :], spread(by_head(k, 32)[:, h, :], P), ALU.mult))
        v.eng.tensor_tensor(m["a"][:, blk, :], four(k.bank(h)), m["a"][:, blk, :], ALU.mult).then_inc(k.sem("products_used"), 1)
        v.eng.wait_ge(k.sem("products_used"), h + 1)
    for h in range(GH):
        v.eng.wait_ge(k.sem("products_turned"), h + 1)
        link(v, v.eng.tensor_copy(m["at"][:, 4 * h:4 * h + 4, :], four(k.bank(h))))
    link(v, v.eng.tensor_copy(m["t"], all_blocks(k.const("ident"))))
    link(v, v.eng.tensor_copy(m["tt"], all_blocks(k.const("ident"))))


LEVELS = 6


def gdn_invert_vector(k, v):
    m = gdn_views(k)
    four = lambda ap: ap.rearrange("p (b n) -> p b n", b=4)
    for lev in range(LEVELS):
        v.eng.tensor_tensor(m["am"], m["at"], all_blocks(k.const("levels", lev * P)), ALU.mult).then_inc(k.sem("inv_masked"), 1)
        v.eng.wait_ge(k.sem("inv_masked"), lev + 1)
        for h in range(GH):
            blk = slice(4 * h, 4 * h + 4)
            v.eng.wait_ge(k.sem("inv_z"), GH * lev + h + 1)
            link(v, v.eng.tensor_tensor(m["t"][:, blk, :], m["t"][:, blk, :], four(k.bank(4 + h)), ALU.subtract))
            v.eng.tensor_tensor(m["tt"][:, blk, :], m["tt"][:, blk, :], four(k.bank(h)), ALU.subtract).then_inc(k.sem("inv_updated"), 1)
            v.eng.wait_ge(k.sem("inv_updated"), GH * lev + h + 1)


def gdn_invert_tensor(k, pe):
    m = gdn_views(k)
    for lev in range(LEVELS):
        pe.wait_ge(k.sem("inv_masked"), lev + 1)
        for h in range(GH):
            if lev >= 1:
                pe.wait_ge(k.sem("inv_updated"), GH * (lev - 1) + h + 1)
            for b in range(PAIRS):
                last = pe.matmul(k.bank(h, P, b * P), m["am"][:, 4 * h + b, :], m["t"][:, 4 * h + b, :], start=True, stop=True)
            last.then_inc(k.sem("inv_x"), 1)
        for h in range(GH):
            pe.wait_ge(k.sem("inv_x_kept"), GH * lev + h + 1)
            for b in range(PAIRS):
                i = 4 * h + b
                pe.matmul(k.bank(4 + h, P, b * P), m["tt"][:, i, :], m["a"][:, i, :], start=True, stop=True)
                last = pe.matmul(k.bank(h, P, b * P), m["a"][:, i, :], m["tt"][:, i, :], start=True, stop=True)
            last.then_inc(k.sem("inv_z"), 1)


def gdn_invert_scalar(k, s):
    m = gdn_views(k)
    for lev in range(LEVELS):
        for h in range(GH):
            s.eng.wait_ge(k.sem("inv_x"), GH * lev + h + 1)
            s.eng.copy(m["a"][:, 4 * h:4 * h + 4, :], k.bank(h).rearrange("p (b n) -> p b n", b=4)).then_inc(k.sem("inv_x_kept"), 1)
            s.eng.wait_ge(k.sem("inv_x_kept"), GH * lev + h + 1)


def gdn_apply_vector(k, v):
    m = gdn_views(k)
    four = lambda ap: ap.rearrange("p (b n) -> p b n", b=4)
    for h in range(GH):
        blk = slice(4 * h, 4 * h + 4)
        v.eng.tensor_tensor(m["kbe"][:, blk, :], m["k_tok"][:, blk, :], spread(by_head(k, 80)[:, h, :], P), ALU.mult).then_inc(k.sem("apply_kbe"), 1)
        v.eng.wait_ge(k.sem("apply_kbe"), h + 1)
        link(v, v.eng.tensor_tensor(m["k_tok"][:, blk, :], m["k_tok"][:, blk, :], spread(by_head(k, 64)[:, h, :], P), ALU.mult))
        link(v, v.eng.tensor_tensor(m["qkvg"][:, h, :], m["qkvg"][:, h, :], m["egc"][:, h, :], ALU.mult))
    for h in range(GH):
        v.eng.wait_ge(k.sem("apply_made"), h + 1)
        link(v, v.eng.tensor_copy(m["t"][:, 4 * h:4 * h + 4, :], four(k.bank(4 + h))))
    link(v, v.eng.memset(m["state"], 0.0))


def gdn_apply_scalar(k, s):
    m = gdn_views(k)
    for h in range(GH):
        s.eng.wait_ge(k.sem("apply_made"), h + 1)
        link(s, s.eng.copy(m["a"][:, 4 * h:4 * h + 4, :], k.bank(h).rearrange("p (b n) -> p b n", b=4)))


def gdn_apply_tensor(k, pe):
    m = gdn_views(k)
    for h in range(GH):
        pe.wait_ge(k.sem("apply_kbe"), h + 1)
        for b in range(PAIRS):
            i = 4 * h + b
            pe.matmul(k.bank(h, P, b * P), m["tt"][:, i, :], m["v_tok"][:, i, :], start=True, stop=True)
            last = pe.matmul(k.bank(4 + h, P, b * P), m["kbe"][:, i, :], m["tt"][:, i, :], start=True, stop=True)
        last.then_inc(k.sem("apply_made"), 1)


def gdn_scan_tensor(k, pe):
    m = gdn_views(k)
    for n in range(S // CHUNK):
        r, c = slice(CHUNK * (n % 2), CHUNK * (n % 2) + CHUNK), slice(CHUNK * n, CHUNK * (n + 1))
        if n:
            pe.wait_ge(k.sem("scan_state"), n)
        for h in range(GH):
            last = pe.matmul(k.ps[r, 4 * 512 + h * P:4 * 512 + (h + 1) * P], m["t"][:, 4 * h + n // 2, r],
                             m["state"][:, h, :], start=True, stop=True)
        last.then_inc(k.sem("scan_read"), 1)
        for a in (2 * n, 2 * n + 1):
            ada_unit(k, pe, FIRST["w_ada0_b"] + a, 6, a)
        for h in range(GH):
            pe.matmul(k.ps[:, h * 512 + n * CHUNK:h * 512 + (n + 1) * CHUNK], m["state"][:, h, :], m["qkvg"][:, h, c],
                      start=True, stop=False)
        pe.wait_ge(k.sem("scan_new"), n + 1)
        for h in range(GH):
            pe.matmul(k.ps[:, h * 512 + n * CHUNK:h * 512 + (n + 1) * CHUNK], m["v_new"][r, h, :],
                      m["attn"][r, 4 * h + n // 2, r], start=False, stop=True)
        for h in range(GH):
            last = pe.matmul(k.bank(5, P, h * P), m["k_tok"][r, 4 * h + n // 2, :], m["v_new"][r, h, :],
                             start=True, stop=True)
        last.then_inc(k.sem("scan_added"), 1)


def gdn_scan_vector(k, v):
    m = gdn_views(k)
    for n in range(S // CHUNK):
        r = slice(CHUNK * (n % 2), CHUNK * (n % 2) + CHUNK)
        u = m["a"].rearrange("p (h b) n -> p h b n", h=GH)[r, :, n // 2, :]
        v.eng.wait_ge(k.sem("scan_read"), n + 1)
        v.eng.tensor_tensor(m["v_new"][r], u, k.bank(4)[r].rearrange("p (h n) -> p h n", h=GH), ALU.subtract).then_inc(k.sem("scan_new"), 1)
        v.eng.wait_ge(k.sem("scan_new"), n + 1)
        v.eng.wait_ge(k.sem("scan_added"), n + 1)
        for h in range(GH):
            ins = v.eng.scalar_tensor_tensor(m["state"][:, h, :], m["state"][:, h, :],
                                             m["egc"][:, h, CHUNK * n + CHUNK - 1:CHUNK * (n + 1)], k.bank(5, P, h * P),
                                             ALU.mult, ALU.add)
            if h < GH - 1:
                link(v, ins)
            else:
                ins.then_inc(k.sem("scan_state"), 1)
                v.eng.wait_ge(k.sem("scan_state"), n + 1)


def gdn_out_scalar(k, s):
    for h in range(GH):
        if h >= 2:
            s.eng.wait_ge(k.sem("gdn_out_sums"), h - 1)
        s.eng.activation(k.sq[:, h % 2, 0:S], k.bank(h), ACT.Square).then_inc(k.sem("gdn_out_squares"), 1)
        s.eng.wait_ge(k.sem("gdn_out_squares"), h + 1)
    for h in range(GH):
        s.eng.wait_ge(k.sem("gdn_out_sums"), h + 1)
        s.eng.activation(k.bank(4 + h), k.bank(4 + h), ACT.Sqrt, bias=k.eps).then_inc(k.sem("gdn_out_roots"), 1)
        s.eng.wait_ge(k.sem("gdn_out_roots"), h + 1)


def gdn_out_tensor(k, pe):
    for h in range(GH):
        pe.wait_ge(k.sem("gdn_out_squares"), h + 1)
        pe.matmul(k.bank(4 + h), k.const("heads128"), k.sq[:, h % 2, 0:S], start=True, stop=True)\
            .then_inc(k.sem("gdn_out_sums"), 1)


def gdn_out_vector(k, v):
    gate = gdn_views(k)["qkvg"]
    for h in range(GH):
        out = k.mix[:, h, 0:S]
        v.eng.wait_ge(k.sem("gdn_out_roots"), h + 1)
        link(v, v.eng.reciprocal(k.rstd[:, 0:S], k.bank(4 + h)))
        link(v, v.eng.scalar_tensor_tensor(out, k.bank(h), k.par("onorm"), k.rstd[:, 0:S], ALU.mult, ALU.mult))
        link(v, v.eng.tensor_tensor(out, out, gate[:, 12 + h, :], ALU.mult))


def mix1_out_vector(k, v):
    m = k.view(k.big, 0, DT, S)
    for j in range(DT):
        v.eng.wait_ge(k.unit_done, FIRST["w_out1"] + j + 1)
        v.eng.tensor_copy(m[:, j, :], k.bank(2 * (j % 4))).then_inc(k.sem("mix1_evac"), 1)
        v.eng.wait_ge(k.sem("mix1_evac"), j + 1)



def hy_project_scalar(k, s):
    x = hy_views(k)["x"]
    for j in range(12):
        s.eng.wait_ge(k.unit_done, FIRST["w_hy"] + j + 1)
        split_ahead(k, s, VFIRST["w_hy"] + j + 1 + SPLITS)
        s.eng.activation(x[:, j, :], k.bank(2 * (j % 4)), ACT.Identity, bias=k.par("hy_conv_b", j),
                         scale=k.par("hy_conv_w", 3 * j + 1)).then_inc(k.sem("hy_lin"), 1)
        s.eng.wait_ge(k.sem("hy_lin"), j + 1)


def hy_project_vector(k, v):
    x = hy_views(k)["x"]
    for j in range(12):
        v.eng.wait_ge(k.sem("hy_lin"), j + 1)
        link(v, v.eng.scalar_tensor_tensor(x[:, j, 1:S], k.bank(2 * (j % 4), S - 1), k.par("hy_conv_w", 3 * j),
                                          x[:, j, 1:S], ALU.mult, ALU.add))
        v.eng.scalar_tensor_tensor(x[:, j, 0:S - 1], k.bank(2 * (j % 4), S - 1, 1), k.par("hy_conv_w", 3 * j + 2),
                                   x[:, j, 0:S - 1], ALU.mult, ALU.add).then_inc(k.sem("hy_taps_done"), 1)
        v.eng.wait_ge(k.sem("hy_taps_done"), j + 1)
    for t in range(4):
        link(v, v.eng.tensor_tensor(x[:, 8 + t, :], x[:, 8 + t, :], x[:, 4 + t, :], ALU.mult))


def hy_filter_tensor(k, pe):
    b = hy_views(k)
    pe.wait_ge(k.sem("hy_net_loaded"), 80)
    pe.matmul(k.ps[0:ORDER, 0:S], b["w1"], b["feats"], start=True, stop=True).then_inc(k.sem("hy_layer"), 1)
    for t in range(4):
        if t >= 2:
            pe.wait_ge(k.sem("hy_z_kept"), t - 1)
        for c in range(4):
            last = pe.transpose(k.bank(6 + t % 2, P, c * P), b["x"][:, 8 + c, t * P:(t + 1) * P], k.const("ident"))
        last.then_inc(k.sem("hy_z_turned"), 1)
    for n, w in ((1, "w2"), (2, "w3")):
        pe.wait_ge(k.sem("hy_sin"), n)
        pe.matmul(k.ps[0:ORDER, 0:S], b[w], k.probs[0:ORDER, 0, 0:S], start=True, stop=True).then_inc(k.sem("hy_layer"), 1)


def hy_filter_scalar(k, s):
    b = hy_views(k)
    for t in range(4):
        s.eng.wait_ge(k.sem("hy_z_turned"), t + 1)
        s.eng.copy(b["z"][:, t, :], k.bank(6 + t % 2)).then_inc(k.sem("hy_z_kept"), 1)
        s.eng.wait_ge(k.sem("hy_z_kept"), t + 1)
    for n in range(3):
        s.eng.wait_ge(k.sem("hy_reduced"), n + 1)
        s.eng.activation(k.probs[0:ORDER, 0, 0:S], k.probs[0:ORDER, 1, 0:S], ACT.Sin).then_inc(k.sem("hy_sin"), 1)
        s.eng.wait_ge(k.sem("hy_sin"), n + 1)


def hy_filter_vector(k, v):
    r = slice(0, ORDER)
    arg, turns = k.probs[r, 1, 0:S], k.sq[r, 0, 0:S]
    for n in range(3):
        v.eng.wait_ge(k.sem("hy_layer"), n + 1)
        link(v, v.eng.tensor_scalar(arg, k.ps[r, 0:S], k.par("hy_b", n)[r], k.par("hy_freq")[r], ALU.add, ALU.mult))
        link(v, v.eng.tensor_scalar(turns, arg, 1.0 / (2.0 * np.pi), ROUND, ALU.mult, ALU.add))
        link(v, v.eng.tensor_scalar(turns, turns, ROUND, None, ALU.subtract))
        link(v, v.eng.scalar_tensor_tensor(arg, turns, -TWO_PI_HI, arg, ALU.mult, ALU.add))
        link(v, v.eng.scalar_tensor_tensor(arg, turns, -TWO_PI_LO, arg, ALU.mult, ALU.add))
        v.eng.tensor_scalar(arg, arg, PI_IN, -PI_IN, ALU.min, ALU.max).then_inc(k.sem("hy_reduced"), 1)
        v.eng.wait_ge(k.sem("hy_reduced"), n + 1)


def hy_taps_tensor(k, pe):
    b = hy_views(k)

    def sums(t):
        pe.wait_ge(k.sem("hy_sizes"), t + 1)
        for c in range(4):
            last = pe.matmul(k.bank(4 + c, 1), k.sq[:, t % 2, c * P:(c + 1) * P], k.const("ones")[:, 0:1],
                             start=t == 0, stop=t == 3)
        last.then_inc(k.sem("hy_summed"), 1)

    for t in range(4):
        if t >= 2:
            pe.wait_ge(k.sem("hy_taps_made"), t - 1)
        hid = k.probs[0:ORDER, 0, t * P:(t + 1) * P]
        pe.matmul(k.bank(2 * (t % 2)), hid, b["w4"][:, 0:S], start=True, stop=True)
        pe.matmul(k.bank(2 * (t % 2) + 1), hid, b["w4"][:, S:2 * S], start=True, stop=True).then_inc(k.sem("hy_raw"), 1)
        if t >= 1:
            sums(t - 1)
    sums(3)


def hy_taps_vector(k, v):
    b = hy_views(k)
    v.eng.wait_ge(k.sem("hy_tables"), 48)
    fwd, bwd = k.rstd[:, 0:S], k.probs_t[:, 0:S]
    for t in range(4):
        v.eng.wait_ge(k.sem("hy_raw"), t + 1)
        link(v, v.eng.tensor_tensor(fwd, k.bank(2 * (t % 2)), b["decay"][:, t, :], ALU.mult))
        if t == 0:
            link(v, v.eng.scalar_tensor_tensor(bwd, k.bank(1), k.par("hy_first"), b["decay"][:, 0, :], ALU.mult, ALU.mult))
        else:
            link(v, v.eng.tensor_tensor(bwd, k.bank(2 * (t % 2) + 1), b["decay"][:, t, :], ALU.mult))
        link(v, v.eng.tensor_tensor(b["even"][:, t, :], fwd, bwd, ALU.add))
        link(v, v.eng.tensor_tensor(b["odd"][:, t, :], fwd, bwd, ALU.subtract))
        v.eng.scalar_tensor_tensor(fwd, fwd, -1.0, fwd, ALU.mult, ALU.max).then_inc(k.sem("hy_taps_made"), 1)
        v.eng.wait_ge(k.sem("hy_taps_made"), t + 1)
        link(v, v.eng.scalar_tensor_tensor(bwd, bwd, -1.0, bwd, ALU.mult, ALU.max))
        if t >= 2:
            v.eng.wait_ge(k.sem("hy_summed"), t - 1)
        v.eng.tensor_tensor(k.sq[:, t % 2, 0:S], fwd, bwd, ALU.add).then_inc(k.sem("hy_sizes"), 1)
        v.eng.wait_ge(k.sem("hy_sizes"), t + 1)
    v.eng.wait_ge(k.sem("hy_summed"), 4)
    for c in range(4):
        link(v, v.eng.reciprocal(k.small[:, 124 + c:125 + c], k.bank(4 + c, 1)))


def hy_forward_tensor(k, pe):
    b = hy_views(k)
    for f in range(4):
        if f >= 2:
            pe.wait_ge(k.sem("hy_product"), f - 1)
        col = slice(f * P, (f + 1) * P)
        for n, (table, src) in enumerate((("cos", "z"), ("sin", "z"), ("cos", "even"), ("sin", "odd"))):
            for t in range(4):
                last = pe.matmul(k.bank(4 * (f % 2) + n), b[table][:, t, col], b[src][:, t, :], start=t == 0, stop=t == 3)
        last.then_inc(k.sem("hy_bins"), 1)


def hy_forward_scalar(k, s):
    for f in range(4):
        s.eng.wait_ge(k.sem("hy_bins"), f + 1)
        if f >= 1:
            s.eng.wait_ge(k.sem("hy_product"), f)
        link(s, s.eng.copy(k.sq[:, 0, 0:S], k.bank(4 * (f % 2))))
        s.eng.copy(k.sq[:, 1, 0:S], k.bank(4 * (f % 2) + 1)).then_inc(k.sem("hy_bins_kept"), 1)
        s.eng.wait_ge(k.sem("hy_bins_kept"), f + 1)


def hy_forward_vector(k, v):
    b = hy_views(k)
    zc, zs, tmp = k.sq[:, 0, 0:S], k.sq[:, 1, 0:S], k.rstd[:, 0:S]
    for f in range(4):
        kc, ks = k.bank(4 * (f % 2) + 2), k.bank(4 * (f % 2) + 3)
        yc, ys = b["yc"][:, f, :], b["ys"][:, f, :]
        v.eng.wait_ge(k.sem("hy_bins_kept"), f + 1)
        link(v, v.eng.tensor_tensor(yc, zc, kc, ALU.mult))
        link(v, v.eng.tensor_tensor(tmp, zs, ks, ALU.mult))
        link(v, v.eng.tensor_tensor(yc, yc, tmp, ALU.subtract))
        link(v, v.eng.tensor_tensor(ys, zc, ks, ALU.mult))
        link(v, v.eng.tensor_tensor(tmp, zs, kc, ALU.mult))
        v.eng.tensor_tensor(ys, ys, tmp, ALU.add).then_inc(k.sem("hy_product"), 1)
        v.eng.wait_ge(k.sem("hy_product"), f + 1)


def hy_inverse_tensor(k, pe):
    b = hy_views(k)
    pe.wait_ge(k.sem("hy_tables"), 80)
    for c in range(4):
        for n, (src, table) in enumerate((("yc", "cos"), ("ys", "sin"))):
            for f in range(4):
                last = pe.matmul(k.bank(c), b[src][:, f, c * P:(c + 1) * P], b[table][:, f, :],
                                 start=n == 0 and f == 0, stop=n == 1 and f == 3)
        last.then_inc(k.sem("hy_back"), 1)


def hy_inverse_vector(k, v):
    x = hy_views(k)["x"]
    for c in range(4):
        out = k.mix[:, 4 + c, 0:S]
        v.eng.wait_ge(k.sem("hy_back"), c + 1)
        link(v, v.eng.tensor_scalar(out, k.bank(c), k.small[:, 124 + c:125 + c], None, ALU.mult))
        link(v, v.eng.scalar_tensor_tensor(out, x[:, 8 + c, :], k.par("hy_skip", c), out, ALU.mult, ALU.add))
        link(v, v.eng.tensor_tensor(out, out, x[:, c, :], ALU.mult))



def sync_program(k, sp):
    d = k.dram
    sp.dma_start(k.x[:, :, 0:S], d["x"]).then_inc(k.loaded, 16)
    sp.dma_start(k.x[:, :, S:T], d["ctx"]).then_inc(k.loaded, 16)
    sp.dma_start(k.params[:, :], d["params"]).then_inc(k.loaded, 16)
    sp.dma_start(k.consts[:, :], d["consts"]).then_inc(k.loaded, 16)
    split_of = {u: v for v, u in enumerate(UNIT_OF)}
    for name, n, width, split in STREAM:
        u0 = FIRST[name]

        def load(i, a, at):
            before = u0 + a - SLOTS
            if before in split_of:
                sp.wait_ge(k.lo_done, at + (split_of[before] + 1))
            elif before >= 0:
                sp.wait_ge(k.unit_done, at + (before + 1))
            sp.dma_start(k.ring[:, (u0 + a) % SLOTS, 0:width], d[name][i])\
                .then_inc(k.slot_landed[(u0 + a) % SLOTS], 16)

        for a in range(min(n, SLOTS)):
            load(a, a, 0)
        passes = max(n - SLOTS, 0) // SLOTS
        if passes > 1:
            with sp.Fori(0, passes) as it:
                for a in range(SLOTS):
                    load(it * SLOTS + (SLOTS + a), SLOTS + a, it * SLOTS)
        for a in range(SLOTS + (passes * SLOTS if passes > 1 else 0), n):
            load(a, a, 0)
    k.after(sp, "ffn3")
    sp.dma_start(d["out"], k.x[:, :, 0:S]).then_inc(k.sem("out_written"), 16)
    sp.wait_ge(k.sem("out_written"), 16)


def gpsimd_program(k, pool):
    v0 = 0
    while v0 < len(UNIT_OF):
        n = 1
        while v0 + n < len(UNIT_OF) and UNIT_OF[v0 + n] == UNIT_OF[v0] + n:
            n += 1

        def lower(a, at):
            v, u = v0 + a, UNIT_OF[v0] + a
            pool.wait_ge(k.hi_done, at + (v + 1))
            pool.tensor_tensor(k.w_lo[:, v % SPLITS, :], k.ring[:, u % SLOTS, :], k.w_hi[:, v % SPLITS, :].bitcast(F32),
                               ALU.subtract).then_inc(k.lo_done, 1)

        with pool.Fori(0, n // SLOTS) as it:
            for a in range(SLOTS):
                lower(a, it * SLOTS)
        for a in range(n // SLOTS * SLOTS, n):
            lower(a, 0)
        v0 += n



def load_distance_tables(k, act):
    hot, d = k.sem("dil_tables"), k.dram
    act.dma_start(k.big[0:BUCKETS, 10240:10240 + LINE], d["buckets"]).then_inc(hot, 16)
    act.dma_start(k.big[0:BUCKETS, 10880:10888], d["rel_bias"]).then_inc(hot, 16)
    act.dma_start(k.big[0:1, 10888:10888 + LINE], d["log_counts"]).then_inc(hot, 16)


def load_na_bias(k, act):
    bias = k.view(k.big, 12 * T, 8, 14 * GRID_W)
    wide = 2 * GRID_W - 1
    for h in range(8):
        for a in range(2):
            act.dma_start(bias[GRID_W * a:GRID_W * (a + 1), h, :].rearrange("p (r c) -> p r c", c=GRID_W),
                          bass.AP(k.dram["rpb"], (h * 15 + a) * wide, [[1, GRID_W], [wide, 14], [1, GRID_W]]))\
                .then_inc(k.sem("na_bias"), 16)


def load_hyena(k, act):
    b, d = hy_views(k), k.dram
    for name, src in (("w1", "hy_w1"), ("w2", "hy_w2"), ("w3", "hy_w3"), ("w4", "hy_w4"), ("feats", "feats")):
        act.dma_start(b[name], d[src]).then_inc(k.sem("hy_net_loaded"), 16)
    for name, src in (("decay", "decay"), ("cos", "dft_cos"), ("sin", "dft_sin")):
        act.dma_start(b[name], d[src]).then_inc(k.sem("hy_tables"), 16)


def load_hyena_inverse(k, act):
    b, d = hy_views(k), k.dram
    for name, src in (("cos", "idft_cos"), ("sin", "idft_sin")):
        act.dma_start(b[name], d[src]).then_inc(k.sem("hy_tables"), 16)


def tensor_program(k, pe):
    start_tensor(k, pe)
    k.after(pe, "start")
    norm_tensor(k, pe, "norm1", S)
    dil_project_tensor(k, pe)
    k.after(pe, "dil_project")
    pe.wait_ge(k.sem("dil_bias"), 16)
    Attention(k, 0, 0, dil_items(k)).tensor(pe, lambda i: ada_unit(k, pe, FIRST["w_ada0_a"] + i, 5, i))
    k.after(pe, "dil_attend")
    gdn_project_tensor(k, pe)
    k.after(pe, "gdn_project")
    gdn_gates_tensor(k, pe)
    k.after(pe, "gdn_gates")
    gdn_norm(k).tensor(pe)
    k.after(pe, "gdn_norm_qk")
    gdn_masks_tensor(k, pe)
    k.after(pe, "gdn_masks")
    gdn_products_tensor(k, pe)
    k.after(pe, "gdn_products")
    gdn_invert_tensor(k, pe)
    k.after(pe, "gdn_invert")
    gdn_apply_tensor(k, pe)
    k.after(pe, "gdn_apply")
    gdn_scan_tensor(k, pe)
    k.after(pe, "gdn_scan")
    gdn_out_tensor(k, pe)
    k.after(pe, "mix1_split")
    dense_tensor(k, pe, "w_out1", DT, k.h_hi, k.mix_lo, (S,), k.sem("mix1_evac"))
    k.after(pe, "mix1_out")
    norm_tensor(k, pe, "mix1_post", S)
    k.after(pe, "mix1_post")
    norm_tensor(k, pe, "norm2", S)
    norm_lo = lambda name: (k.sem("norm_lo"), DT * LOWERED.index(name))
    ffn_tensor(ffn1(k), pe, norm_lo("norm2"))
    k.after(pe, "ffn1")
    norm_tensor(k, pe, "ffn1_post", S)
    k.after(pe, "ffn1_post")
    norm_tensor(k, pe, "mod_a0", T)
    dense_tensor(k, pe, "w_diff_qk", 8, k.h_hi, k.lo2, (S, CTX), k.sem("diff_project_evac"), norm_lo("mod_a0"))
    pe.wait_ge(k.sem("diff_project_evac"), 8)
    values_tensor(k, pe, "w_diff_v", k.lo2, 6, HALF)
    k.after(pe, "diff_project")
    diff_norm(k).tensor(pe)
    k.after(pe, "diff_norm")
    Attention(k, 32, 32, diff_items(k)).tensor(pe)
    k.after(pe, "diff_attend")
    subln(k).tensor(pe)
    k.after(pe, "diff_subln")
    dense_tensor(k, pe, "w_na_qk", 8, k.h_hi, k.lo2, (S, CTX), k.sem("na_project_evac"))
    pe.wait_ge(k.sem("na_project_evac"), 8)
    values_tensor(k, pe, "w_na_v", k.lo2, 6, HALF)
    k.after(pe, "na_project")
    na_norm(k).tensor(pe)
    k.after(pe, "na_norm")
    pe.wait_ge(k.sem("na_bias"), 256)
    Attention(k, 80, 56, na_items(k)).tensor(pe, lambda i: ada_unit(k, pe, FIRST["w_ada1"] + i, 5, i))
    k.after(pe, "mix_e_split")
    dense_tensor(k, pe, "w_out_e", DT, k.h_hi, k.mix_lo, (S, CTX), k.sem("mix_e_evac"))
    k.after(pe, "mix_e_out")
    norm_tensor(k, pe, "mod_f0", T)
    ffn_tensor(Ffn(k, "w_ffn2", 0, T), pe, norm_lo("mod_f0"))
    k.after(pe, "ffn2")
    norm_tensor(k, pe, "mod_a1", T)
    dense_tensor(k, pe, "w_gqa_qk", 5, k.h_hi, k.lo2, (S, CTX), k.sem("gqa_project_evac"), norm_lo("mod_a1"))
    pe.wait_ge(k.sem("gqa_project_evac"), 5)
    values_tensor(k, pe, "w_gqa_v", k.lo2, 6, P)
    k.after(pe, "gqa_project")
    gqa_norm(k).tensor(pe)
    k.after(pe, "gqa_norm")
    Attention(k, 128, 104, gqa_items(k)).tensor(pe)
    k.after(pe, "gqa_attend")
    dense_tensor(k, pe, "w_hy", 12, k.h_hi, k.lo2, (S,), k.sem("hy_taps_done"))
    k.after(pe, "hy_project")
    hy_filter_tensor(k, pe)
    k.after(pe, "hy_filter")
    hy_taps_tensor(k, pe)
    k.after(pe, "hy_taps")
    hy_forward_tensor(k, pe)
    k.after(pe, "hy_forward")
    hy_inverse_tensor(k, pe)
    k.after(pe, "mix_o_split")
    dense_tensor(k, pe, "w_out_o", DT, k.h_hi, k.mix_lo, (S,), k.sem("mix_o_evac"))
    k.after(pe, "mix_o_out")
    norm_tensor(k, pe, "mod_f1", S)
    ffn_tensor(Ffn(k, "w_ffn3", 1, S), pe, norm_lo("mod_f1"))


def scalar_program(k, act):
    s = Serial(act, k.sem("scalar_own"))
    end = lambda stage: stage_end(k, act, k.scalar_stages, stage)
    m1 = k.view(k.big, 0, DT, S)
    load_distance_tables(k, act)
    start_scalar(k, s)
    split_ahead(k, s, SPLITS)
    end("start")
    plain_norm_scalar(k, s, "norm1")
    end("norm1")
    dil_project_scalar(k, s)
    end("dil_project")
    Attention(k, 0, 0, dil_items(k)).scalar(s)
    split_ahead(k, s, VFIRST["w_gdn"] + SPLITS)
    end("dil_attend")
    gdn_project_scalar(k, s)
    end("gdn_project")
    gdn_gates_scalar(k, s)
    end("gdn_gates")
    gdn_norm(k).scalar(s)
    end("gdn_norm_qk")
    gdn_masks_scalar(k, s)
    end("gdn_masks")
    end("gdn_products")
    gdn_invert_scalar(k, s)
    end("gdn_invert")
    gdn_apply_scalar(k, s)
    end("gdn_apply")
    split_ahead(k, s, VFIRST["w_out1"] + SPLITS)
    end("gdn_scan")
    gdn_out_scalar(k, s)
    end("gdn_out")
    mix_split_scalar(k, s, "mix1", S)
    end("mix1_split")
    split_along(k, s, "w_out1", DT, SPLITS)
    end("mix1_out")
    norm_scalar(k, s, "mix1_post", m1, S)
    end("mix1_post")
    plain_norm_scalar(k, s, "norm2")
    end("norm2")
    f1 = ffn1(k)
    ffn_scalar(f1, s)
    end("ffn1")
    norm_scalar(k, s, "ffn1_post", f1.total, S)
    end("ffn1_post")
    modulate_scalar(k, s, "mod_a0", 0, 0, T)
    end("mod_a0")
    q, key, _ = attn_views(k)
    copy_out_scalar(k, s, "w_diff_qk", 8, lambda j: (q if j < 4 else key)[:, j % 4, :], lambda j: T,
                    k.sem("diff_project_evac"))
    split_along(k, s, "w_diff_v", 4, SPLITS)
    end("diff_project")
    diff_norm(k).scalar(s)
    end("diff_norm")
    Attention(k, 32, 32, diff_items(k)).scalar(s)
    end("diff_attend")
    subln(k).scalar(s)
    end("diff_subln")
    copy_out_scalar(k, s, "w_na_qk", 8, lambda j: (q if j < 4 else key)[:, j % 4, :], lambda j: T, k.sem("na_project_evac"))
    split_along(k, s, "w_na_v", 4, 0)
    end("na_project")
    load_na_bias(k, act)
    na_norm(k).scalar(s)
    end("na_norm")
    Attention(k, 80, 56, na_items(k)).scalar(s)
    split_ahead(k, s, VFIRST["w_out_e"] + SPLITS)
    end("na_attend")
    mix_split_scalar(k, s, "mix_e", T)
    end("mix_e_split")
    split_along(k, s, "w_out_e", DT, SPLITS)
    end("mix_e_out")
    modulate_scalar(k, s, "mod_f0", 0, 24, T)
    end("mod_f0")
    ffn_scalar(Ffn(k, "w_ffn2", 0, T), s)
    end("ffn2")
    modulate_scalar(k, s, "mod_a1", 1, 0, T)
    end("mod_a1")
    gq, gk, _ = gqa_views(k)
    copy_out_scalar(k, s, "w_gqa_qk", 5, lambda j: gq[:, j, :] if j < 4 else gk[:, 0, :], lambda j: T,
                    k.sem("gqa_project_evac"))
    split_along(k, s, "w_gqa_v", 1, SPLITS)
    end("gqa_project")
    gqa_norm(k).scalar(s)
    end("gqa_norm")
    Attention(k, 128, 104, gqa_items(k)).scalar(s)
    end("gqa_attend")
    hy_project_scalar(k, s)
    end("hy_project")
    load_hyena(k, act)
    hy_filter_scalar(k, s)
    end("hy_filter")
    end("hy_taps")
    hy_forward_scalar(k, s)
    end("hy_forward")
    load_hyena_inverse(k, act)
    end("hy_inverse")
    mix_split_scalar(k, s, "mix_o", S)
    end("mix_o_split")
    split_along(k, s, "w_out_o", DT, SPLITS)
    end("mix_o_out")
    modulate_scalar(k, s, "mod_f1", 1, 24, S)
    end("mod_f1")
    ffn_scalar(Ffn(k, "w_ffn3", 1, S), s)
    end("ffn3")


def vector_program(k, dve):
    v = Serial(dve, k.sem("vector_own"))
    end = lambda stage: stage_end(k, dve, k.vector_stages, stage)
    m1 = k.view(k.big, 0, DT, S)
    start_vector(k, v)
    end("start")
    plain_norm_vector(k, v, "norm1", "g_mix_pre", k.lo1)
    end("norm1")
    dil_project_vector(k, v)
    end("dil_project")
    Attention(k, 0, 0, dil_items(k)).vector(v)
    ada_vector(k, v, "w_ada0_a", 0, 5, 0, 32)
    end("dil_attend")
    gdn_project_vector(k, v)
    end("gdn_project")
    gdn_gates_vector(k, v)
    end("gdn_gates")
    gdn_norm(k).vector(v)
    end("gdn_norm_qk")
    gdn_masks_vector(k, v)
    end("gdn_masks")
    gdn_products_vector(k, v)
    end("gdn_products")
    gdn_invert_vector(k, v)
    end("gdn_invert")
    gdn_apply_vector(k, v)
    end("gdn_apply")
    gdn_scan_vector(k, v)
    ada_vector(k, v, "w_ada0_b", 0, 6, 32, 16)
    end("gdn_scan")
    gdn_out_vector(k, v)
    end("gdn_out")
    mix_split_vector(k, v, "mix1", S)
    end("mix1_split")
    mix1_out_vector(k, v)
    end("mix1_out")
    post_norm_vector(k, v, "mix1_post", m1, "g_mix_post")
    end("mix1_post")
    plain_norm_vector(k, v, "norm2", "g_ffn_pre", k.lo3)
    end("norm2")
    f1 = ffn1(k)
    ffn_vector(f1, v)
    end("ffn1")
    post_norm_vector(k, v, "ffn1_post", f1.total, "g_ffn_post")
    end("ffn1_post")
    modulate_vector(k, v, "mod_a0", 0, 8, k.lo2, T)
    end("mod_a0")
    values_vector(k, v, "w_diff_v", 4, attn_views(k)[2], HALF, 6)
    end("diff_project")
    diff_norm(k).vector(v)
    end("diff_norm")
    Attention(k, 32, 32, diff_items(k)).vector(v)
    end("diff_attend")
    subln(k).vector(v)
    end("diff_subln")
    values_vector(k, v, "w_na_v", 4, attn_views(k)[2], HALF, 6)
    end("na_project")
    na_norm(k).vector(v)
    end("na_norm")
    Attention(k, 80, 56, na_items(k)).vector(v)
    ada_vector(k, v, "w_ada1", 1, 5, 0, 48)
    end("na_attend")
    mix_split_vector(k, v, "mix_e", T)
    end("mix_e_split")
    residual_vector(k, v, "w_out_e", 0, T, k.sem("mix_e_evac"))
    end("mix_e_out")
    modulate_vector(k, v, "mod_f0", 0, 32, k.lo3, T)
    end("mod_f0")
    ffn_vector(Ffn(k, "w_ffn2", 0, T), v)
    end("ffn2")
    modulate_vector(k, v, "mod_a1", 1, 8, k.lo2, T)
    end("mod_a1")
    values_vector(k, v, "w_gqa_v", 1, gqa_views(k)[2], P, 6)
    end("gqa_project")
    gqa_norm(k).vector(v)
    end("gqa_norm")
    Attention(k, 128, 104, gqa_items(k)).vector(v)
    end("gqa_attend")
    hy_project_vector(k, v)
    end("hy_project")
    hy_filter_vector(k, v)
    end("hy_filter")
    hy_taps_vector(k, v)
    end("hy_taps")
    hy_forward_vector(k, v)
    end("hy_forward")
    hy_inverse_vector(k, v)
    end("hy_inverse")
    mix_split_vector(k, v, "mix_o", S)
    end("mix_o_split")
    residual_vector(k, v, "w_out_o", 1, S, k.sem("mix_o_evac"))
    end("mix_o_out")
    modulate_vector(k, v, "mod_f1", 1, 32, k.lo3, S)
    end("mod_f1")
    ffn_vector(Ffn(k, "w_ffn3", 1, S), v)
    end("ffn3")


def build(nc, dram):
    with ExitStack() as ctx:
        k = Core(nc, ctx, dram)
        block = ctx.enter_context(nc.Block())

        @block.sync
        def _(sp):
            sync_program(k, sp)

        @block.gpsimd
        def _(pool):
            gpsimd_program(k, pool)

        @block.tensor
        def _(pe):
            tensor_program(k, pe)

        @block.scalar
        def _(act):
            scalar_program(k, act)

        @block.vector
        def _(dve):
            vector_program(k, dve)



def constants():
    f = np.float32
    out = {name: np.zeros((P, n), f) for name, n in CONSTS}
    i, j = np.arange(P)[:, None], np.arange(P)[None, :]
    same = i // CHUNK == j // CHUNK
    out["ident"][:] = i == j
    out["ones"][:] = 1
    out["ones_d"][:] = 1 / D
    out["heads64"][:] = (i // HD == j // HD) / HD
    out["heads128"][:] = 1 / P
    out["flip"][:] = i == P - 1 - j
    out["rope_swap"][:] = np.where((i == j + 1) & (j % 2 == 0), -1, 0) + np.where((i == j - 1) & (j % 2 == 1), 1, 0)
    out["later"][:] = same & (i > j)
    out["upto"][:] = same & (i <= j)
    for lev in range(LEVELS):
        s = 1 << lev
        out["levels"][:, lev * P:(lev + 1) * P] = (i // (2 * s) == j // (2 * s)) & (i // s + 1 == j // s)
    cq, ck = np.arange(P)[:, None] % GRID_W, np.arange(S)[None, :] % GRID_W
    first = np.clip(cq - WIN_C // 2, 0, GRID_W - WIN_C)
    out["na_mask"][:] = np.where((ck >= first) & (ck < first + WIN_C), 0, MASKED)
    t = np.arange(S)
    pairs = HD // 4
    inv = f(10000.0) ** (-np.arange(pairs, dtype=f) / f(pairs))
    ang = np.concatenate([(t // GRID_W).astype(f)[:, None] * inv, (t % GRID_W).astype(f)[:, None] * inv], axis=1)
    which = (np.arange(P) % HD) // 2
    out["cos"][:] = np.cos(ang)[:, which].T
    out["sin"][:] = np.sin(ang)[:, which].T
    return np.concatenate([out[name] for name, _ in CONSTS], axis=1)


def distance_tables():
    f = np.float32
    d = S - 1 - np.arange(LINE)
    far = np.maximum(d, 1).astype(f)
    log_b = 16 + (np.log(far / f(16)) / f(np.log(2048 / 16)) * f(16)).astype(np.int32)
    bucket = np.where(d < 16, np.maximum(d, 0), np.minimum(log_b, BUCKETS - 1))
    hot = (np.arange(BUCKETS)[:, None] == bucket[None, :]).astype(f)
    count = (d <= 128).astype(int) + (d % 4 == 0) + (d % 16 == 0)
    logs = np.where((d >= 0) & (count > 0), np.log(np.maximum(count, 1)), MASKED)
    return hot, logs.astype(f)[None, :]


def hyena_tables():
    f = np.float32
    t = np.linspace(0.0, 1.0, S, dtype=f)[:, None]
    bands = (EMB - 1) // 2
    w = f(2.0 * np.pi) * np.arange(S, dtype=f)[:, None] / f(S)
    freq = np.linspace(1e-4, bands - 1, bands, dtype=f)[None, :]
    feats = np.concatenate([t, np.cos(freq * w), -np.sin(freq * w)], axis=1).T
    deltas = np.linspace(np.log(1e-2) / 1.5, np.log(1e-2) / 0.3, HALF, dtype=f)
    decay = np.exp(-t * np.abs(deltas))
    angle = np.pi / (2 * S) * ((2 * np.arange(S)[None, :] + 1) * np.arange(S)[:, None] % (4 * S))
    tiles = lambda a: np.ascontiguousarray(a.reshape(4, P, -1).transpose(1, 0, 2).astype(f))
    return {"feats": np.ascontiguousarray(feats.astype(f)), "decay": tiles(decay),
            "dft_cos": tiles(np.cos(angle)), "dft_sin": tiles(np.sin(angle)),
            "idft_cos": tiles(np.cos(angle).T / S), "idft_sin": tiles(np.sin(angle).T / S)}



def by_output(w, blocks=DT):
    kt, nt = w.shape[0] // P, w.shape[1] // P
    a = w.reshape(kt // blocks, blocks, P, nt, P).transpose(3, 0, 2, 1, 4)
    return np.ascontiguousarray(a.reshape(nt * (kt // blocks), P, blocks * P))


def by_input(w):
    n = w.shape[1]
    per = 1024 // n
    return np.ascontiguousarray(w.reshape(DT // per, per, P, n).transpose(0, 2, 1, 3).reshape(DT // per, P, per * n))


def alternate(a, b):
    a, b = by_output(a), by_output(b)
    return np.stack([a, b], axis=1).reshape(2 * len(a), P, D)


def by_chunk(gate, up, down):
    first, out = alternate(gate, up), []
    for m0, nm in CHUNKS:
        out.append(first[2 * m0:2 * (m0 + nm)])
        rows = np.zeros((DT, P, D), np.float32)
        rows[:, :, 0:nm * P] = by_output(down[m0 * P:(m0 + nm) * P], nm)
        out.append(rows)
    return np.concatenate(out)


def cols(vec):
    return np.asarray(vec).reshape(-1, P).T


def padded(a):
    a = np.asarray(a, np.float32)
    out = np.zeros((P, a.shape[1]), np.float32)
    out[:a.shape[0]] = a
    return out


def layout(i):
    g = {name: np.asarray(a) for name, a in i.items()}
    W = g["w_in"][0]
    o = {}
    gw = GH * P
    q0 = 4 * gw + 2 * GH
    o["w_dil_qk"] = by_output(W[:, q0:q0 + 2 * HALF])
    o["w_dil_v"] = by_input(W[:, q0 + 2 * HALF:q0 + 3 * HALF])
    o["w_gdn"] = by_output(W[:, 0:4 * gw])
    o["w_gdn_gates"] = np.zeros((1, P, D), np.float32)
    o["w_gdn_gates"][0, :, 0:8 * DT] = W[:, 4 * gw:q0].reshape(DT, P, 2 * GH).transpose(1, 0, 2).reshape(P, 8 * DT)
    o["w_out1"] = by_output(g["w_out"][0])
    o["w_ffn1"] = by_chunk(g["w_gate"][0], g["w_up"][0], g["w_down"][0])
    for l in range(2):
        up = g["w_up_2"][l]
        o[f"w_ffn{l + 2}"] = by_chunk(up[:, 0:F], up[:, F:], g["w_down_2"][l])
    ada = by_output(g["w_ada_2"][0])
    o["w_ada0_a"], o["w_ada0_b"], o["w_ada1"] = ada[:32], ada[32:], by_output(g["w_ada_2"][1])
    E = g["w_in_e_2"][0]
    o["w_na_qk"], o["w_na_v"] = by_output(E[:, 0:1024]), by_input(E[:, 1024:1536])
    o["w_diff_qk"], o["w_diff_v"] = by_output(E[:, 1536:2560]), by_input(E[:, 2560:3072])
    o["w_out_e"] = by_output(g["w_out_e_2"][0])
    O = g["w_in_o_2"][0]
    order = [t + 4 * e for t in range(4) for e in range(2)]
    q = O[:, 0:HALF].reshape(D, 8, HD)[:, order].reshape(D, HALF)
    o["w_gqa_qk"] = by_output(np.concatenate([q, O[:, HALF:HALF + P]], axis=1))
    o["w_gqa_v"] = by_input(O[:, HALF + P:HALF + 2 * P])
    o["w_hy"] = by_output(O[:, HALF + 2 * P:])
    wo = g["w_out_o_2"][0]
    o["w_out_o"] = by_output(np.concatenate([wo[0:HALF].reshape(8, HD, D)[order].reshape(HALF, D), wo[HALF:]]))

    o["x"] = np.ascontiguousarray(g["x"][0].T.reshape(DT, P, S).transpose(1, 0, 2))
    o["ctx"] = np.ascontiguousarray(g["ctx_2"][0].T.reshape(DT, P, CTX).transpose(1, 0, 2))
    taps = lambda w: np.stack([cols(r) for r in w], axis=2).reshape(P, -1)
    twice = lambda v: np.concatenate([v, v]).reshape(P, 1)
    both = lambda v: np.repeat(cols(v), 2, axis=1)
    p = {
        "g_mix_pre": cols(g["g_mix_pre"]), "g_mix_post": cols(g["g_mix_post"]),
        "g_ffn_pre": cols(g["g_ffn_pre"]), "g_ffn_post": cols(g["g_ffn_post"]),
        "conv_w": taps(g["conv_w"][0]), "a_log": padded(g["a_log"].T), "dt_bias": padded(g["dt_bias"].T),
        "onorm": cols(g["onorm_g"]), "na_q": twice(g["na_q_gain_2"][0]), "na_k": twice(g["na_k_gain_2"][0]),
        "da_q": twice(g["da_q_gain_2"][0]), "da_k": twice(g["da_k_gain_2"][0]), "subln": cols(g["da_subln_gain_2"]),
        "gqa_q": twice(g["gqa_q_gain_2"][0]), "gqa_k": twice(g["gqa_k_gain_2"][0]),
        "lambdas": padded(np.stack([g[f"da_lambda_{n}_2"][0] for n in ("q1", "q2", "k1", "k2")], axis=1)),
        "cond": np.stack([cols(g["c_2"]), cols(g["c_ctx_2"])], axis=2).reshape(P, 16),
        "b_ada0": both(g["b_ada_2"][0]), "b_ada1": both(g["b_ada_2"][1]),
        "ffn_w0": taps(g["ffn_conv_w_2"][0]), "ffn_w1": taps(g["ffn_conv_w_2"][1]),
        "ffn_b0": cols(g["ffn_conv_b_2"][0]), "ffn_b1": cols(g["ffn_conv_b_2"][1]),
        "hy_conv_w": taps(g["hy_conv_w_2"][0]), "hy_conv_b": cols(g["hy_conv_b_2"]),
        "hy_b": padded(np.stack([g[f"hy_b{n}_2"][0] for n in (1, 2, 3)], axis=1)), "hy_freq": padded(g["hy_freq_2"].T),
        "hy_skip": cols(g["hy_skip_2"]), "hy_first": (np.arange(P) > 0).astype(np.float32)[:, None],
        "eps": np.full((P, 1), EPS, np.float32), "one": np.ones((P, 1), np.float32),
    }
    o["params"] = np.concatenate([p[name].reshape(P, n) for name, n in PARAMS], axis=1)
    o["rel_bias"] = g["rel_bias"]
    o["rpb"] = np.pad(g["na_rpb_2"][0], ((0, 0), (0, 0), (GRID_W - WIN_C, GRID_W - WIN_C)))
    for n in (1, 2, 3, 4):
        o[f"hy_w{n}"] = g[f"hy_w{n}_2"][0]
    o["consts"] = constants()
    o["buckets"], o["log_counts"] = distance_tables()
    o.update(hyena_tables())
    return {name: np.ascontiguousarray(a) for name, a in o.items()}


def kernel(**inputs):
    import concourse.bacc as bacc
    from concourse.bass_utils import run_bass_kernel_spmd

    nc = bacc.Bacc("TRN2", target_bir_lowering=False, num_devices=1)
    arrays, dram = {}, {}
    for name, a in layout(inputs).items():
        arrays[f"in_{name}"] = a
        handle = nc.dram_tensor(f"in_{name}", a.shape, F32, kind="ExternalInput")
        dram[name] = handle if name == "rpb" else handle.ap()
    dram["lines"] = nc.dram_tensor("bias_lines", (8, LINE), F32)
    dram["out"] = nc.dram_tensor("out_0", (P, DT, S), F32, kind="ExternalOutput").ap()
    build(nc, dram)
    r = run_bass_kernel_spmd(nc, [arrays], core_ids=[0])
    got = r.results[0]["out_0"]
    return np.ascontiguousarray(np.asarray(got).transpose(2, 1, 0).reshape(1, S, D))
```

```python
import concourse.bass as bass
import numpy as np
from concourse import mybir
from concourse.alu_op_type import AluOpType as ALU
from contextlib import ExitStack

F32 = mybir.dt.float32
R32 = mybir.dt.float32r
ACT = mybir.ActivationFunctionType
AX = mybir.AxisListType

P = 128
D = 1024
DT = D // P
S = 512
CTX = 256
T = S + CTX
F = 2816
FT = F // P
HALF = D // 2
HT = HALF // P
HD = 64
CHUNK = 64
PAIRS = S // P
GH = 4
GRID_W = 64
WIN_R, WIN_C = 8, 16
EMB, ORDER = 33, 64
BUCKETS = 32
MASKED = -1.0e30
EPS = 1e-6
ROUND = 1.5 * 2.0 ** 23
TWO_PI_HI = 6.28125
TWO_PI_LO = 2.0 * np.pi - TWO_PI_HI
PI_IN = 3.1415925
SUBLN = 1 / 0.8 ** 2
LAM_INIT = 0.2

SLOTS = 4
SPLITS = 2
CHUNKS = ((0, 6), (6, 8), (14, 8))
FFN_UNITS = 2 * FT + DT * len(CHUNKS)
LINE = 640

PARAMS = [
    ("g_mix_pre", 8), ("g_mix_post", 8), ("g_ffn_pre", 8), ("g_ffn_post", 8), ("conv_w", 48),
    ("a_log", 1), ("dt_bias", 1), ("onorm", 1),
    ("na_q", 1), ("na_k", 1), ("da_q", 1), ("da_k", 1), ("subln", 1), ("gqa_q", 1), ("gqa_k", 1),
    ("lambdas", 4), ("b_ada0", 96), ("b_ada1", 96),
    ("ffn_w0", 66), ("ffn_w1", 66), ("ffn_b0", 22), ("ffn_b1", 22),
    ("hy_conv_w", 36), ("hy_conv_b", 12), ("hy_b", 3), ("hy_freq", 1), ("hy_skip", 4), ("hy_first", 1), ("eps", 1), ("eps_query", 1), ("eps_subln", 1), ("eps_delta", 1), ("one", 1),
]
COL = {}
_at = 0
for _name, _n in PARAMS:
    COL[_name] = (_at, _n)
    _at += _n
NPARAM = _at

CONSTS = [("levels", 7 * P), ("ident", P), ("ones", P), ("ones_d", P), ("heads64", P), ("heads128", P), ("flip", P), ("rope_swap", P),
          ("later", P), ("upto", P), ("na_mask", GRID_W), ("cos", S), ("sin", S)]
CCOL = {}
_at = 0
for _name, _n in CONSTS:
    CCOL[_name] = (_at, _n)
    _at += _n
NCONST = _at

STAGES = [
    "start", "norm1", "dil_project", "dil_attend", "gdn_project", "gdn_masks",
    "gdn_products", "gdn_invert", "gdn_apply", "gdn_scan", "gdn_out", "mix1_split", "mix1_out", "mix1_post", "norm2",
    "ffn1", "ffn1_post",
    "mod_a0", "diff_project", "diff_attend", "na_project", "na_attend",
    "mix_e_split", "mix_e_out", "mod_f0", "ffn2",
    "mod_a1", "gqa_project", "gqa_attend", "hy_project", "hy_filter", "hy_taps", "hy_forward",
    "hy_inverse", "mix_o_split", "mix_o_out", "mod_f1", "ffn3", "end",
]

STREAM = [
    ("w_dil_qk", 8), ("w_dil_v", 4), ("w_gdn_gates", 1), ("w_gdn", 16), ("w_out1", 8), ("w_ffn1", FFN_UNITS),
    ("w_diff_qk", 8), ("w_diff_v", 4), ("w_na_qk", 8), ("w_na_v", 4), ("w_out_e", 8), ("w_ffn2", FFN_UNITS),
    ("w_gqa_qk", 5), ("w_gqa_v", 1), ("w_hy", 12), ("w_out_o", 8), ("w_ffn3", FFN_UNITS),
]
FIRST = {}
UNITS = 0
for _name, _n in STREAM:
    FIRST[_name] = UNITS
    UNITS += _n
ADA = 6 * DT


class Serial:

    def __init__(self, eng, own):
        self.eng, self.own, self.n, self.at, self.per = eng, own, 0, None, 0
        self.counts = {}

    def enter(self, at, per):
        self.at, self.per, self.begin = at, per, self.n

    def leave(self, passes):
        assert self.n == self.begin + self.per
        self.n = self.begin + passes * self.per
        self.at = None


def link(e, ins):
    e.n += 1
    ins.then_inc(e.own, 1)
    e.eng.wait_ge(e.own, e.n if e.at is None else e.at * e.per + (e.n - e.per))


class Core:

    def __init__(self, nc, ctx, dram):
        self.nc, self.ctx, self.dram = nc, ctx, dram
        self.at = nc.sbuf_base + (-nc.sbuf_base) % 32
        self.x = self.place("x_res", DT * T).rearrange("p (t n) -> p t n", t=DT)
        h_at = self.at
        self.h_hi = self.place("act_hi", DT * T, R32).rearrange("p (t n) -> p t n", t=DT)
        self.h_flat = self.over(h_at, "act_place", DT * T)
        mix_at = self.at
        self.mix_flat = self.place("mix", DT * T)
        self.mix = self.mix_flat.rearrange("p (t n) -> p t n", t=DT)
        self.mix_lo = self.over(mix_at, "mix_lo", DT * T, R32).rearrange("p (t n) -> p t n", t=DT)
        big_at = self.at
        self.big = self.place("big", 16384)
        self.lo1 = self.over(big_at + 4 * 12288, "act_lo_first", DT * S, R32).rearrange("p (t n) -> p t n", t=DT)
        self.lo2 = self.over(big_at + 4 * 9216, "act_lo_mixer", DT * T, R32).rearrange("p (t n) -> p t n", t=DT)
        self.lo3 = self.over(mix_at, "act_lo_ffn", DT * T, R32).rearrange("p (t n) -> p t n", t=DT)
        self.hid_hi = self.over(big_at, "hidden_hi", 8 * T, R32).rearrange("p (t n) -> p t n", t=8)
        self.hid_lo = self.over(big_at + 4 * 8 * T, "hidden_lo", 8 * T, R32).rearrange("p (t n) -> p t n", t=8)
        self.ring = self.place("ring", SLOTS * D).rearrange("p (s n) -> p s n", s=SLOTS)
        self.w_hi = self.place("w_hi", SPLITS * D, R32).rearrange("p (s n) -> p s n", s=SPLITS)
        self.w_lo = self.place("w_lo", SPLITS * D, R32).rearrange("p (s n) -> p s n", s=SPLITS)
        self.probs = self.place("probs", 2 * T).rearrange("p (s n) -> p s n", s=2)
        self.params = self.place("params", NPARAM)
        self.eps = self.par("eps")
        ada_at = self.at
        self.sq = self.place("sq", 2 * T).rearrange("p (s n) -> p s n", s=2)
        self.rstd = self.place("rstd", T)
        self.probs_t = self.place("probs_t", T)
        levels_at = max(self.at, ada_at + 4 * (5 * D - CCOL["levels"][1]))
        self.at = levels_at + (-levels_at) % 32
        self.turns = [self.probs[:, 0, :], self.probs[:, 1, :],
                      self.over(levels_at - 4 * T - (-4 * T) % 32, "probs_third", T)]
        self.ada = self.over(ada_at, "ada_place", 5 * D).rearrange("p (s n) -> p s n", s=5)
        self.consts = self.place("consts", NCONST)
        self.mod_flat = self.place("mod", 2 * 96)
        self.mod = self.mod_flat.rearrange("p (l n s) -> p l n s", l=2, s=2)
        self.small = self.place("small", 128)
        self.ps = ctx.enter_context(nc.psum_tensor("ps", [P, 8 * 512], F32))
        self.sems = {}
        self.sem = self._sem
        self.slot_landed = [self.sem(f"slot_landed_{i}") for i in range(SLOTS)]
        self.unit_done = self.sem("unit_done")
        self.hi_done = self.sem("hi_done")
        self.lo_done = self.sem("lo_done")
        self.ada_rows, self.ada_rows_ready = self.sem("ada_rows"), self.sem("ada_rows_ready")
        self.ada_landed = [self.sem(f"ada_landed_{i}") for i in range(2)]
        self.ada_used = self.sem("ada_used")
        self.u_next = 0
        self.loaded = self.sem("loaded")
        self.loaded_late = self.sem("loaded_late")
        self.vector_stages = self.sem("vector_stages")
        self.scalar_stages = self.sem("scalar_stages")

    def over(self, at, name, cols, dtype=F32):
        return self.nc.alloc_sbuf_tensor_at(name, [P, cols], dtype, offset=at)[:, :]

    def place(self, name, cols, dtype=F32):
        ap = self.over(self.at, name, cols, dtype)
        self.at += 4 * cols + (-4 * cols) % 32
        return ap

    def _sem(self, name):
        if name not in self.sems:
            self.sems[name] = self.ctx.enter_context(self.nc.semaphore(name))
        return self.sems[name]

    def bank(self, b, n=512, off=0):
        return self.ps[:, b * 512 + off:b * 512 + off + n]

    def view(self, buf, off, *shape):
        n = int(np.prod(shape))
        ap = buf[:, off:off + n]
        if len(shape) == 2:
            ap = ap.rearrange("p (a b) -> p a b", a=shape[0])
        if len(shape) == 3:
            ap = ap.rearrange("p (a b c) -> p a b c", a=shape[0], b=shape[1])
        return ap

    def par(self, name, i=0, n=1):
        return self.params[:, COL[name][0] + i:COL[name][0] + i + n]

    def const(self, name, i=0, n=None):
        return self.consts[:, CCOL[name][0] + i:CCOL[name][0] + i + (n or P)]

    def after(self, eng, stage):
        eng.wait_ge(self.vector_stages, STAGES.index(stage) + 1)
        eng.wait_ge(self.scalar_stages, STAGES.index(stage) + 1)

    def slot_ready(self, eng, u, loop=None):
        more = 0 if loop is None else loop[0] * (16 * loop[1] // SLOTS)
        eng.wait_ge(self.slot_landed[u % SLOTS], more + 16 * (u // SLOTS + 1))



def stage_end(k, eng, sem, stage):
    eng.sem_inc(sem, 1)
    k.after(eng, stage)


def split_ahead(k, s, upto):
    upto = min(upto, UNITS)
    for u in range(k.u_next, upto):
        k.slot_ready(s.eng, u)
        if u >= SPLITS:
            s.eng.wait_ge(k.unit_done, u - SPLITS + 1)
        s.eng.copy(k.w_hi[:, u % SPLITS, :], k.ring[:, u % SLOTS, :]).then_inc(k.hi_done, 1)
    k.u_next = max(k.u_next, upto)


def products(pe, out, w, x, start, stop):
    pe.matmul(out, w[0], x[0], start=start, stop=False)
    pe.matmul(out, w[0], x[1], start=False, stop=False)
    return pe.matmul(out, w[1], x[0], start=False, stop=stop)


def unit_products(k, pe, buf, slot, hi, lo, blocks, widths, ready=None):
    for b in range(blocks):
        if ready is not None:
            pe.wait_ge(ready[0], ready[1] + b + 1)
        w = (k.w_hi[:, slot, b * P:(b + 1) * P], k.w_lo[:, slot, b * P:(b + 1) * P])
        col = 0
        for n in widths:
            last = products(pe, k.bank(2 * buf, n, col), w, (hi[:, b, col:col + n], lo[:, b, col:col + n]),
                            b == 0, b == blocks - 1)
            col += n
    last.then_inc(k.unit_done, 1)


def dense_tensor(k, pe, name, tiles, hi, lo, widths, evac, ready=None, nbuf=4, behind=None):
    v0 = FIRST[name]
    for j in range(tiles):
        if j >= nbuf:
            pe.wait_ge(evac, j - nbuf + 1)
        pe.wait_ge(k.lo_done, v0 + j + 1)
        unit_products(k, pe, j % nbuf, (v0 + j) % SPLITS, hi, lo, DT, widths, ready if j == 0 else None)
        if behind is not None:
            behind(j)


def values_unit(k, pe, name, lo, blocks, width, u):
    per = D // width
    slot = (FIRST[name] + u) % SPLITS
    pe.wait_ge(k.lo_done, FIRST[name] + u + 1)
    for b in range(blocks):
        for i in range(per):
            kt = u * per + i
            x = (k.h_hi[:, kt, b * P:(b + 1) * P], lo[:, kt, b * P:(b + 1) * P])
            w = (k.w_hi[:, slot, i * width:(i + 1) * width], k.w_lo[:, slot, i * width:(i + 1) * width])
            pe.matmul(k.bank(b, width), x[0], w[0], start=kt == 0, stop=False, skip_group_check=True)
            pe.matmul(k.bank(b, width), x[0], w[1], start=False, stop=False, skip_group_check=True)
            last = pe.matmul(k.bank(b, width), x[1], w[0], start=False, stop=kt == DT - 1, skip_group_check=True)
    last.then_inc(k.unit_done, 1)


NORMS = ["norm1", "mix1_post", "norm2", "ffn1_post", "mod_a0", "mod_f0", "mod_a1", "mod_f1"]


LOWERED = ["norm1", "norm2", "mod_a0", "mod_f0", "mod_a1", "mod_f1"]


def norms_before(name):
    return NORMS.index(name)


GATHERED = ["mix1_post", "ffn1_post", "mod_f0", "mod_a1", "mod_f1"]


def summed_before(name):
    return sum(1 if other in GATHERED else DT for other in NORMS[:norms_before(name)])


def gathered_before(name):
    return (DT - 1) * GATHERED.index(name)


def norm_square(k, s, name, t, src, n, sq=None):
    if name in GATHERED:
        buf = min(t, 1)
        if t >= 2:
            s.eng.wait_ge(k.sem("norm_gathered"), gathered_before(name) + t - 1)
    else:
        buf = t % 2
        if t >= 2:
            s.eng.wait_ge(k.sem("norm_summed"), summed_before(name) + t - 1)
    s.eng.activation((k.sq if sq is None else sq)[:, buf, 0:n], src[:, t, 0:n], ACT.Square).then_inc(k.sem("norm_squares"), 1)


def norm_gather(k, v, name, t, n, sq=None):
    sq = k.sq if sq is None else sq
    v.eng.wait_ge(k.sem("norm_squares"), DT * norms_before(name) + t + 1)
    v.eng.tensor_tensor(sq[:, 0, 0:n], sq[:, 0, 0:n], sq[:, 1, 0:n], ALU.add).then_inc(k.sem("norm_gathered"), 1)
    v.eng.wait_ge(k.sem("norm_gathered"), gathered_before(name) + t)


def norm_root(k, s, name, n):
    s.eng.wait_ge(k.sem("norm_summed"), summed_before(name) + (1 if name in GATHERED else DT))
    s.eng.activation(k.rstd[:, 0:n], k.ps[:, 6 * 512:6 * 512 + n], ACT.Sqrt, bias=k.eps).then_inc(k.sem("norm_rooted"), 1)


def norm_sum(k, pe, name, t, n, sq=None):
    sq = k.sq if sq is None else sq
    start, stop, buf = t in (0, None), t in (DT - 1, None), 0 if t is None else t % 2
    if start and norms_before(name):
        pe.wait_ge(k.sem("norm_rooted"), norms_before(name))
    if t is None:
        pe.wait_ge(k.sem("norm_gathered"), gathered_before(name) + DT - 1)
    else:
        pe.wait_ge(k.sem("norm_squares"), DT * norms_before(name) + t + 1)
    last = pe.matmul(k.bank(6), k.const("ones_d"), sq[:, buf, 0:S], start=start, stop=stop)
    if n > S:
        last = pe.matmul(k.bank(7, n - S), k.const("ones_d"), sq[:, buf, S:n], start=start, stop=stop)
    last.then_inc(k.sem("norm_summed"), 1)


def norm_tensor(k, pe, name, n):
    for t in range(DT):
        norm_sum(k, pe, name, t, n)


def along_scalar(k, s, weight, evac, name, src, n):
    for j in range(DT):
        split_ahead(k, s, FIRST[weight] + j + 1 + SPLITS)
        s.eng.wait_ge(evac, j + 1)
        norm_square(k, s, name, j, src, n)


def updated_scalar(k, s, name, before, n):
    for t in range(DT):
        s.eng.wait_ge(k.sem("x_updated"), before + t + 1)
        norm_square(k, s, name, t, k.x, n)


def norm_rstd(k, v, name, n):
    v.eng.wait_ge(k.sem("norm_rooted"), norms_before(name) + 1)
    link(v, v.eng.reciprocal(k.rstd[:, 0:n], k.rstd[:, 0:n]))


def modulate_vector(k, v, name, lo, n):
    norm_rstd(k, v, name, n)
    c0, bufs = DT * LOWERED.index(name), (k.sq[:, 0, 0:n], k.sq[:, 1, 0:n], k.probs[:, 0, 0:n])

    def lower(t):
        v.eng.wait_ge(k.sem("norm_hi"), c0 + t + 1)
        v.eng.tensor_tensor(lo[:, t, 0:n], bufs[t % 3], k.h_hi[:, t, 0:n].bitcast(F32), ALU.subtract)\
            .then_inc(k.sem("norm_lo"), 1)
        v.eng.wait_ge(k.sem("norm_lo"), c0 + t + 1)

    for t in range(DT):
        v.eng.tensor_tensor(bufs[t % 3], k.x[:, t, 0:n], k.rstd[:, 0:n], ALU.mult).then_inc(k.sem("norm_scaled"), 1)
        if t >= 2:
            lower(t - 2)
    lower(DT - 2)
    lower(DT - 1)


def modulate_scalar(k, s, name, layer, shift0, n):
    norm_root(k, s, name, n)
    c0, bufs = DT * LOWERED.index(name), (k.sq[:, 0, 0:n], k.sq[:, 1, 0:n], k.probs[:, 0, 0:n])
    for t in range(DT):
        s.eng.wait_ge(k.sem("norm_scaled"), c0 + t + 1)
        for q, (a, b) in enumerate(((0, S), (S, n))):
            if b > a:
                ins = s.eng.activation(bufs[t % 3][:, a:b], bufs[t % 3][:, a:b], ACT.Identity,
                                       bias=k.mod[:, layer, shift0 + t, q:q + 1], scale=k.mod[:, layer, shift0 + 8 + t, q:q + 1])
        link(s, ins)
        s.eng.copy(k.h_hi[:, t, 0:n], bufs[t % 3]).then_inc(k.sem("norm_hi"), 1)


class Projection:

    def __init__(self, k, name, tiles, values, units, width, dst, before, rotated_before, jobs):
        self.k, self.name, self.tiles, self.values, self.units = k, name, tiles, values, units
        self.width, self.dst, self.b, self.r, self.jobs = width, dst, before, rotated_before, jobs
        self.evac = k.sem(name + "_evac")
        self.squares, self.summed = k.sem("head_squares"), k.sem("head_summed")
        self.rooted, self.normed = k.sem("head_rooted"), k.sem("head_normed")
        self.swapped, self.rotated = k.sem("head_swapped"), k.sem("head_rotated")
        n, slots = tiles, [[] for _ in range(max(tiles + units, len(jobs)) + 3)]
        rotates = jobs[0][5]
        for i in range(1, n):
            if rotates and i >= 2:
                slots[i].append(("turn", i - 2, 4))
            slots[i].append(("norm", i - 1, None))
        if rotates:
            slots[n] += [("turn", n - 2, 6)]
            slots[n + 1] += [("norm", n - 1, None)]
            slots[n + 2] += [("turn", n - 1, 6)]
        else:
            for j in range(n - 1, len(jobs)):
                slots[j + 1].append(("norm", j, None))
        self.slots = slots

    def tensor(self, pe, lo, ready=None):
        k, n = self.k, self.tiles
        for i, events in enumerate(self.slots):
            if i < n:
                if i >= 2:
                    pe.wait_ge(self.evac, i - 1)
                u = FIRST[self.name] + i
                pe.wait_ge(k.lo_done, u + 1)
                size = self.jobs[i][0].shape[-1]
                unit_products(k, pe, i % 2, u % SPLITS, k.h_hi, lo, DT, (S, size - S) if size > S else (S,),
                              ready if i == 0 else None)
            elif i < n + self.units:
                if i == n:
                    pe.wait_ge(self.evac, n)
                    if self.jobs[0][5]:
                        pe.wait_ge(self.rotated, self.r + n - 2)
                values_unit(k, pe, self.values, lo, T // P, self.width, i - n)
            for what, j, bank in events:
                x, mean, _, _, _, _ = self.jobs[j]
                size = x.shape[-1]
                if what == "norm":
                    pe.wait_ge(self.squares, self.b + j + 1)
                    if j >= 1:
                        pe.wait_ge(self.rooted, self.b + j)
                    if j == n - 1 and self.jobs[0][5]:
                        pe.wait_ge(self.rotated, self.r + j)
                    last = pe.matmul(k.bank(6), mean, k.sq[:, j % 2, 0:S], start=True, stop=True)
                    if size > S:
                        last = pe.matmul(k.bank(7, size - S), mean, k.sq[:, j % 2, S:size], start=True, stop=True)
                    last.then_inc(self.summed, 1)
                else:
                    pe.wait_ge(self.normed, self.b + j + 1)
                    if j >= 1:
                        pe.wait_ge(self.rotated, self.r + j)
                    pe.matmul(k.bank(bank), k.const("rope_swap"), x[:, 0:S], start=True, stop=True).then_inc(self.swapped, 1)

    def scalar(self, s):
        k, n = self.k, self.tiles
        for i, events in enumerate(self.slots):
            if i < n:
                s.eng.wait_ge(k.unit_done, FIRST[self.name] + i + 1)
                split_ahead(k, s, FIRST[self.name] + i + 1 + SPLITS)
            elif i < n + self.units:
                split_ahead(k, s, FIRST[self.values] + i - n + 1 + SPLITS)
            if i < len(self.jobs):
                x = self.jobs[i][0]
                size = x.shape[-1]
                src = k.ps[:, 1024 * (i % 2):1024 * (i % 2) + size] if i < n else x
                if i >= 2:
                    s.eng.wait_ge(self.summed, self.b + i - 1)
                s.eng.activation(k.sq[:, i % 2, 0:size], src, ACT.Square).then_inc(self.squares, 1)
                if i < n:
                    s.eng.copy(x, src).then_inc(self.evac, 1)
            for what, j, _ in events:
                if what == "norm":
                    _, _, _, eps, factor, _ = self.jobs[j]
                    size = self.jobs[j][0].shape[-1]
                    s.eng.wait_ge(self.summed, self.b + j + 1)
                    if j >= 2:
                        s.eng.wait_ge(self.normed, self.b + j - 1)
                    s.eng.activation(k.probs[:, j % 2, 0:size], k.ps[:, 6 * 512:6 * 512 + size], ACT.Sqrt,
                                     bias=k.par(eps), scale=factor).then_inc(self.rooted, 1)
        s.eng.wait_ge(k.unit_done, FIRST[self.values] + self.units)
        for b in range(3, 6):
            link(s, s.eng.copy(self.dst[:, b, :], k.bank(b, self.width)))

    def vector(self, v):
        k, n = self.k, self.tiles
        for events in self.slots:
            for what, j, bank in events:
                x, _, gain, _, _, _ = self.jobs[j]
                size = x.shape[-1]
                if what == "norm":
                    v.eng.wait_ge(self.rooted, self.b + j + 1)
                    if j < n:
                        v.eng.wait_ge(self.evac, j + 1)
                    link(v, v.eng.reciprocal(k.rstd[:, 0:size], k.probs[:, j % 2, 0:size]))
                    v.eng.scalar_tensor_tensor(x, x, gain, k.rstd[:, 0:size], ALU.mult, ALU.mult).then_inc(self.normed, 1)
                    v.eng.wait_ge(self.normed, self.b + j + 1)
                else:
                    v.eng.wait_ge(self.swapped, self.r + j + 1)
                    link(v, v.eng.tensor_tensor(k.probs_t[:, 0:S], k.bank(bank), k.const("sin", 0, S), ALU.mult))
                    link(v, v.eng.tensor_tensor(x[:, 0:S], x[:, 0:S], k.const("cos", 0, S), ALU.mult))
                    v.eng.tensor_tensor(x[:, 0:S], x[:, 0:S], k.probs_t[:, 0:S], ALU.add).then_inc(self.rotated, 1)
                    v.eng.wait_ge(self.rotated, self.r + j + 1)
        v.eng.wait_ge(k.unit_done, FIRST[self.values] + self.units)
        for b in range(3):
            link(v, v.eng.tensor_copy(self.dst[:, b, :], k.bank(b, self.width)))


class Attention:

    def __init__(self, k, before, products_before, items):
        self.k, self.b, self.items = k, before, items
        self.scores, self.maxed, self.exps = k.sem("att_scores"), k.sem("att_maxed"), k.sem("att_exps")
        self.normed, self.turned, self.copied = k.sem("att_normed"), k.sem("att_turned"), k.sem("att_copied")
        self.summed, self.stored = k.sem("att_summed"), k.sem("att_stored")
        self.m, n = [], products_before
        for it in items:
            self.m.append(n)
            n += not it["open"]

    def tensor(self, pe, bias_loaded=None):
        k, N = self.k, len(self.items)
        for i in range(N + 3):
            if i < N:
                it = self.items[i]
                if it["bias"] and bias_loaded is not None:
                    pe.wait_ge(*bias_loaded)
                if i >= 2:
                    pe.wait_ge(self.exps, self.b + i - 1)
                base = 1024 * (i % 2)
                for kap, col in it["keys"]:
                    n = kap.shape[-1]
                    extra = [(a, b) for a, b, c in it["bias"] if c == col]
                    last = pe.matmul(k.ps[:, base + col:base + col + n], it["q"], kap, start=True, stop=not extra)
                    for e, (a, b) in enumerate(extra):
                        last = pe.matmul(k.ps[:, base + col:base + col + n], a, b, start=False, stop=e == len(extra) - 1)
                last.then_inc(self.scores, 1)
            if i >= 3 and not self.items[i - 3]["open"]:
                it, m = self.items[i - 3], self.m[i - 3]
                pe.wait_ge(self.copied, m + 1)
                if m >= self.m[0] + 2:
                    pe.wait_ge(self.stored, m - 1)
                for b, val in enumerate(it["values"]):
                    last = pe.matmul(k.bank(6 + m % 2, P), val, k.probs_t[:, b * P:(b + 1) * P], start=b == 0,
                                     stop=b == len(it["values"]) - 1)
                last.then_inc(self.summed, 1)
            if 2 <= i <= N + 1 and not self.items[i - 2]["open"]:
                it = self.items[i - 2]
                pe.wait_ge(self.normed, self.b + i - 1)
                if self.m[i - 2] >= self.m[0] + 1:
                    pe.wait_ge(self.copied, self.m[i - 2])
                for b in range(len(it["values"])):
                    last = pe.transpose(k.bank(4 + b // 4, P, (b % 4) * P), k.turns[(i - 2) % 3][:, b * P:(b + 1) * P],
                                        k.const("ident"))
                last.then_inc(self.turned, 1)

    def vector(self, v, between=None):
        k, N = self.k, len(self.items)
        for i in range(N + 3):
            if between is not None:
                between(i)
            if i < N:
                n = P * len(self.items[i]["values"])
                v.eng.wait_ge(self.scores, self.b + i + 1)
                v.eng.tensor_reduce(k.small[:, i % 4:i % 4 + 1], k.ps[:, 1024 * (i % 2):1024 * (i % 2) + n],
                                    AX.X, ALU.max, negate=True).then_inc(self.maxed, 1)
                v.eng.wait_ge(self.maxed, self.b + i + 1)
            if 1 <= i <= N:
                it = self.items[i - 1]
                j, n = (i - 1) % 4, P * len(it["values"])
                pr = k.turns[(i - 1) % 3][:, 0:n]
                v.eng.wait_ge(self.exps, self.b + i)
                link(v, v.eng.reciprocal(k.small[:, 8 + j:9 + j], k.small[:, 4 + j:5 + j]))
                if it["factor"] is not None:
                    link(v, v.eng.tensor_tensor(k.small[:, 8 + j:9 + j], k.small[:, 8 + j:9 + j], it["factor"], ALU.mult))
                if it["adds"]:
                    ins = v.eng.scalar_tensor_tensor(pr, pr, k.small[:, 8 + j:9 + j], k.turns[(i - 2) % 3][:, 0:n],
                                                     ALU.mult, ALU.add)
                else:
                    ins = v.eng.tensor_scalar(pr, pr, k.small[:, 8 + j:9 + j], None, ALU.mult)
                ins.then_inc(self.normed, 1)
                v.eng.wait_ge(self.normed, self.b + i)
            if i >= 3 and not self.items[i - 3]["open"]:
                it, m = self.items[i - 3], self.m[i - 3]
                v.eng.wait_ge(self.summed, m + 1)
                v.eng.tensor_copy(it["out"], k.bank(6 + m % 2, P)[it["rows"]]).then_inc(self.stored, 1)
                v.eng.wait_ge(self.stored, m + 1)

    def scalar(self, s):
        k, N = self.k, len(self.items)
        for i in range(N + 2):
            if i < N:
                n = P * len(self.items[i]["values"])
                s.eng.wait_ge(self.maxed, self.b + i + 1)
                if i >= 3:
                    if self.items[i - 3]["open"]:
                        s.eng.wait_ge(self.normed, self.b + i - 1)
                    else:
                        s.eng.wait_ge(self.turned, self.m[i - 3] + 1)
                s.eng.activation(k.turns[i % 3][:, 0:n], k.ps[:, 1024 * (i % 2):1024 * (i % 2) + n], ACT.Exp,
                                 bias=k.small[:, i % 4:i % 4 + 1],
                                 accum_out=k.small[:, 4 + i % 4:5 + i % 4]).then_inc(self.exps, 1)
            if i >= 2 and not self.items[i - 2]["open"]:
                n = P * len(self.items[i - 2]["values"])
                m = self.m[i - 2]
                s.eng.wait_ge(self.turned, m + 1)
                if m >= self.m[0] + 1:
                    s.eng.wait_ge(self.summed, m)
                s.eng.copy(k.probs_t[:, 0:n], k.ps[:, 2048:2048 + n]).then_inc(self.copied, 1)


def plain_norm_vector(k, v, name, gain, lo):
    norm_rstd(k, v, name, S)
    c0 = DT * LOWERED.index(name)

    def lower(t):
        v.eng.wait_ge(k.sem("norm_hi"), c0 + t + 1)
        v.eng.tensor_tensor(lo[:, t, 0:S], k.sq[:, t % 2, 0:S], k.h_hi[:, t, 0:S].bitcast(F32),
                            ALU.subtract).then_inc(k.sem("norm_lo"), 1)
        v.eng.wait_ge(k.sem("norm_lo"), c0 + t + 1)

    for t in range(DT):
        v.eng.scalar_tensor_tensor(k.sq[:, t % 2, 0:S], k.x[:, t, 0:S], k.par(gain, t), k.rstd[:, 0:S],
                                   ALU.mult, ALU.mult).then_inc(k.sem("norm_scaled"), 1)
        v.eng.wait_ge(k.sem("norm_scaled"), c0 + t + 1)
        if t >= 1:
            lower(t - 1)
    lower(DT - 1)


def plain_norm_scalar(k, s, name):
    norm_root(k, s, name, S)
    c0 = DT * LOWERED.index(name)
    for t in range(DT):
        s.eng.wait_ge(k.sem("norm_scaled"), c0 + t + 1)
        s.eng.copy(k.h_hi[:, t, 0:S], k.sq[:, t % 2, 0:S]).then_inc(k.sem("norm_hi"), 1)


MIXES = ["mix1", "mix_e", "mix_o"]


def mix_split_scalar(k, s, name, n):
    for t in range(DT):
        s.eng.copy(k.h_hi[:, t, 0:n], k.mix[:, t, 0:n]).then_inc(k.sem("mix_hi"), 1)


def mix_split_vector(k, v, name, n):
    c0 = DT * MIXES.index(name)
    for t in range(DT):
        v.eng.wait_ge(k.sem("mix_hi"), c0 + t + 1)
        v.eng.tensor_tensor(k.mix_lo[:, t, 0:n], k.mix[:, t, 0:n], k.h_hi[:, t, 0:n].bitcast(F32), ALU.subtract)\
            .then_inc(k.sem("mix_lower"), 1)


def split_along(k, s, name, units):
    split_ahead(k, s, FIRST[name] + units + SPLITS)


def post_norm_vector(k, v, name, m, gain):
    norm_rstd(k, v, name, S)
    for t in range(DT):
        link(v, v.eng.scalar_tensor_tensor(m[:, t, 0:S], m[:, t, 0:S], k.par(gain, t), k.rstd[:, 0:S],
                                          ALU.mult, ALU.mult))
        v.eng.tensor_tensor(k.x[:, t, 0:S], k.x[:, t, 0:S], m[:, t, 0:S], ALU.add).then_inc(k.sem("x_updated"), 1)


def copy_out_scalar(k, s, name, tiles, dst, width, evac, scale=None):
    for j in range(tiles):
        s.eng.wait_ge(k.unit_done, FIRST[name] + j + 1)
        split_ahead(k, s, FIRST[name] + j + 1 + SPLITS)
        w = width(j)
        src = k.ps[:, 1024 * (j % 4):1024 * (j % 4) + w]
        s.eng.activation(dst(j), src, ACT.Copy, scale=1.0 if scale is None else scale(j)).then_inc(evac, 1)
        s.eng.wait_ge(evac, j + 1)


def residual_vector(k, v, name, layer, n, evac, norm):
    parts = ((0, S), (S, n)) if n > S else ((0, S),)
    for j in range(DT):
        v.eng.wait_ge(k.unit_done, FIRST[name] + j + 1)
        for q, (a, b) in enumerate(parts):
            base = 1024 * (j % 3)
            ins = v.eng.scalar_tensor_tensor(k.x[:, j, a:b], k.ps[:, base + a:base + b], k.mod[:, layer, 16 + j, q:q + 1],
                                             k.x[:, j, a:b], ALU.mult, ALU.add)
            if q == len(parts) - 1:
                ins.then_inc(evac, 1)
                v.eng.wait_ge(evac, j + 1)
            else:
                link(v, ins)
        if j >= 2:
            norm_gather(k, v, norm, j - 1, n)
    norm_gather(k, v, norm, DT - 1, n)



class Ffn:

    def __init__(self, k, name, layer, n, ada, norm, total=None):
        self.k, self.name, self.layer, self.n, self.total = k, name, layer, n, total
        self.parts = ((0, S), (S, n)) if n > S else ((0, S),)
        self.u0, self.ada, self.norm = FIRST[name], ada, norm
        self.lin, self.act, self.taps = k.sem(name + "_lin"), k.sem(name + "_act"), k.sem(name + "_taps")
        self.hidden, self.upper, self.ready = k.sem(name + "_hidden"), k.sem(name + "_upper"), k.sem(name + "_ready")
        self.added = k.sem(name + "_added")
        if layer is not None:
            self.w, self.b = COL[f"ffn_w{layer}"][0], COL[f"ffn_b{layer}"][0]

    def off(self, c):
        return 2 * CHUNKS[c][0] + DT * c

    def step(self, c):
        return CHUNKS[c][0] + DT * c

    def ada_load(self, s, n, it=0):
        if self.ada is None or n >= ADA:
            return
        k, at = self.k, ADA * self.ada + n
        if at >= 2:
            s.eng.wait_ge(k.ada_used, it * 2 + (at - 1))
        s.eng.dma_start(k.ada[:, 2 + n % 2, :], k.dram[f"w_ada{self.ada}"][it * 2 + n]).then_inc(k.ada_landed[n % 2], 16)

    def ada_begin(self, s):
        if self.ada is None:
            return
        k = self.k
        s.eng.dma_start(k.ada[:, 0:2, :], bass.AP(k.dram["cond_rows"], 0, [[0, P], [D, 2], [1, D]])).then_inc(k.ada_rows, 16)
        self.ada_load(s, 0)
        self.ada_load(s, 1)
        s.eng.wait_ge(k.ada_rows, 16 * (self.ada + 1))
        s.eng.activation(k.ada[:, 0:2, :], k.ada[:, 0:2, :], ACT.Silu).then_inc(k.ada_rows_ready, 1)

    def ada_tile(self, v, n, it=0):
        if self.ada is None:
            return
        k, at = self.k, ADA * self.ada + n
        w = k.ada[:, 2 + n % 2, :]
        v.eng.wait_ge(k.ada_landed[n % 2], it * 16 + 16 * (at // 2 + 1))
        for q in range(2):
            ins = v.eng.scalar_tensor_tensor(k.ada[:, 4, :], w, 1.0, k.ada[:, q, :], ALU.mult, ALU.mult,
                                             accum_out=k.mod_flat[:, bass.ds(it * 4 + (2 * at + q), 1)])
            if q == 0:
                link(v, ins)
        ins.then_inc(k.ada_used, 1)
        v.eng.wait_ge(k.ada_used, it * 2 + (at + 1))

    def ada_end(self, v):
        if self.ada is None:
            return
        k, layer = self.k, self.ada
        mod = k.mod_flat[:, 2 * ADA * layer:2 * ADA * (layer + 1)]
        link(v, v.eng.tensor_tensor(mod, mod, k.par(f"b_ada{layer}", 0, 2 * ADA), ALU.add))
        for scale in (8, 32):
            part = k.mod[:, layer, scale:scale + DT, :]
            link(v, v.eng.tensor_scalar(part, part, 1.0, None, ALU.add))


def ffn1(k):
    return Ffn(k, "w_ffn1", None, S, 0, "ffn1_post", k.view(k.big, 12288, DT, S))


def ffn_tensor(f, pe, ready):
    k = f.k
    widths = tuple(b - a for a, b in f.parts)
    for c, (m0, nm) in enumerate(CHUNKS):
        off = f.off(c)

        def up(it, static):
            for s in range(4):
                if not static:
                    pe.wait_ge(f.hidden, it * 2 + (m0 + s // 2 - 1))
                elif c and s < 3:
                    pe.wait_ge(f.added, DT * c - (1, 0, 2)[s])
                pe.wait_ge(k.lo_done, it * 4 + (f.u0 + off + s + 1))
                unit_products(k, pe, s, (f.u0 + off + s) % SPLITS, k.h_hi, k.lo3, DT, widths,
                              ready if static and c == 0 and s == 0 else None)

        up(0, True)
        with pe.Fori(1, nm // 2) as it:
            up(it, False)
        for j in range(DT):
            if j < 3:
                pe.wait_ge(f.hidden, m0 + nm - 1 + j // 2)
            else:
                pe.wait_ge(f.added, DT * c + j - 2)
            v = f.u0 + off + 2 * nm + j
            pe.wait_ge(k.lo_done, v + 1)
            unit_products(k, pe, j % 3, v % SPLITS, k.hid_hi, k.hid_lo, nm, widths, (f.ready, m0) if j == 0 else None)
    if f.norm is not None:
        norm_sum(k, pe, f.norm, None, f.n, k.probs)


def ffn_scalar(f, s):
    k, n = f.k, f.n
    for c, (m0, nm) in enumerate(CHUNKS):
        u = f.u0 + f.off(c)

        def upper(it, j):
            s.eng.wait_ge(k.unit_done, it * 4 + (u + j + 1))
            k.slot_ready(s.eng, u + j + 2, (it, 4))
            s.eng.copy(k.w_hi[:, (u + j) % SPLITS, :], k.ring[:, (u + j + 2) % SLOTS, :]).then_inc(k.hi_done, 1)

        def up(it, static):
            for a in range(2):
                m = it * 2 + (m0 + a)
                g = 2048 * a
                tmp = k.probs[:, a, 0:n]
                upper(it, 2 * a)
                if static and c == 0 and a == 0:
                    f.ada_load(s, 2)
                if not (static and c == 0):
                    s.eng.wait_ge(f.ready, m - 1)
                if f.layer is None:
                    s.eng.activation(tmp, k.ps[:, g:g + n], ACT.Silu).then_inc(f.act, 1)
                else:
                    s.eng.activation(tmp, k.ps[:, g:g + n], ACT.Identity, bias=k.params[:, bass.ds(m + f.b, 1)],
                                     scale=k.params[:, bass.ds(m * 3 + (f.w + 1), 1)]).then_inc(f.lin, 1)
                    s.eng.wait_ge(f.taps, m + 1)
                    s.eng.activation(tmp, tmp, ACT.Silu).then_inc(f.act, 1)
                upper(it, 2 * a + 1)
                s.eng.wait_ge(f.hidden, m + 1)
                s.eng.copy(k.hid_hi[:, it * 2 + a, 0:n], tmp).then_inc(f.upper, 1)
                f.ada_load(s, f.step(c) + a + 3, it)

        if c == 0:
            f.ada_begin(s)
        up(0, True)
        with s.eng.Fori(1, nm // 2) as it:
            up(it, False)
        k.u_next = u + 2 * nm + SPLITS
        for j in range(DT):
            split_ahead(k, s, u + 2 * nm + j + 1 + SPLITS)
            if f.norm is not None and c == len(CHUNKS) - 1:
                s.eng.wait_ge(f.added, DT * c + j + 1)
                norm_square(k, s, f.norm, j, k.x if f.total is None else f.total, n, k.probs)
            f.ada_load(s, f.step(c) + nm + j + 3)


def ffn_vector(f, v):
    k, n = f.k, f.n
    for c, (m0, nm) in enumerate(CHUNKS):
        u = f.u0 + f.off(c)

        def up(it):
            for a in range(2):
                m = it * 2 + (m0 + a)
                g, val = 2048 * a, 2048 * a + 1024
                tmp = k.probs[:, a, :]
                if f.layer is not None:
                    v.eng.wait_ge(f.lin, m + 1)
                    for q, (lo, hi) in enumerate(f.parts):
                        link(v, v.eng.scalar_tensor_tensor(tmp[:, lo + 1:hi], k.ps[:, g + lo:g + hi - 1],
                                                           k.params[:, bass.ds(m * 3 + f.w, 1)], tmp[:, lo + 1:hi],
                                                           ALU.mult, ALU.add))
                        ins = v.eng.scalar_tensor_tensor(tmp[:, lo:hi - 1], k.ps[:, g + lo + 1:g + hi],
                                                         k.params[:, bass.ds(m * 3 + (f.w + 2), 1)], tmp[:, lo:hi - 1],
                                                         ALU.mult, ALU.add)
                        if q == len(f.parts) - 1:
                            ins.then_inc(f.taps, 1)
                            v.eng.wait_ge(f.taps, m + 1)
                        else:
                            link(v, ins)
                v.eng.wait_ge(k.unit_done, it * 4 + (u + 2 * a + 2))
                v.eng.wait_ge(f.act, m + 1)
                v.eng.tensor_tensor(tmp[:, 0:n], tmp[:, 0:n], k.ps[:, val:val + n], ALU.mult).then_inc(f.hidden, 1)
                v.eng.wait_ge(f.upper, m + 1)
                v.eng.tensor_tensor(k.hid_lo[:, it * 2 + a, 0:n], tmp[:, 0:n], k.hid_hi[:, it * 2 + a, 0:n].bitcast(F32),
                                    ALU.subtract).then_inc(f.ready, 1)
                v.eng.wait_ge(f.ready, m + 1)
                f.ada_tile(v, f.step(c) + a + 2, it)

        per = (2 * (2 * len(f.parts) - 1) if f.layer is not None else 0) + (2 if f.ada is not None else 0)
        if c == 0 and f.ada is not None:
            v.eng.wait_ge(k.ada_rows_ready, f.ada + 1)
            f.ada_tile(v, 0)
            f.ada_tile(v, 1)
        up(0)
        with v.eng.Fori(1, nm // 2) as it:
            v.enter(it, per)
            up(it)
        v.leave(nm // 2 - 1)
        for j in range(DT):
            buf = 1024 * (j % 3)
            v.eng.wait_ge(k.unit_done, u + 2 * nm + j + 1)
            if f.layer is None:
                if c == 0:
                    ins = v.eng.tensor_copy(f.total[:, j, :], k.bank(2 * (j % 3)))
                else:
                    ins = v.eng.tensor_tensor(f.total[:, j, :], k.bank(2 * (j % 3)), f.total[:, j, :], ALU.add)
            else:
                for q, (a, b) in enumerate(f.parts):
                    ins = v.eng.scalar_tensor_tensor(k.x[:, j, a:b], k.ps[:, buf + a:buf + b],
                                                     k.mod[:, f.layer, 40 + j, q:q + 1], k.x[:, j, a:b],
                                                     ALU.mult, ALU.add)
                    if q < len(f.parts) - 1:
                        link(v, ins)
            ins.then_inc(f.added, 1)
            v.eng.wait_ge(f.added, DT * c + j + 1)
            if f.norm is not None and c == len(CHUNKS) - 1 and j >= 2:
                norm_gather(k, v, f.norm, j - 1, n, k.probs)
            f.ada_tile(v, f.step(c) + nm + j + 2)
    if f.norm is not None:
        norm_gather(k, v, f.norm, DT - 1, n, k.probs)
    f.ada_end(v)



def gdn_views(k):
    b = {}
    b["qkvg"] = k.view(k.big, 0, 16, S)
    b["v_out"] = k.view(k.big, 4096, GH, PAIRS * P)
    b["at"] = k.view(k.big, 4096, 16, P)
    b["k_tok"] = k.view(k.big, 8192, 16, P)
    b["v_tok"] = k.view(k.big, 10240, 16, P)
    b["a"] = k.view(k.big, 12288, 16, P)
    b["t"] = k.view(k.big, 14336, 16, P)
    b["kbe"] = k.view(k.big, 2048, 16, P)
    b["tt"] = k.view(k.h_flat, 0, 16, P)
    b["attn"] = k.view(k.h_flat, 2048, 16, P)
    b["egc"] = k.view(k.h_flat, 4096, GH, S)
    b["am"] = k.view(k.mix_flat, 0, 16, P)
    b["state"] = k.view(k.probs_t, 0, GH, P)
    b["v_new"] = k.sq[:, 0, 0:S].rearrange("p (h n) -> p h n", h=GH)
    return b


def attn_views(k):
    return (k.view(k.big, 0, 4, T), k.view(k.big, 4 * T, 4, T), k.view(k.big, 8 * T, 6, HALF))


def dil_views(k):
    return (k.view(k.big, 0, 4, S), k.view(k.big, 2048, 4, S), k.view(k.big, 4096, 4, HALF),
            k.view(k.big, 6144, 8, S))


def item(q, keys, bias, values, out, rows=slice(0, P), factor=None, adds=False, is_open=False):
    return dict(q=q, keys=keys, bias=bias, values=values, out=out, rows=rows, factor=factor, adds=adds, open=is_open)


def dil_items(k):
    q, key, val, bias = dil_views(k)
    out = []
    for h in range(8):
        r, t = slice(HD * (h % 2), HD * (h % 2) + HD), h // 2
        for i in range(4):
            n = (i + 1) * P
            blk = slice(i * P, n)
            out.append(item(q[r, t, blk], [(key[r, t, 0:n], 0)],
                            [(k.const("flip"), bias[:, h, S - n:S], 0)],
                            [val[:, b, t * P:(t + 1) * P] for b in range(i + 1)], k.mix[r, 4 + t, blk], rows=r))
    return out


def na_items(k):
    q, key, val = attn_views(k)
    bias = k.view(k.big, 12 * T, 8, 14 * GRID_W)
    out = []
    for i in (4, 5, 0, 1, 2, 3):
        for h in range(8):
            r, t = slice(HD * (h % 2), HD * (h % 2) + HD), h // 2
            vals = [val[:, b, t * P:(t + 1) * P] for b in range(6)]
            blk = slice(i * P, (i + 1) * P)
            if i < 4:
                out.append(item(q[r, t, blk], [(key[r, t, 0:S], 0), (key[r, t, S:T], S)],
                                [(k.const("flip"), bias[:, h, (6 - 2 * i) * GRID_W:(6 - 2 * i) * GRID_W + S], 0)],
                                vals, k.mix[r, t, blk], rows=r))
            else:
                out.append(item(q[r, t, blk], [(key[r, t, S:T], 0)], [], vals[4:], k.mix[r, t, blk], rows=r))
    return out


def na_mask_vector(k, v, i):
    if 6 <= i < 14:
        if i == 6:
            v.eng.wait_ge(k.sem("na_bias"), 256)
        bias = k.view(k.big, 12 * T + (i - 6) * 14 * GRID_W, 14, GRID_W)
        v.eng.tensor_tensor(bias, bias, k.const("na_mask", 0, GRID_W).unsqueeze(1).broadcast_to([P, 14, GRID_W]),
                            ALU.add).then_inc(k.sem("na_masked"), 1)


def diff_items(k):
    q, key, val = attn_views(k)
    out = []
    for t in range(4):
        vals = [val[:, b, t * P:(t + 1) * P] for b in range(6)]
        for i in range(6):
            blk = slice(i * P, (i + 1) * P)
            for sub in range(2):
                r = slice(HD * sub, HD * sub + HD)
                keys = [(key[r, t, 0:S], 0), (key[r, t, S:T], S)] if i < 4 else [(key[r, t, S:T], 0)]
                out.append(item(q[r, t, blk], keys, [], vals if i < 4 else vals[4:], k.mix[:, 4 + t, blk],
                                factor=k.small[:, 116:117] if sub else None, adds=sub == 1, is_open=sub == 0))
    return out


def gqa_views(k):
    return k.view(k.big, 0, 4, T), k.view(k.big, 4 * T, 1, T), k.view(k.big, 5 * T, 6, P)


def gqa_items(k):
    q, key, val = gqa_views(k)
    out = []
    for t in range(4):
        for e in range(2):
            r = slice(HD * e, HD * e + HD)
            for i in range(4):
                blk = slice(i * P, (i + 1) * P)
                out.append(item(q[r, t, blk], [(key[r, 0, 0:S], 0), (key[r, 0, S:T], S)], [],
                                [val[:, b, :] for b in range(6)], k.mix[r, t, blk], rows=r))
    return out


def na_project(k):
    q, key, val = attn_views(k)
    return Projection(k, "w_na_qk", 8, "w_na_v", 4, HALF, val, 16, 8,
                      [(q[:, t, :], k.const("heads64"), k.par("na_q"), "eps_query", float(HD), False) for t in range(4)]
                      + [(key[:, t, :], k.const("heads64"), k.par("na_k"), "eps", 1.0, False) for t in range(4)]
                      + [(k.mix[:, 4 + t, :], k.const("heads128"), k.par("subln"), "eps_subln", SUBLN, False)
                         for t in range(4)])


def diff_project(k):
    q, key, val = attn_views(k)
    return Projection(k, "w_diff_qk", 8, "w_diff_v", 4, HALF, val, 8, 0,
                      [(q[:, t, :], k.const("heads64"), k.par("da_q"), "eps_query", float(HD), True) for t in range(4)]
                      + [(key[:, t, :], k.const("heads64"), k.par("da_k"), "eps", 1.0, True) for t in range(4)])


def gqa_project(k):
    q, key, val = gqa_views(k)
    return Projection(k, "w_gqa_qk", 5, "w_gqa_v", 1, P, val, 28, 8,
                      [(q[:, t, 0:S], k.const("heads64"), k.par("gqa_q"), "eps_query", float(HD), True) for t in range(4)]
                      + [(key[:, 0, :], k.const("heads64"), k.par("gqa_k"), "eps", 1.0, True)])


def hy_views(k):
    b = {}
    b["x"] = k.view(k.big, 0, 12, S)
    b["z"] = k.view(k.big, 6144, 4, S)
    b["even"] = k.view(k.big, 8192, 4, S)
    b["odd"] = k.view(k.big, 10240, 4, S)
    b["yc"] = k.view(k.big, 12288, 4, S)
    b["ys"] = k.view(k.big, 14336, 4, S)
    b["w4"] = k.big[0:ORDER, 12288:12288 + D]
    b["w1"] = k.big[0:EMB, 13312:13312 + ORDER]
    b["w2"] = k.big[0:ORDER, 13376:13376 + ORDER]
    b["w3"] = k.big[0:ORDER, 13440:13440 + ORDER]
    b["feats"] = k.big[0:EMB, 13568:13568 + S]
    b["cos"] = k.view(k.h_flat, 0, 4, S)
    b["sin"] = k.view(k.h_flat, 2048, 4, S)
    b["decay"] = k.view(k.h_flat, 4096, 4, S)
    return b



def spread(ap, n):
    return ap.unsqueeze(2).broadcast_to([ap.shape[0], ap.shape[1], n])


def by_head(k, col):
    return k.small[:, col:col + 16].rearrange("p (b h) -> p h b", h=GH)


def all_blocks(mat):
    return mat.unsqueeze(1).broadcast_to([P, 16, P])


def start_vector(k, v):
    v.eng.wait_ge(k.loaded, 48)
    v.eng.tensor_tensor(k.small[0:HD, 112:114], k.params[0:HD, COL["lambdas"][0]:COL["lambdas"][0] + 2],
                        k.params[0:HD, COL["lambdas"][0] + 2:COL["lambdas"][0] + 4], ALU.mult).then_inc(k.sem("lam_products"), 1)
    v.eng.wait_ge(k.sem("lam_products"), 1)
    v.eng.wait_ge(k.sem("lam_exps"), 1)
    link(v, v.eng.scalar_tensor_tensor(k.small[:, 116:117], k.small[:, 115:116], -LAM_INIT, k.small[:, 114:115],
                                      ALU.add, ALU.subtract))


def start_tensor(k, pe):
    pe.wait_ge(k.loaded, 48)
    pe.wait_ge(k.sem("lam_products"), 1)
    pe.matmul(k.bank(7, 2), k.consts[0:HD, CCOL["ones"][0]:CCOL["ones"][0] + P], k.small[0:HD, 112:114],
              start=True, stop=True).then_inc(k.sem("lam_sums"), 1)


def start_scalar(k, s):
    s.eng.wait_ge(k.loaded, 48)
    s.eng.wait_ge(k.sem("lam_sums"), 1)
    s.eng.activation(k.small[:, 114:116], k.bank(7, 2), ACT.Exp).then_inc(k.sem("lam_exps"), 1)
    s.eng.wait_ge(k.sem("lam_exps"), 1)


def values_vector(k, v, name, units, dst, width, blocks):
    v.eng.wait_ge(k.unit_done, FIRST[name] + units)
    for b in range(blocks):
        link(v, v.eng.tensor_copy(dst[:, b, :], k.bank(b, width)))



def dil_project_tensor(k, pe):
    dense_tensor(k, pe, "w_dil_qk", 8, k.h_hi, k.lo1, (S,), k.sem("dil_project_evac"), (k.sem("norm_lo"), 0))
    pe.wait_ge(k.sem("dil_project_evac"), 8)
    pe.wait_ge(k.sem("dil_tables"), 48)
    hot, rel, logs = k.big[0:BUCKETS, 10240:10240 + LINE], k.big[0:BUCKETS, 10880:10888], k.big[0:1, 10888:10888 + LINE]
    for off, n, b in ((0, 512, 6), (512, LINE - 512, 7)):
        pe.matmul(k.ps[0:8, b * 512:b * 512 + n], rel, hot[:, off:off + n], start=True, stop=False)
        last = pe.matmul(k.ps[0:8, b * 512:b * 512 + n], k.consts[0:1, CCOL["ones"][0]:CCOL["ones"][0] + 8],
                         logs[:, off:off + n], start=False, stop=True)
    last.then_inc(k.sem("dil_lines"), 1)
    for u in range(4):
        values_unit(k, pe, "w_dil_v", k.lo1, 4, HALF, u)


def dil_project_vector(k, v):
    v.eng.wait_ge(k.sem("dil_lines"), 1)
    v.eng.tensor_copy(k.big[0:8, 11528:11528 + LINE], k.ps[0:8, 6 * 512:6 * 512 + LINE]).then_inc(k.sem("dil_lines_kept"), 1)
    v.eng.wait_ge(k.sem("dil_lines_kept"), 1)
    values_vector(k, v, "w_dil_v", 4, dil_views(k)[2], HALF, 4)


def dil_project_scalar(k, s):
    q, key, _, _ = dil_views(k)
    copy_out_scalar(k, s, "w_dil_qk", 8, lambda j: (q if j < 4 else key)[:, j % 4, :], lambda j: S,
                    k.sem("dil_project_evac"), lambda j: HD ** -0.5 if j < 4 else 1.0)
    s.eng.wait_ge(k.sem("dil_lines_kept"), 1)
    s.eng.dma_start(k.dram["lines"].ap(), k.big[0:8, 11528:11528 + LINE]).then_inc(k.sem("dil_lines_out"), 16)
    split_along(k, s, "w_dil_v", 4)
    s.eng.wait_ge(k.sem("dil_lines_out"), 16)
    s.eng.dma_start(dil_views(k)[3], bass.AP(k.dram["lines"], 0, [[1, P], [LINE, 8], [1, S]])).then_inc(k.sem("dil_bias"), 16)


def gdn_project_tensor(k, pe):
    slot = FIRST["w_gdn_gates"] % SPLITS
    pe.wait_ge(k.lo_done, FIRST["w_gdn_gates"] + 1)
    for half in range(2):
        for b in range(DT):
            w = slice(b * 8 + half * GH, b * 8 + half * GH + GH)
            last = products(pe, k.ps[0:GH, GATE_BANK[half] * 512:(GATE_BANK[half] + 1) * 512],
                            (k.w_hi[:, slot, w], k.w_lo[:, slot, w]), (k.h_hi[:, b, 0:S], k.lo1[:, b, 0:S]), b == 0, b == DT - 1)
    last.then_inc(k.unit_done, 1)

    def behind(j):
        gdn_gates_tensor(k, pe, j)
        if 2 <= j < 10:
            pe.wait_ge(k.sem("head_squares"), j - 1)
            if j >= 4:
                pe.wait_ge(k.sem("head_rooted"), j - 3)
            pe.matmul(k.bank(5 + 2 * (j % 2)), k.const("ones"), k.sq[:, j % 2, 0:S], start=True, stop=True)\
                .then_inc(k.sem("head_summed"), 1)

    dense_tensor(k, pe, "w_gdn", 16, k.h_hi, k.lo1, (S,), k.sem("gdn_taps"), behind=behind)


def gdn_project_scalar(k, s):
    x = gdn_views(k)["qkvg"]
    split_ahead(k, s, FIRST["w_gdn_gates"] + 1 + SPLITS)
    s.eng.wait_ge(k.unit_done, FIRST["w_gdn_gates"] + 1)

    def silu(j):
        s.eng.wait_ge(k.sem("gdn_taps"), j + 1)
        link(s, s.eng.activation(x[:, j, :], x[:, j, :], ACT.Silu))
        if j < 8:
            if j >= 2:
                s.eng.wait_ge(k.sem("head_summed"), j - 1)
            s.eng.activation(k.sq[:, j % 2, 0:S], x[:, j, :], ACT.Square).then_inc(k.sem("head_squares"), 1)

    def root(j):
        s.eng.wait_ge(k.sem("head_summed"), j + 1)
        if j >= 2:
            s.eng.wait_ge(k.sem("head_normed"), j - 1)
        s.eng.activation(k.probs[:, j % 2, 0:S], k.bank(5 + 2 * (j % 2)), ACT.Sqrt, bias=k.par("eps_delta" if j < 4 else "eps"),
                         scale=float(P) if j < 4 else 1.0).then_inc(k.sem("head_rooted"), 1)

    for j in range(16):
        s.eng.wait_ge(k.unit_done, FIRST["w_gdn"] + j + 1)
        split_ahead(k, s, FIRST["w_gdn"] + j + 1 + SPLITS)
        gdn_gates_scalar(k, s, j)
        src = k.bank(2 * (j % 4))
        if j < 12:
            s.eng.activation(x[:, j, :], src, ACT.Copy, scale=k.par("conv_w", 4 * j + 3)).then_inc(k.sem("gdn_lin"), 1)
            s.eng.wait_ge(k.sem("gdn_lin"), j + 1)
        else:
            s.eng.activation(x[:, j, :], src, ACT.Silu).then_inc(k.sem("gdn_gate_left"), 1)
            s.eng.wait_ge(k.sem("gdn_gate_left"), j - 11)
        if 1 <= j <= 12:
            silu(j - 1)
        if 2 <= j < 10:
            root(j - 2)


def gdn_project_vector(k, v):
    x = gdn_views(k)["qkvg"]
    v.eng.wait_ge(k.unit_done, FIRST["w_gdn_gates"] + 1)
    for j in range(12):
        gdn_gates_vector(k, v, j)
        v.eng.wait_ge(k.sem("gdn_lin"), j + 1)
        for back in (1, 2, 3):
            ins = v.eng.scalar_tensor_tensor(x[:, j, back:S], k.bank(2 * (j % 4), S - back), k.par("conv_w", 4 * j + 3 - back),
                                             x[:, j, back:S], ALU.mult, ALU.add)
            if back == 3:
                ins.then_inc(k.sem("gdn_taps"), 1)
                v.eng.wait_ge(k.sem("gdn_taps"), j + 1)
            else:
                link(v, ins)
        if 2 <= j < 10:
            v.eng.wait_ge(k.sem("head_rooted"), j - 1)
            link(v, v.eng.reciprocal(k.rstd[:, 0:S], k.probs[:, j % 2, 0:S]))
            v.eng.tensor_tensor(x[:, j - 2, :], x[:, j - 2, :], k.rstd[:, 0:S], ALU.mult).then_inc(k.sem("head_normed"), 1)
            v.eng.wait_ge(k.sem("head_normed"), j - 1)


GATE_BANK = (1, 3)


def gate_rows(k):
    return (k.mix_flat[0:GH, 0:S], k.mix_flat[0:GH, S:2 * S], k.mix_flat[0:GH, 2 * S:3 * S])


def gdn_gates_scalar(k, s, j):
    r = slice(0, GH)
    beta, _, soft = gate_rows(k)
    if j == 0:
        s.eng.activation(beta, k.ps[r, GATE_BANK[0] * 512:GATE_BANK[0] * 512 + S], ACT.Exp, scale=-1.0).then_inc(k.sem("gates_exp"), 1)
        link(s, s.eng.activation(k.small[r, 120:121], k.par("a_log")[r], ACT.Exp))
        s.eng.wait_ge(k.sem("gates_exp"), 1)
    if j == 1:
        s.eng.wait_ge(k.sem("gates_abs"), 1)
        link(s, s.eng.activation(soft, soft, ACT.Exp, scale=-1.0))
        s.eng.activation(soft, soft, ACT.Ln, bias=k.par("one")[r]).then_inc(k.sem("gates_exp"), 1)
        s.eng.wait_ge(k.sem("gates_exp"), 2)
    if j == 7:
        s.eng.wait_ge(k.sem("gates_sums"), 1)
        link(s, s.eng.activation(k.small[:, 48:64], k.bank(GATE_BANK[0], 16, 64), ACT.Exp))
        s.eng.activation(k.small[:, 64:80], k.bank(GATE_BANK[0], 16, 96), ACT.Exp).then_inc(k.sem("gates_exp"), 1)
        s.eng.wait_ge(k.sem("gates_exp"), 3)


def gdn_gates_vector(k, v, j):
    r = slice(0, GH)
    beta, y, soft = gate_rows(k)
    if j == 0:
        link(v, v.eng.tensor_scalar(y, k.ps[r, GATE_BANK[1] * 512:GATE_BANK[1] * 512 + S], k.par("dt_bias")[r], None, ALU.add))
        v.eng.scalar_tensor_tensor(soft, y, -1.0, y, ALU.mult, ALU.max).then_inc(k.sem("gates_abs"), 1)
        v.eng.wait_ge(k.sem("gates_abs"), 1)
    if j == 2:
        v.eng.wait_ge(k.sem("gates_exp"), 2)
        link(v, v.eng.tensor_scalar(beta, beta, 1.0, None, ALU.add))
        link(v, v.eng.reciprocal(beta, beta))
        link(v, v.eng.scalar_tensor_tensor(y, y, 0.0, soft, ALU.max, ALU.add))
        v.eng.tensor_scalar(y, y, k.small[r, 120:121], -1.0, ALU.mult, ALU.mult).then_inc(k.sem("gates_rows"), 1)
        v.eng.wait_ge(k.sem("gates_rows"), 1)
    if j == 4:
        v.eng.wait_ge(k.sem("gates_turned"), 1)
        v.eng.tensor_copy(k.small[:, 16:48], k.bank(GATE_BANK[0], 32)).then_inc(k.sem("gates_cols"), 1)
        v.eng.wait_ge(k.sem("gates_cols"), 1)
    if j == 8:
        v.eng.wait_ge(k.sem("gates_exp"), 3)
        link(v, v.eng.tensor_tensor(k.small[:, 80:96], k.small[:, 48:64], k.small[:, 32:48], ALU.mult))


def gdn_gates_tensor(k, pe, j):
    r = slice(0, GH)
    beta, y, _ = gate_rows(k)
    if j == 3:
        pe.wait_ge(k.sem("gates_rows"), 1)
        for row, col in ((y, 0), (beta, 16)):
            for b in range(PAIRS):
                last = pe.transpose(k.bank(GATE_BANK[0], GH, col + GH * b), row[:, b * P:(b + 1) * P], k.const("ident")[r, 0:GH])
        last.then_inc(k.sem("gates_turned"), 1)
    if j == 5:
        pe.wait_ge(k.sem("gates_cols"), 1)
        pe.matmul(k.bank(GATE_BANK[0], 16, 64), k.const("upto"), k.small[:, 16:32], start=True, stop=True)
        pe.matmul(k.bank(GATE_BANK[0], 16, 96), k.const("later"), k.small[:, 16:32], start=True, stop=True)\
            .then_inc(k.sem("gates_sums"), 1)


def gdn_masks_tensor(k, pe):
    m = gdn_views(k)
    for h in range(GH):
        for bank, tile, left in ((0, 8 + h, "masks_v_left"), (1, 4 + h, "masks_k_left")):
            if h >= 1:
                pe.wait_ge(k.sem(left), h)
            for b in range(PAIRS):
                last = pe.transpose(k.bank(bank, P, b * P), m["qkvg"][:, tile, b * P:(b + 1) * P], k.const("ident"))
            last.then_inc(k.sem("masks_turned"), 1)
        pe.wait_ge(k.sem("masks_decays"), h + 1)
        if h >= 2:
            pe.wait_ge(k.sem("masks_exp"), 3 * (h - 1))
        base = 2 + 3 * (h % 2)
        for b in range(PAIRS):
            i = 4 * h + b
            pe.matmul(k.bank(base, P, b * P), k.const("upto"), m["tt"][:, i, :], start=True, stop=True)
            pe.matmul(k.bank(base + 1, P, b * P), m["tt"][:, i, :], k.const("upto"), start=True, stop=True)
            last = pe.matmul(k.bank(base + 2, P, b * P), m["attn"][:, i, :], k.const("upto"), start=True, stop=True)
        last.then_inc(k.sem("masks_sums"), 1)


def gdn_masks_vector(k, v):
    m = gdn_views(k)
    g_col = by_head(k, 16)
    mats = lambda mat: mat.unsqueeze(1).broadcast_to([P, 4, P])

    def masked(h):
        blk = slice(4 * h, 4 * h + 4)
        v.eng.wait_ge(k.sem("masks_exp"), 3 * h + 3)
        link(v, v.eng.tensor_tensor(m["a"][:, blk, :], m["a"][:, blk, :], mats(k.const("later")), ALU.mult))
        link(v, v.eng.tensor_tensor(m["at"][:, blk, :], m["at"][:, blk, :], mats(k.const("upto")), ALU.mult))

    for h in range(GH):
        blk = slice(4 * h, 4 * h + 4)
        link(v, v.eng.tensor_tensor(m["tt"][:, blk, :], mats(k.const("later")), spread(g_col[:, h, :], P), ALU.mult))
        v.eng.tensor_tensor(m["attn"][:, blk, :], mats(k.const("ones")), spread(g_col[:, h, :], P), ALU.mult)\
            .then_inc(k.sem("masks_decays"), 1)
        v.eng.wait_ge(k.sem("masks_turned"), 2 * h + 1)
        v.eng.tensor_tensor(m["v_tok"][:, blk, :], k.bank(0).rearrange("p (b n) -> p b n", b=PAIRS),
                            spread(by_head(k, 32)[:, h, :], P), ALU.mult).then_inc(k.sem("masks_v_left"), 1)
        if h >= 2:
            masked(h - 2)
    masked(GH - 2)
    masked(GH - 1)


def gdn_masks_scalar(k, s):
    m = gdn_views(k)
    for h in range(GH):
        blk = slice(4 * h, 4 * h + 4)
        s.eng.wait_ge(k.sem("masks_turned"), 2 * h + 2)
        s.eng.copy(m["k_tok"][:, blk, :], k.bank(1).rearrange("p (b n) -> p b n", b=4)).then_inc(k.sem("masks_k_left"), 1)
        s.eng.wait_ge(k.sem("masks_sums"), h + 1)
        base = 2 + 3 * (h % 2)
        for dst, b in ((m["a"][:, blk, :], base), (m["at"][:, blk, :], base + 1),
                       (m["egc"][:, h, :].rearrange("p (b n) -> p b n", b=4), base + 2)):
            s.eng.activation(dst, k.bank(b).rearrange("p (b n) -> p b n", b=4), ACT.Exp).then_inc(k.sem("masks_exp"), 1)
    s.eng.wait_ge(k.sem("masks_exp"), 3 * GH)


def gdn_products_tensor(k, pe):
    m = gdn_views(k)
    x = m["qkvg"]
    for h in range(GH):
        for b in range(PAIRS):
            kb = x[:, 4 + h, b * P:(b + 1) * P]
            pe.matmul(k.bank(h, P, b * P), kb, kb, start=True, stop=True)
            last = pe.matmul(k.bank(4 + h, P, b * P), kb, x[:, h, b * P:(b + 1) * P], start=True, stop=True)
        last.then_inc(k.sem("products_made"), 1)
    for h in range(GH):
        pe.wait_ge(k.sem("products_used"), h + 1)
        for b in range(PAIRS):
            last = pe.transpose(k.bank(h, P, b * P), m["a"][:, 4 * h + b, :], k.const("ident"))
        last.then_inc(k.sem("products_turned"), 1)


def gdn_products_vector(k, v):
    m = gdn_views(k)
    four = lambda ap: ap.rearrange("p (b n) -> p b n", b=4)
    for h in range(GH):
        blk = slice(4 * h, 4 * h + 4)
        v.eng.wait_ge(k.sem("products_made"), h + 1)
        link(v, v.eng.tensor_tensor(m["attn"][:, blk, :], four(k.bank(4 + h)), m["at"][:, blk, :], ALU.mult))
        link(v, v.eng.tensor_tensor(m["a"][:, blk, :], m["a"][:, blk, :], spread(by_head(k, 32)[:, h, :], P), ALU.mult))
        v.eng.tensor_tensor(m["a"][:, blk, :], four(k.bank(h)), m["a"][:, blk, :], ALU.mult).then_inc(k.sem("products_used"), 1)
        v.eng.wait_ge(k.sem("products_used"), h + 1)
    for h in range(GH):
        v.eng.wait_ge(k.sem("products_turned"), h + 1)
        link(v, v.eng.tensor_copy(m["at"][:, 4 * h:4 * h + 4, :], four(k.bank(h))))
    for dst, src, level in (("t", "a", LEVELS), ("tt", "at", 0)):
        link(v, v.eng.tensor_tensor(m[dst], m[src], all_blocks(k.const("levels", level * P)), ALU.mult))
        link(v, v.eng.tensor_tensor(m[dst], all_blocks(k.const("ident")), m[dst], ALU.subtract))


LEVELS = 6


def gdn_invert_vector(k, v):
    m = gdn_views(k)
    four = lambda ap: ap.rearrange("p (b n) -> p b n", b=4)

    def mask(lev):
        v.eng.tensor_tensor(m["am"], m["at"], all_blocks(k.const("levels", (lev + 1) * P)), ALU.mult)\
            .then_inc(k.sem("inv_masked"), 1)
        v.eng.wait_ge(k.sem("inv_masked"), lev + 1)

    mask(0)
    for lev in range(LEVELS - 1):
        if lev < LEVELS - 2:
            v.eng.wait_ge(k.sem("inv_x"), GH * lev + GH)
            mask(lev + 1)
        for h in range(GH):
            blk = slice(4 * h, 4 * h + 4)
            v.eng.wait_ge(k.sem("inv_z"), GH * lev + h + 1)
            link(v, v.eng.tensor_tensor(m["t"][:, blk, :], m["t"][:, blk, :], four(k.bank(4 + h)), ALU.subtract))
            v.eng.tensor_tensor(m["tt"][:, blk, :], m["tt"][:, blk, :], four(k.bank(h)), ALU.subtract).then_inc(k.sem("inv_updated"), 1)
            v.eng.wait_ge(k.sem("inv_updated"), GH * lev + h + 1)


def gdn_invert_tensor(k, pe):
    m = gdn_views(k)
    for lev in range(LEVELS - 1):
        pe.wait_ge(k.sem("inv_masked"), lev + 1)
        for h in range(GH):
            if lev >= 1:
                pe.wait_ge(k.sem("inv_updated"), GH * (lev - 1) + h + 1)
            for b in range(PAIRS):
                last = pe.matmul(k.bank(h, P, b * P), m["am"][:, 4 * h + b, :], m["t"][:, 4 * h + b, :], start=True, stop=True)
            last.then_inc(k.sem("inv_x"), 1)
        for h in range(GH):
            pe.wait_ge(k.sem("inv_x_kept"), GH * lev + h + 1)
            for b in range(PAIRS):
                i = 4 * h + b
                pe.matmul(k.bank(4 + h, P, b * P), m["tt"][:, i, :], m["a"][:, i, :], start=True, stop=True)
                last = pe.matmul(k.bank(h, P, b * P), m["a"][:, i, :], m["tt"][:, i, :], start=True, stop=True)
            last.then_inc(k.sem("inv_z"), 1)


def gdn_invert_scalar(k, s):
    m = gdn_views(k)
    for lev in range(LEVELS - 1):
        for h in range(GH):
            s.eng.wait_ge(k.sem("inv_x"), GH * lev + h + 1)
            s.eng.copy(m["a"][:, 4 * h:4 * h + 4, :], k.bank(h).rearrange("p (b n) -> p b n", b=4)).then_inc(k.sem("inv_x_kept"), 1)
            s.eng.wait_ge(k.sem("inv_x_kept"), GH * lev + h + 1)


def gdn_apply_vector(k, v):
    m = gdn_views(k)
    four = lambda ap: ap.rearrange("p (b n) -> p b n", b=4)
    for h in range(GH):
        blk = slice(4 * h, 4 * h + 4)
        v.eng.tensor_tensor(m["kbe"][:, blk, :], m["k_tok"][:, blk, :], spread(by_head(k, 80)[:, h, :], P), ALU.mult).then_inc(k.sem("apply_kbe"), 1)
        v.eng.wait_ge(k.sem("apply_kbe"), h + 1)
        link(v, v.eng.tensor_tensor(m["k_tok"][:, blk, :], m["k_tok"][:, blk, :], spread(by_head(k, 64)[:, h, :], P), ALU.mult))
        link(v, v.eng.tensor_tensor(m["qkvg"][:, h, :], m["qkvg"][:, h, :], m["egc"][:, h, :], ALU.mult))
    for h in range(GH):
        v.eng.wait_ge(k.sem("apply_made"), h + 1)
        link(v, v.eng.tensor_copy(m["t"][:, 4 * h:4 * h + 4, :], four(k.bank(4 + h))))
    link(v, v.eng.memset(m["state"], 0.0))


def gdn_apply_scalar(k, s):
    m = gdn_views(k)
    for h in range(GH):
        s.eng.wait_ge(k.sem("apply_made"), h + 1)
        link(s, s.eng.copy(m["a"][:, 4 * h:4 * h + 4, :], k.bank(h).rearrange("p (b n) -> p b n", b=4)))


def gdn_apply_tensor(k, pe):
    m = gdn_views(k)
    for h in range(GH):
        pe.wait_ge(k.sem("apply_kbe"), h + 1)
        for b in range(PAIRS):
            i = 4 * h + b
            pe.matmul(k.bank(h, P, b * P), m["tt"][:, i, :], m["v_tok"][:, i, :], start=True, stop=True)
            last = pe.matmul(k.bank(4 + h, P, b * P), m["kbe"][:, i, :], m["tt"][:, i, :], start=True, stop=True)
        last.then_inc(k.sem("apply_made"), 1)


def gdn_scan_tensor(k, pe):
    m = gdn_views(k)
    for n in range(S // CHUNK):
        r, c = slice(CHUNK * (n % 2), CHUNK * (n % 2) + CHUNK), slice(CHUNK * n, CHUNK * (n + 1))
        out = lambda h: k.ps[:, h * 512 + n * CHUNK:h * 512 + (n + 1) * CHUNK]
        for h in range(GH):
            if n:
                pe.wait_ge(k.sem("scan_state"), GH * (n - 1) + h + 1)
            pe.matmul(k.ps[r, (4 + h) * 512:(4 + h) * 512 + P], m["t"][:, 4 * h + n // 2, r],
                      m["state"][:, h, :], start=True, stop=True).then_inc(k.sem("scan_read"), 1)
            pe.matmul(out(h), m["state"][:, h, :], m["qkvg"][:, h, c], start=True, stop=False)
        for h in range(GH):
            pe.wait_ge(k.sem("scan_new"), GH * n + h + 1)
            pe.matmul(k.bank(4 + h, P, P), m["k_tok"][r, 4 * h + n // 2, :], m["v_new"][r, h, :],
                      start=True, stop=True).then_inc(k.sem("scan_added"), 1)
            last = pe.matmul(out(h), m["v_new"][r, h, :], m["attn"][r, 4 * h + n // 2, r], start=False, stop=True)
    last.then_inc(k.sem("scan_made"), 1)


def gdn_scan_vector(k, v):
    m = gdn_views(k)
    for n in range(S // CHUNK):
        r = slice(CHUNK * (n % 2), CHUNK * (n % 2) + CHUNK)
        for h in range(GH):
            v.eng.wait_ge(k.sem("scan_read"), GH * n + h + 1)
            v.eng.tensor_tensor(m["v_new"][r, h, :], m["a"][r, 4 * h + n // 2, :], k.ps[r, (4 + h) * 512:(4 + h) * 512 + P],
                                ALU.subtract).then_inc(k.sem("scan_new"), 1)
        for h in range(GH):
            v.eng.wait_ge(k.sem("scan_added"), GH * n + h + 1)
            v.eng.scalar_tensor_tensor(m["state"][:, h, :], m["state"][:, h, :],
                                       m["egc"][:, h, CHUNK * n + CHUNK - 1:CHUNK * (n + 1)], k.bank(4 + h, P, P),
                                       ALU.mult, ALU.add).then_inc(k.sem("scan_state"), 1)
    v.eng.wait_ge(k.sem("scan_state"), GH * (S // CHUNK))


def gdn_out_scalar(k, s):
    s.eng.wait_ge(k.sem("scan_made"), 1)
    for h in range(GH):
        if h >= 2:
            s.eng.wait_ge(k.sem("gdn_out_sums"), h - 1)
        s.eng.activation(k.sq[:, h % 2, 0:S], k.bank(h), ACT.Square).then_inc(k.sem("gdn_out_squares"), 1)
        s.eng.wait_ge(k.sem("gdn_out_squares"), h + 1)
    for h in range(GH):
        s.eng.wait_ge(k.sem("gdn_out_sums"), h + 1)
        s.eng.activation(k.bank(4 + h), k.bank(4 + h), ACT.Sqrt, bias=k.eps).then_inc(k.sem("gdn_out_roots"), 1)
        s.eng.wait_ge(k.sem("gdn_out_roots"), h + 1)


def gdn_out_tensor(k, pe):
    for h in range(GH):
        pe.wait_ge(k.sem("gdn_out_squares"), h + 1)
        pe.matmul(k.bank(4 + h), k.const("heads128"), k.sq[:, h % 2, 0:S], start=True, stop=True)\
            .then_inc(k.sem("gdn_out_sums"), 1)


def gdn_out_vector(k, v):
    gate = gdn_views(k)["qkvg"]
    for h in range(GH):
        out = k.mix[:, h, 0:S]
        v.eng.wait_ge(k.sem("gdn_out_roots"), h + 1)
        link(v, v.eng.reciprocal(k.rstd[:, 0:S], k.bank(4 + h)))
        link(v, v.eng.scalar_tensor_tensor(out, k.bank(h), k.par("onorm"), k.rstd[:, 0:S], ALU.mult, ALU.mult))
        link(v, v.eng.tensor_tensor(out, out, gate[:, 12 + h, :], ALU.mult))


def mix1_out_vector(k, v):
    m = k.view(k.big, 0, DT, S)
    for j in range(DT):
        v.eng.wait_ge(k.unit_done, FIRST["w_out1"] + j + 1)
        v.eng.tensor_copy(m[:, j, :], k.bank(2 * (j % 3))).then_inc(k.sem("mix1_evac"), 1)
        v.eng.wait_ge(k.sem("mix1_evac"), j + 1)
        if j >= 2:
            norm_gather(k, v, "mix1_post", j - 1, S)
    norm_gather(k, v, "mix1_post", DT - 1, S)



def hy_project_scalar(k, s):
    x = hy_views(k)["x"]
    for j in range(12):
        s.eng.wait_ge(k.unit_done, FIRST["w_hy"] + j + 1)
        split_ahead(k, s, FIRST["w_hy"] + j + 1 + SPLITS)
        s.eng.activation(x[:, j, :], k.bank(2 * (j % 4)), ACT.Identity, bias=k.par("hy_conv_b", j),
                         scale=k.par("hy_conv_w", 3 * j + 1)).then_inc(k.sem("hy_lin"), 1)
        s.eng.wait_ge(k.sem("hy_lin"), j + 1)


def hy_project_vector(k, v):
    x = hy_views(k)["x"]
    for j in range(12):
        v.eng.wait_ge(k.sem("hy_lin"), j + 1)
        link(v, v.eng.scalar_tensor_tensor(x[:, j, 1:S], k.bank(2 * (j % 4), S - 1), k.par("hy_conv_w", 3 * j),
                                          x[:, j, 1:S], ALU.mult, ALU.add))
        v.eng.scalar_tensor_tensor(x[:, j, 0:S - 1], k.bank(2 * (j % 4), S - 1, 1), k.par("hy_conv_w", 3 * j + 2),
                                   x[:, j, 0:S - 1], ALU.mult, ALU.add).then_inc(k.sem("hy_taps_done"), 1)
        v.eng.wait_ge(k.sem("hy_taps_done"), j + 1)
    for t in range(4):
        link(v, v.eng.tensor_tensor(x[:, 8 + t, :], x[:, 8 + t, :], x[:, 4 + t, :], ALU.mult))


def hy_filter_tensor(k, pe):
    b = hy_views(k)
    pe.wait_ge(k.sem("hy_net_loaded"), 80)
    pe.matmul(k.ps[0:ORDER, 0:S], b["w1"], b["feats"], start=True, stop=True).then_inc(k.sem("hy_layer"), 1)
    for t in range(4):
        if t >= 2:
            pe.wait_ge(k.sem("hy_z_kept"), t - 1)
        for c in range(4):
            last = pe.transpose(k.bank(6 + t % 2, P, c * P), b["x"][:, 8 + c, t * P:(t + 1) * P], k.const("ident"))
        last.then_inc(k.sem("hy_z_turned"), 1)
    for n, w in ((1, "w2"), (2, "w3")):
        pe.wait_ge(k.sem("hy_sin"), n)
        pe.matmul(k.ps[0:ORDER, 0:S], b[w], k.probs[0:ORDER, 0, 0:S], start=True, stop=True).then_inc(k.sem("hy_layer"), 1)


def hy_filter_scalar(k, s):
    b = hy_views(k)
    for t in range(4):
        s.eng.wait_ge(k.sem("hy_z_turned"), t + 1)
        s.eng.copy(b["z"][:, t, :], k.bank(6 + t % 2)).then_inc(k.sem("hy_z_kept"), 1)
        s.eng.wait_ge(k.sem("hy_z_kept"), t + 1)
    for n in range(3):
        s.eng.wait_ge(k.sem("hy_reduced"), n + 1)
        s.eng.activation(k.probs[0:ORDER, 0, 0:S], k.probs[0:ORDER, 1, 0:S], ACT.Sin).then_inc(k.sem("hy_sin"), 1)
        s.eng.wait_ge(k.sem("hy_sin"), n + 1)


def hy_filter_vector(k, v):
    r = slice(0, ORDER)
    arg, turns = k.probs[r, 1, 0:S], k.sq[r, 0, 0:S]
    for n in range(3):
        v.eng.wait_ge(k.sem("hy_layer"), n + 1)
        link(v, v.eng.tensor_scalar(arg, k.ps[r, 0:S], k.par("hy_b", n)[r], k.par("hy_freq")[r], ALU.add, ALU.mult))
        link(v, v.eng.tensor_scalar(turns, arg, 1.0 / (2.0 * np.pi), ROUND, ALU.mult, ALU.add))
        link(v, v.eng.tensor_scalar(turns, turns, ROUND, None, ALU.subtract))
        link(v, v.eng.scalar_tensor_tensor(arg, turns, -TWO_PI_HI, arg, ALU.mult, ALU.add))
        link(v, v.eng.scalar_tensor_tensor(arg, turns, -TWO_PI_LO, arg, ALU.mult, ALU.add))
        v.eng.tensor_scalar(arg, arg, PI_IN, -PI_IN, ALU.min, ALU.max).then_inc(k.sem("hy_reduced"), 1)
        v.eng.wait_ge(k.sem("hy_reduced"), n + 1)


def hy_taps_tensor(k, pe):
    b = hy_views(k)

    def sums(t):
        pe.wait_ge(k.sem("hy_sizes"), t + 1)
        for c in range(4):
            last = pe.matmul(k.bank(4 + c, 1), k.sq[:, t % 2, c * P:(c + 1) * P], k.const("ones")[:, 0:1],
                             start=t == 0, stop=t == 3)
        last.then_inc(k.sem("hy_summed"), 1)

    for t in range(4):
        if t >= 2:
            pe.wait_ge(k.sem("hy_taps_made"), t - 1)
        hid = k.probs[0:ORDER, 0, t * P:(t + 1) * P]
        pe.matmul(k.bank(2 * (t % 2)), hid, b["w4"][:, 0:S], start=True, stop=True)
        pe.matmul(k.bank(2 * (t % 2) + 1), hid, b["w4"][:, S:2 * S], start=True, stop=True).then_inc(k.sem("hy_raw"), 1)
        if t >= 1:
            sums(t - 1)
    sums(3)


def hy_taps_vector(k, v):
    b = hy_views(k)
    v.eng.wait_ge(k.sem("hy_tables"), 48)
    fwd, bwd = k.rstd[:, 0:S], k.probs_t[:, 0:S]
    for t in range(4):
        v.eng.wait_ge(k.sem("hy_raw"), t + 1)
        link(v, v.eng.tensor_tensor(fwd, k.bank(2 * (t % 2)), b["decay"][:, t, :], ALU.mult))
        if t == 0:
            link(v, v.eng.scalar_tensor_tensor(bwd, k.bank(1), k.par("hy_first"), b["decay"][:, 0, :], ALU.mult, ALU.mult))
        else:
            link(v, v.eng.tensor_tensor(bwd, k.bank(2 * (t % 2) + 1), b["decay"][:, t, :], ALU.mult))
        link(v, v.eng.tensor_tensor(b["even"][:, t, :], fwd, bwd, ALU.add))
        link(v, v.eng.tensor_tensor(b["odd"][:, t, :], fwd, bwd, ALU.subtract))
        v.eng.scalar_tensor_tensor(fwd, fwd, -1.0, fwd, ALU.mult, ALU.max).then_inc(k.sem("hy_taps_made"), 1)
        v.eng.wait_ge(k.sem("hy_taps_made"), t + 1)
        link(v, v.eng.scalar_tensor_tensor(bwd, bwd, -1.0, bwd, ALU.mult, ALU.max))
        if t >= 2:
            v.eng.wait_ge(k.sem("hy_summed"), t - 1)
        v.eng.tensor_tensor(k.sq[:, t % 2, 0:S], fwd, bwd, ALU.add).then_inc(k.sem("hy_sizes"), 1)
        v.eng.wait_ge(k.sem("hy_sizes"), t + 1)
    v.eng.wait_ge(k.sem("hy_summed"), 4)
    for c in range(4):
        link(v, v.eng.reciprocal(k.small[:, 124 + c:125 + c], k.bank(4 + c, 1)))


def hy_forward_tensor(k, pe):
    b = hy_views(k)
    for f in range(4):
        if f >= 2:
            pe.wait_ge(k.sem("hy_product"), f - 1)
        col = slice(f * P, (f + 1) * P)
        for n, (table, src) in enumerate((("cos", "z"), ("sin", "z"), ("cos", "even"), ("sin", "odd"))):
            for t in range(4):
                last = pe.matmul(k.bank(4 * (f % 2) + n), b[table][:, t, col], b[src][:, t, :], start=t == 0, stop=t == 3)
        last.then_inc(k.sem("hy_bins"), 1)


def hy_forward_scalar(k, s):
    for f in range(4):
        s.eng.wait_ge(k.sem("hy_bins"), f + 1)
        if f >= 1:
            s.eng.wait_ge(k.sem("hy_product"), f)
        link(s, s.eng.copy(k.sq[:, 0, 0:S], k.bank(4 * (f % 2))))
        s.eng.copy(k.sq[:, 1, 0:S], k.bank(4 * (f % 2) + 1)).then_inc(k.sem("hy_bins_kept"), 1)
        s.eng.wait_ge(k.sem("hy_bins_kept"), f + 1)


def hy_forward_vector(k, v):
    b = hy_views(k)
    zc, zs, tmp = k.sq[:, 0, 0:S], k.sq[:, 1, 0:S], k.rstd[:, 0:S]
    for f in range(4):
        kc, ks = k.bank(4 * (f % 2) + 2), k.bank(4 * (f % 2) + 3)
        yc, ys = b["yc"][:, f, :], b["ys"][:, f, :]
        v.eng.wait_ge(k.sem("hy_bins_kept"), f + 1)
        link(v, v.eng.tensor_tensor(yc, zc, kc, ALU.mult))
        link(v, v.eng.tensor_tensor(tmp, zs, ks, ALU.mult))
        link(v, v.eng.tensor_tensor(yc, yc, tmp, ALU.subtract))
        link(v, v.eng.tensor_tensor(ys, zc, ks, ALU.mult))
        link(v, v.eng.tensor_tensor(tmp, zs, kc, ALU.mult))
        v.eng.tensor_tensor(ys, ys, tmp, ALU.add).then_inc(k.sem("hy_product"), 1)
        v.eng.wait_ge(k.sem("hy_product"), f + 1)


def hy_inverse_tensor(k, pe):
    b = hy_views(k)
    pe.wait_ge(k.sem("hy_tables"), 80)
    for c in range(4):
        for n, (src, table) in enumerate((("yc", "cos"), ("ys", "sin"))):
            for f in range(4):
                last = pe.matmul(k.bank(c), b[src][:, f, c * P:(c + 1) * P], b[table][:, f, :],
                                 start=n == 0 and f == 0, stop=n == 1 and f == 3)
        last.then_inc(k.sem("hy_back"), 1)


def hy_inverse_vector(k, v):
    x = hy_views(k)["x"]
    for c in range(4):
        out = k.mix[:, 4 + c, 0:S]
        v.eng.wait_ge(k.sem("hy_back"), c + 1)
        link(v, v.eng.tensor_scalar(out, k.bank(c), k.small[:, 124 + c:125 + c], None, ALU.mult))
        link(v, v.eng.scalar_tensor_tensor(out, x[:, 8 + c, :], k.par("hy_skip", c), out, ALU.mult, ALU.add))
        link(v, v.eng.tensor_tensor(out, out, x[:, c, :], ALU.mult))



def sync_program(k, sp):
    d = k.dram
    sp.dma_start(k.x[:, :, 0:S], d["x"]).then_inc(k.loaded, 16)
    sp.dma_start(k.params[:, :], d["params"]).then_inc(k.loaded, 16)
    early, late = CCOL["levels"][1], CCOL["na_mask"][0]
    sp.dma_start(k.consts[:, early:late], d["consts"][:, early:late]).then_inc(k.loaded, 16)
    for name, n in STREAM:
        u0 = FIRST[name]

        def load(a, it=0):
            if u0 + a >= SLOTS:
                sp.wait_ge(k.lo_done, it * SLOTS + (u0 + a - SLOTS + 1))
            sp.dma_start(k.ring[:, (u0 + a) % SLOTS, :], d[name][it * SLOTS + a]).then_inc(k.slot_landed[(u0 + a) % SLOTS], 16)

        looped = n // SLOTS if u0 >= SLOTS and n >= 3 * SLOTS else 0
        if looped:
            with sp.Fori(0, looped) as it:
                for a in range(SLOTS):
                    load(a, it)
        for a in range(looped * SLOTS, n):
            load(a)
            if u0 + a == SLOTS - 1:
                for dst, src in ((k.consts[:, 0:early], d["consts"][:, 0:early]),
                                 (k.consts[:, late:NCONST], d["consts"][:, late:NCONST]), (k.x[:, :, S:T], d["ctx"])):
                    sp.dma_start(dst, src).then_inc(k.loaded_late, 16)
    k.after(sp, "ffn3")
    sp.dma_start(d["out"], k.x[:, :, 0:S]).then_inc(k.sem("out_written"), 16)
    sp.wait_ge(k.sem("out_written"), 16)


def gpsimd_program(k, pool):
    def lower(a, it=0):
        pool.wait_ge(k.hi_done, it * SLOTS + (a + 1))
        pool.tensor_tensor(k.w_lo[:, a % SPLITS, :], k.ring[:, a % SLOTS, :], k.w_hi[:, a % SPLITS, :].bitcast(F32),
                           ALU.subtract).then_inc(k.lo_done, 1)

    with pool.Fori(0, UNITS // SLOTS) as it:
        for a in range(SLOTS):
            lower(a, it)
    for a in range(UNITS // SLOTS * SLOTS, UNITS):
        lower(a)



def load_distance_tables(k, act):
    hot, d = k.sem("dil_tables"), k.dram
    act.dma_start(k.big[0:BUCKETS, 10240:10240 + LINE], d["buckets"]).then_inc(hot, 16)
    act.dma_start(k.big[0:BUCKETS, 10880:10888], d["rel_bias"]).then_inc(hot, 16)
    act.dma_start(k.big[0:1, 10888:10888 + LINE], d["log_counts"]).then_inc(hot, 16)


def load_na_bias(k, act):
    bias = k.view(k.big, 12 * T, 8, 14 * GRID_W)
    wide = 2 * GRID_W - 1
    for h in range(8):
        for a in range(2):
            act.dma_start(bias[GRID_W * a:GRID_W * (a + 1), h, :].rearrange("p (r c) -> p r c", c=GRID_W),
                          bass.AP(k.dram["rpb"], (h * 15 + a) * wide, [[1, GRID_W], [wide, 14], [1, GRID_W]]))\
                .then_inc(k.sem("na_bias"), 16)


def load_hyena(k, act):
    b, d = hy_views(k), k.dram
    for name, src in (("w1", "hy_w1"), ("w2", "hy_w2"), ("w3", "hy_w3"), ("w4", "hy_w4"), ("feats", "feats")):
        act.dma_start(b[name], d[src]).then_inc(k.sem("hy_net_loaded"), 16)
    for name, src in (("decay", "decay"), ("cos", "dft_cos"), ("sin", "dft_sin")):
        act.dma_start(b[name], d[src]).then_inc(k.sem("hy_tables"), 16)


def load_hyena_inverse(k, act):
    b, d = hy_views(k), k.dram
    for name, src in (("cos", "idft_cos"), ("sin", "idft_sin")):
        act.dma_start(b[name], d[src]).then_inc(k.sem("hy_tables"), 16)


def tensor_program(k, pe):
    start_tensor(k, pe)
    k.after(pe, "start")
    norm_tensor(k, pe, "norm1", S)
    dil_project_tensor(k, pe)
    k.after(pe, "dil_project")
    pe.wait_ge(k.sem("dil_bias"), 16)
    Attention(k, 0, 0, dil_items(k)).tensor(pe)
    k.after(pe, "dil_attend")
    pe.wait_ge(k.loaded_late, 48)
    gdn_project_tensor(k, pe)
    k.after(pe, "gdn_project")
    gdn_masks_tensor(k, pe)
    k.after(pe, "gdn_masks")
    gdn_products_tensor(k, pe)
    k.after(pe, "gdn_products")
    gdn_invert_tensor(k, pe)
    k.after(pe, "gdn_invert")
    gdn_apply_tensor(k, pe)
    k.after(pe, "gdn_apply")
    gdn_scan_tensor(k, pe)
    k.after(pe, "gdn_scan")
    gdn_out_tensor(k, pe)
    mix_lower = lambda name: (k.sem("mix_lower"), DT * MIXES.index(name))
    k.after(pe, "gdn_out")
    dense_tensor(k, pe, "w_out1", DT, k.h_hi, k.mix_lo, (S,), k.sem("mix1_evac"), mix_lower("mix1"), nbuf=3)
    norm_sum(k, pe, "mix1_post", None, S)
    norm_tensor(k, pe, "norm2", S)
    norm_lo = lambda name: (k.sem("norm_lo"), DT * LOWERED.index(name))
    ffn_tensor(ffn1(k), pe, norm_lo("norm2"))
    norm_tensor(k, pe, "mod_a0", T)
    diff_project(k).tensor(pe, k.lo2, norm_lo("mod_a0"))
    k.after(pe, "diff_project")
    Attention(k, 32, 32, diff_items(k)).tensor(pe)
    k.after(pe, "diff_attend")
    na_project(k).tensor(pe, k.lo2)
    k.after(pe, "na_project")
    Attention(k, 80, 56, na_items(k)).tensor(pe, (k.sem("na_masked"), 8))
    k.after(pe, "na_attend")
    dense_tensor(k, pe, "w_out_e", DT, k.h_hi, k.mix_lo, (S, CTX), k.sem("mix_e_evac"), mix_lower("mix_e"), nbuf=3)
    norm_sum(k, pe, "mod_f0", None, T)
    ffn_tensor(Ffn(k, "w_ffn2", 0, T, 1, "mod_a1"), pe, norm_lo("mod_f0"))
    gqa_project(k).tensor(pe, k.lo2, norm_lo("mod_a1"))
    k.after(pe, "gqa_project")
    Attention(k, 128, 104, gqa_items(k)).tensor(pe)
    k.after(pe, "gqa_attend")
    dense_tensor(k, pe, "w_hy", 12, k.h_hi, k.lo2, (S,), k.sem("hy_taps_done"))
    k.after(pe, "hy_project")
    hy_filter_tensor(k, pe)
    k.after(pe, "hy_filter")
    hy_taps_tensor(k, pe)
    k.after(pe, "hy_taps")
    hy_forward_tensor(k, pe)
    k.after(pe, "hy_forward")
    hy_inverse_tensor(k, pe)
    k.after(pe, "hy_inverse")
    dense_tensor(k, pe, "w_out_o", DT, k.h_hi, k.mix_lo, (S,), k.sem("mix_o_evac"), mix_lower("mix_o"), nbuf=3)
    norm_sum(k, pe, "mod_f1", None, S)
    ffn_tensor(Ffn(k, "w_ffn3", 1, S, None, None), pe, norm_lo("mod_f1"))


def scalar_program(k, act):
    s = Serial(act, k.sem("scalar_own"))
    end = lambda stage: stage_end(k, act, k.scalar_stages, stage)
    m1 = k.view(k.big, 0, DT, S)
    load_distance_tables(k, act)
    start_scalar(k, s)
    split_ahead(k, s, SPLITS)
    end("start")
    for t in range(DT):
        norm_square(k, s, "norm1", t, k.x, S)
    plain_norm_scalar(k, s, "norm1")
    end("norm1")
    dil_project_scalar(k, s)
    end("dil_project")
    Attention(k, 0, 0, dil_items(k)).scalar(s)
    end("dil_attend")
    act.wait_ge(k.loaded_late, 48)
    gdn_project_scalar(k, s)
    end("gdn_project")
    gdn_masks_scalar(k, s)
    end("gdn_masks")
    end("gdn_products")
    gdn_invert_scalar(k, s)
    end("gdn_invert")
    gdn_apply_scalar(k, s)
    end("gdn_apply")
    end("gdn_scan")
    gdn_out_scalar(k, s)
    end("gdn_out")
    mix_split_scalar(k, s, "mix1", S)
    end("mix1_split")
    along_scalar(k, s, "w_out1", k.sem("mix1_evac"), "mix1_post", m1, S)
    end("mix1_out")
    norm_root(k, s, "mix1_post", S)
    updated_scalar(k, s, "norm2", 0, S)
    end("mix1_post")
    plain_norm_scalar(k, s, "norm2")
    end("norm2")
    f1 = ffn1(k)
    ffn_scalar(f1, s)
    end("ffn1")
    norm_root(k, s, "ffn1_post", S)
    updated_scalar(k, s, "mod_a0", DT, T)
    end("ffn1_post")
    modulate_scalar(k, s, "mod_a0", 0, 0, T)
    end("mod_a0")
    diff_project(k).scalar(s)
    end("diff_project")
    Attention(k, 32, 32, diff_items(k)).scalar(s)
    end("diff_attend")
    na_project(k).scalar(s)
    end("na_project")
    load_na_bias(k, act)
    Attention(k, 80, 56, na_items(k)).scalar(s)
    end("na_attend")
    mix_split_scalar(k, s, "mix_e", T)
    end("mix_e_split")
    along_scalar(k, s, "w_out_e", k.sem("mix_e_evac"), "mod_f0", k.x, T)
    end("mix_e_out")
    modulate_scalar(k, s, "mod_f0", 0, 24, T)
    end("mod_f0")
    ffn_scalar(Ffn(k, "w_ffn2", 0, T, 1, "mod_a1"), s)
    end("ffn2")
    modulate_scalar(k, s, "mod_a1", 1, 0, T)
    end("mod_a1")
    gqa_project(k).scalar(s)
    end("gqa_project")
    Attention(k, 128, 104, gqa_items(k)).scalar(s)
    end("gqa_attend")
    hy_project_scalar(k, s)
    end("hy_project")
    load_hyena(k, act)
    hy_filter_scalar(k, s)
    end("hy_filter")
    end("hy_taps")
    hy_forward_scalar(k, s)
    end("hy_forward")
    load_hyena_inverse(k, act)
    end("hy_inverse")
    mix_split_scalar(k, s, "mix_o", S)
    end("mix_o_split")
    along_scalar(k, s, "w_out_o", k.sem("mix_o_evac"), "mod_f1", k.x, S)
    end("mix_o_out")
    modulate_scalar(k, s, "mod_f1", 1, 24, S)
    end("mod_f1")
    ffn_scalar(Ffn(k, "w_ffn3", 1, S, None, None), s)
    end("ffn3")


def vector_program(k, dve):
    v = Serial(dve, k.sem("vector_own"))
    end = lambda stage: stage_end(k, dve, k.vector_stages, stage)
    m1 = k.view(k.big, 0, DT, S)
    start_vector(k, v)
    end("start")
    plain_norm_vector(k, v, "norm1", "g_mix_pre", k.lo1)
    end("norm1")
    dil_project_vector(k, v)
    end("dil_project")
    Attention(k, 0, 0, dil_items(k)).vector(v)
    end("dil_attend")
    dve.wait_ge(k.loaded_late, 48)
    gdn_project_vector(k, v)
    end("gdn_project")
    gdn_masks_vector(k, v)
    end("gdn_masks")
    gdn_products_vector(k, v)
    end("gdn_products")
    gdn_invert_vector(k, v)
    end("gdn_invert")
    gdn_apply_vector(k, v)
    end("gdn_apply")
    gdn_scan_vector(k, v)
    end("gdn_scan")
    gdn_out_vector(k, v)
    end("gdn_out")
    mix_split_vector(k, v, "mix1", S)
    end("mix1_split")
    mix1_out_vector(k, v)
    end("mix1_out")
    post_norm_vector(k, v, "mix1_post", m1, "g_mix_post")
    end("mix1_post")
    plain_norm_vector(k, v, "norm2", "g_ffn_pre", k.lo3)
    end("norm2")
    f1 = ffn1(k)
    ffn_vector(f1, v)
    end("ffn1")
    post_norm_vector(k, v, "ffn1_post", f1.total, "g_ffn_post")
    end("ffn1_post")
    modulate_vector(k, v, "mod_a0", k.lo2, T)
    end("mod_a0")
    diff_project(k).vector(v)
    end("diff_project")
    Attention(k, 32, 32, diff_items(k)).vector(v)
    end("diff_attend")
    na_project(k).vector(v)
    end("na_project")
    Attention(k, 80, 56, na_items(k)).vector(v, lambda i: na_mask_vector(k, v, i))
    end("na_attend")
    mix_split_vector(k, v, "mix_e", T)
    end("mix_e_split")
    residual_vector(k, v, "w_out_e", 0, T, k.sem("mix_e_evac"), "mod_f0")
    end("mix_e_out")
    modulate_vector(k, v, "mod_f0", k.lo3, T)
    end("mod_f0")
    ffn_vector(Ffn(k, "w_ffn2", 0, T, 1, "mod_a1"), v)
    end("ffn2")
    modulate_vector(k, v, "mod_a1", k.lo2, T)
    end("mod_a1")
    gqa_project(k).vector(v)
    end("gqa_project")
    Attention(k, 128, 104, gqa_items(k)).vector(v)
    end("gqa_attend")
    hy_project_vector(k, v)
    end("hy_project")
    hy_filter_vector(k, v)
    end("hy_filter")
    hy_taps_vector(k, v)
    end("hy_taps")
    hy_forward_vector(k, v)
    end("hy_forward")
    hy_inverse_vector(k, v)
    end("hy_inverse")
    mix_split_vector(k, v, "mix_o", S)
    end("mix_o_split")
    residual_vector(k, v, "w_out_o", 1, S, k.sem("mix_o_evac"), "mod_f1")
    end("mix_o_out")
    modulate_vector(k, v, "mod_f1", k.lo3, S)
    end("mod_f1")
    ffn_vector(Ffn(k, "w_ffn3", 1, S, None, None), v)
    end("ffn3")


def build(nc, dram):
    with ExitStack() as ctx:
        k = Core(nc, ctx, dram)
        block = ctx.enter_context(nc.Block())

        @block.sync
        def _(sp):
            sync_program(k, sp)

        @block.gpsimd
        def _(pool):
            gpsimd_program(k, pool)

        @block.tensor
        def _(pe):
            tensor_program(k, pe)

        @block.scalar
        def _(act):
            scalar_program(k, act)

        @block.vector
        def _(dve):
            vector_program(k, dve)



def constants():
    f = np.float32
    out = {name: np.zeros((P, n), f) for name, n in CONSTS}
    i, j = np.arange(P)[:, None], np.arange(P)[None, :]
    same = i // CHUNK == j // CHUNK
    out["ident"][:] = i == j
    out["ones"][:] = 1
    out["ones_d"][:] = 1 / D
    out["heads64"][:] = (i // HD == j // HD) / HD
    out["heads128"][:] = 1 / P
    out["flip"][:] = i == P - 1 - j
    out["rope_swap"][:] = np.where((i == j + 1) & (j % 2 == 0), -1, 0) + np.where((i == j - 1) & (j % 2 == 1), 1, 0)
    out["later"][:] = same & (i > j)
    out["upto"][:] = same & (i <= j)
    for lev in range(LEVELS):
        s = 1 << lev
        out["levels"][:, lev * P:(lev + 1) * P] = (i // (2 * s) == j // (2 * s)) & (i // s + 1 == j // s)
    out["levels"][:, LEVELS * P:] = out["levels"][:, 0:P].T
    cq, ck = np.arange(P)[::-1, None] % GRID_W, np.arange(GRID_W)[None, :]
    first = np.clip(cq - WIN_C // 2, 0, GRID_W - WIN_C)
    out["na_mask"][:] = np.where((ck >= first) & (ck < first + WIN_C), 0, MASKED)
    t = np.arange(S)
    pairs = HD // 4
    inv = f(10000.0) ** (-np.arange(pairs, dtype=f) / f(pairs))
    ang = np.concatenate([(t // GRID_W).astype(f)[:, None] * inv, (t % GRID_W).astype(f)[:, None] * inv], axis=1)
    which = (np.arange(P) % HD) // 2
    out["cos"][:] = np.cos(ang)[:, which].T
    out["sin"][:] = np.sin(ang)[:, which].T
    return np.concatenate([out[name] for name, _ in CONSTS], axis=1)


def distance_tables():
    f = np.float32
    d = S - 1 - np.arange(LINE)
    far = np.maximum(d, 1).astype(f)
    log_b = 16 + (np.log(far / f(16)) / f(np.log(2048 / 16)) * f(16)).astype(np.int32)
    bucket = np.where(d < 16, np.maximum(d, 0), np.minimum(log_b, BUCKETS - 1))
    hot = (np.arange(BUCKETS)[:, None] == bucket[None, :]).astype(f)
    count = (d <= 128).astype(int) + (d % 4 == 0) + (d % 16 == 0)
    logs = np.where((d >= 0) & (count > 0), np.log(np.maximum(count, 1)), MASKED)
    return hot, logs.astype(f)[None, :]


def hyena_tables():
    f = np.float32
    t = np.linspace(0.0, 1.0, S, dtype=f)[:, None]
    bands = (EMB - 1) // 2
    w = f(2.0 * np.pi) * np.arange(S, dtype=f)[:, None] / f(S)
    freq = np.linspace(1e-4, bands - 1, bands, dtype=f)[None, :]
    feats = np.concatenate([t, np.cos(freq * w), -np.sin(freq * w)], axis=1).T
    deltas = np.linspace(np.log(1e-2) / 1.5, np.log(1e-2) / 0.3, HALF, dtype=f)
    decay = np.exp(-t * np.abs(deltas))
    angle = np.pi / (2 * S) * ((2 * np.arange(S)[None, :] + 1) * np.arange(S)[:, None] % (4 * S))
    tiles = lambda a: np.ascontiguousarray(a.reshape(4, P, -1).transpose(1, 0, 2).astype(f))
    return {"feats": np.ascontiguousarray(feats.astype(f)), "decay": tiles(decay),
            "dft_cos": tiles(np.cos(angle)), "dft_sin": tiles(np.sin(angle)),
            "idft_cos": tiles(np.cos(angle).T / S), "idft_sin": tiles(np.sin(angle).T / S)}



def by_output(w, blocks=DT):
    kt, nt = w.shape[0] // P, w.shape[1] // P
    a = w.reshape(kt // blocks, blocks, P, nt, P).transpose(3, 0, 2, 1, 4)
    return np.ascontiguousarray(a.reshape(nt * (kt // blocks), P, blocks * P))


def by_input(w):
    n = w.shape[1]
    per = 1024 // n
    return np.ascontiguousarray(w.reshape(DT // per, per, P, n).transpose(0, 2, 1, 3).reshape(DT // per, P, per * n))


def alternate(a, b):
    a, b = by_output(a), by_output(b)
    return np.stack([a, b], axis=1).reshape(2 * len(a), P, D)


def by_chunk(gate, up, down):
    first, out = alternate(gate, up), []
    for m0, nm in CHUNKS:
        out.append(first[2 * m0:2 * (m0 + nm)])
        rows = np.zeros((DT, P, D), np.float32)
        rows[:, :, 0:nm * P] = by_output(down[m0 * P:(m0 + nm) * P], nm)
        out.append(rows)
    return np.concatenate(out)


def cols(vec):
    return np.asarray(vec).reshape(-1, P).T


def padded(a):
    a = np.asarray(a, np.float32)
    out = np.zeros((P, a.shape[1]), np.float32)
    out[:a.shape[0]] = a
    return out


def layout(i):
    g = {name: np.asarray(a) for name, a in i.items()}
    W = g["w_in"][0]
    o = {}
    gw = GH * P
    q0 = 4 * gw + 2 * GH
    o["w_dil_qk"] = by_output(W[:, q0:q0 + 2 * HALF])
    o["w_dil_v"] = by_input(W[:, q0 + 2 * HALF:q0 + 3 * HALF])
    o["w_gdn"] = by_output(W[:, 0:4 * gw])
    o["w_gdn_gates"] = np.zeros((1, P, D), np.float32)
    o["w_gdn_gates"][0, :, 0:8 * DT] = W[:, 4 * gw:q0].reshape(DT, P, 2 * GH).transpose(1, 0, 2).reshape(P, 8 * DT)
    o["w_out1"] = by_output(g["w_out"][0])
    o["w_ffn1"] = by_chunk(g["w_gate"][0], g["w_up"][0], g["w_down"][0])
    for l in range(2):
        up = g["w_up_2"][l]
        o[f"w_ffn{l + 2}"] = by_chunk(up[:, 0:F], up[:, F:], g["w_down_2"][l])
        o[f"w_ada{l}"] = g["w_ada_2"][l].T.reshape(ADA, P, D)
    o["cond_rows"] = np.concatenate([g["c_2"].reshape(1, D), g["c_ctx_2"].reshape(1, D)])
    E = g["w_in_e_2"][0]
    o["w_na_qk"], o["w_na_v"] = by_output(E[:, 0:1024]), by_input(E[:, 1024:1536])
    o["w_diff_qk"], o["w_diff_v"] = by_output(E[:, 1536:2560]), by_input(E[:, 2560:3072])
    o["w_out_e"] = by_output(g["w_out_e_2"][0])
    O = g["w_in_o_2"][0]
    order = [t + 4 * e for t in range(4) for e in range(2)]
    q = O[:, 0:HALF].reshape(D, 8, HD)[:, order].reshape(D, HALF)
    o["w_gqa_qk"] = by_output(np.concatenate([q, O[:, HALF:HALF + P]], axis=1))
    o["w_gqa_v"] = by_input(O[:, HALF + P:HALF + 2 * P])
    o["w_hy"] = by_output(O[:, HALF + 2 * P:])
    wo = g["w_out_o_2"][0]
    o["w_out_o"] = by_output(np.concatenate([wo[0:HALF].reshape(8, HD, D)[order].reshape(HALF, D), wo[HALF:]]))

    o["x"] = np.ascontiguousarray(g["x"][0].T.reshape(DT, P, S).transpose(1, 0, 2))
    o["ctx"] = np.ascontiguousarray(g["ctx_2"][0].T.reshape(DT, P, CTX).transpose(1, 0, 2))
    taps = lambda w: np.stack([cols(r) for r in w], axis=2).reshape(P, -1)
    twice = lambda v: np.concatenate([v, v]).reshape(P, 1)
    both = lambda v: np.repeat(cols(v), 2, axis=1)
    p = {
        "g_mix_pre": cols(g["g_mix_pre"]), "g_mix_post": cols(g["g_mix_post"]),
        "g_ffn_pre": cols(g["g_ffn_pre"]), "g_ffn_post": cols(g["g_ffn_post"]),
        "conv_w": taps(g["conv_w"][0]), "a_log": padded(g["a_log"].T), "dt_bias": padded(g["dt_bias"].T),
        "onorm": cols(g["onorm_g"]), "na_q": twice(g["na_q_gain_2"][0]), "na_k": twice(g["na_k_gain_2"][0]),
        "da_q": twice(g["da_q_gain_2"][0]), "da_k": twice(g["da_k_gain_2"][0]), "subln": cols(g["da_subln_gain_2"]),
        "gqa_q": twice(g["gqa_q_gain_2"][0]), "gqa_k": twice(g["gqa_k_gain_2"][0]),
        "lambdas": padded(np.stack([g[f"da_lambda_{n}_2"][0] for n in ("q1", "q2", "k1", "k2")], axis=1)),
        "b_ada0": both(g["b_ada_2"][0]), "b_ada1": both(g["b_ada_2"][1]),
        "ffn_w0": taps(g["ffn_conv_w_2"][0]), "ffn_w1": taps(g["ffn_conv_w_2"][1]),
        "ffn_b0": cols(g["ffn_conv_b_2"][0]), "ffn_b1": cols(g["ffn_conv_b_2"][1]),
        "hy_conv_w": taps(g["hy_conv_w_2"][0]), "hy_conv_b": cols(g["hy_conv_b_2"]),
        "hy_b": padded(np.stack([g[f"hy_b{n}_2"][0] for n in (1, 2, 3)], axis=1)), "hy_freq": padded(g["hy_freq_2"].T),
        "hy_skip": cols(g["hy_skip_2"]), "hy_first": (np.arange(P) > 0).astype(np.float32)[:, None],
        "eps": np.full((P, 1), EPS, np.float32), "eps_query": np.full((P, 1), EPS * HD, np.float32),
        "eps_delta": np.full((P, 1), EPS * P, np.float32), "eps_subln": np.full((P, 1), EPS * SUBLN, np.float32), "one": np.ones((P, 1), np.float32),
    }
    o["params"] = np.concatenate([p[name].reshape(P, n) for name, n in PARAMS], axis=1)
    o["rel_bias"] = g["rel_bias"]
    o["rpb"] = np.pad(g["na_rpb_2"][0], ((0, 0), (0, 0), (GRID_W - WIN_C, GRID_W - WIN_C)))
    for n in (1, 2, 3, 4):
        o[f"hy_w{n}"] = g[f"hy_w{n}_2"][0]
    o["consts"] = constants()
    o["buckets"], o["log_counts"] = distance_tables()
    o.update(hyena_tables())
    return {name: np.ascontiguousarray(a) for name, a in o.items()}


def kernel(**inputs):
    import concourse.bacc as bacc
    from concourse.bass_utils import run_bass_kernel_spmd

    nc = bacc.Bacc("TRN2", target_bir_lowering=False, num_devices=1)
    arrays, dram = {}, {}
    for name, a in layout(inputs).items():
        arrays[f"in_{name}"] = a
        handle = nc.dram_tensor(f"in_{name}", a.shape, F32, kind="ExternalInput")
        dram[name] = handle if name in ("rpb", "cond_rows") else handle.ap()
    dram["lines"] = nc.dram_tensor("bias_lines", (8, LINE), F32)
    dram["out"] = nc.dram_tensor("out_0", (P, DT, S), F32, kind="ExternalOutput").ap()
    build(nc, dram)
    r = run_bass_kernel_spmd(nc, [arrays], core_ids=[0])
    got = r.results[0]["out_0"]
    return np.ascontiguousarray(np.asarray(got).transpose(2, 1, 0).reshape(1, S, D))
```
